# Optimizing a Trainium2 kernel written in Bass

```python
import jax, jax.numpy as jnp
from jax import lax
import numpy as np

D_MODEL = 1024
BATCH = 1
SEQ = 256
DEPTH = 1

GRID_W = 64
CTX_LEN = 256
GLA_HEADS = 4
GLA_DK = 64
GLA_DV = 128
GLA_WIDTH = GLA_HEADS * GLA_DV
GATE_RANK = 16
GATE_NORMALIZER = 16.0
CHUNK = 64
POOL_WINDOWS = (2, 4, 8, 16)
POOL_GROUP = 128
POOL_WIDTH = POOL_GROUP * len(POOL_WINDOWS)
MIX_WIDTH = GLA_WIDTH + POOL_WIDTH
Q_COLS = GLA_HEADS * GLA_DK
K_COLS = GLA_HEADS * GLA_DK
V_COLS = GLA_WIDTH
G_COLS = GLA_WIDTH
A_COLS = 2 * GATE_RANK
P_COLS = POOL_WIDTH
OFF_K = Q_COLS
OFF_V = OFF_K + K_COLS
OFF_G = OFF_V + V_COLS
OFF_A = OFF_G + G_COLS
OFF_P = OFF_A + A_COLS
IN_COLS = OFF_P + P_COLS
N_GROUPS = 4
EXPERTS_PER_GROUP = 8
N_EXPERTS = N_GROUPS * EXPERTS_PER_GROUP
TOP_K_INNER = 2
D_EXPERT = 256
EPS = 1e-6


def rmsnorm(x, g):
    xf = x.astype(jnp.float32)
    y = xf * lax.rsqrt(jnp.mean(xf * xf, axis=-1, keepdims=True) + EPS)
    return (y * g).astype(x.dtype)

def modulate(h, shift, scale):
    return h * (1.0 + scale) + shift

def flip(t):
    return jnp.flip(t, axis=1)

def split_heads_qkv(q, k, v):
    B, L, _ = q.shape
    q = q.reshape(B, L, GLA_HEADS, GLA_DK) * (GLA_DK ** -0.5)
    k = k.reshape(B, L, GLA_HEADS, GLA_DK)
    v = v.reshape(B, L, GLA_HEADS, GLA_DV)
    return q, k, v

def log_decay(a_low, w_dec, b_dec):
    B, L, _ = a_low.shape
    a = a_low.reshape(B, L, 2, GATE_RANK).astype(jnp.float32)
    la = jax.nn.log_sigmoid(jnp.einsum('bldr,drk->bldk', a, w_dec) + b_dec) / GATE_NORMALIZER
    la = la.reshape(B, L, 2, GLA_HEADS, GLA_DK)
    return la[:, :, 0], la[:, :, 1]

def gla_state(k, v, la, s0):
    B, L, H, dk = k.shape
    dv = v.shape[-1]
    N = L // CHUNK
    kc = k.reshape(B, N, CHUNK, H, dk).astype(jnp.float32)
    vc = v.reshape(B, N, CHUNK, H, dv)
    b = jnp.cumsum(la.reshape(B, N, CHUNK, H, dk), axis=2)
    b_last = b[:, :, -1]
    k_st = kc * jnp.exp(b_last[:, :, None] - b)
    d_state = jnp.einsum('bnchd,bnche->nbhde', k_st, vc)
    decay = jnp.exp(b_last).transpose(1, 0, 2, 3)

    def step(S, inp):
        d, ds = inp
        return d[..., None] * S + ds, S

    s_fin, s_prev = lax.scan(step, s0, (decay, d_state))
    return s_prev, s_fin, b

def gla_chunked(q, k, v, la, s0):
    s_prev, s_fin, b = gla_state(k, v, la, s0)
    B, L, H, dk = q.shape
    dv = v.shape[-1]
    N = L // CHUNK
    qb = q.reshape(B, N, CHUNK, H, dk).astype(jnp.float32) * jnp.exp(b)
    kb = k.reshape(B, N, CHUNK, H, dk).astype(jnp.float32) * jnp.exp(-b)
    vc = v.reshape(B, N, CHUNK, H, dv)
    mask = jnp.tril(jnp.ones((CHUNK, CHUNK), dtype=bool))
    scores = jnp.where(mask, jnp.einsum('bnihd,bnjhd->bnhij', qb, kb), 0.0)
    o = jnp.einsum('bnhij,bnjhe->bnihe', scores, vc) + jnp.einsum('bnihd,nbhde->bnihe', qb, s_prev)
    return o.reshape(B, L, H, dv), s_fin

def gla_bidirectional(q, k, v, la_f, la_b, s0_f, s0_b):
    o_f, s_f = gla_chunked(q, k, v, la_f, s0_f)
    o_b, s_b = gla_chunked(flip(q), flip(k), flip(v), flip(la_b), s0_b)
    return o_f + flip(o_b), s_f, s_b

def window_mean(x, w, axis):
    n = x.shape[axis]
    lo = w // 2
    hi = w - 1 - lo
    cs = jnp.cumsum(x.astype(jnp.float32), axis=axis)
    pad = [(0, 0)] * x.ndim
    pad[axis] = (1, 0)
    cs = jnp.pad(cs, pad)
    idx = np.arange(n)
    start = np.clip(idx - lo, 0, n)
    end = np.clip(idx + hi + 1, 0, n)
    s = jnp.take(cs, jnp.asarray(end), axis=axis) - jnp.take(cs, jnp.asarray(start), axis=axis)
    cshape = [1] * x.ndim
    cshape[axis] = n
    cnt = jnp.asarray((end - start).astype(np.float32).reshape(cshape))
    return s / cnt

def pool_mixer(p, w_pool, pool_scale, rows):
    B, L, _ = p.shape
    groups = p.reshape(B, L, len(POOL_WINDOWS), POOL_GROUP)
    outs = []
    for gi, w in enumerate(POOL_WINDOWS):
        xg = groups[:, :, gi]
        if rows is None:
            m = window_mean(xg, w, 1)
        else:
            xg2 = xg.reshape(B, rows, GRID_W, POOL_GROUP)
            m = window_mean(window_mean(xg2, w, 2), w, 1).reshape(B, L, POOL_GROUP)
        outs.append(m - xg)
    y = jnp.stack(outs, axis=2)
    y = jnp.einsum('blgc,gcd->blgd', y, w_pool).reshape(B, L, POOL_WIDTH)
    return y * pool_scale

def token_mixer(h, w_in, w_dec, b_dec, gla_norm_g, w_pool, pool_scale, w_out, s0_f, s0_b, rows):
    B, L, _ = h.shape
    proj = h @ w_in
    q, k, v, g, a_low, p = jnp.split(proj, [OFF_K, OFF_V, OFF_G, OFF_A, OFF_P], axis=-1)
    q, k, v = split_heads_qkv(q, k, v)
    la_f, la_b = log_decay(a_low, w_dec, b_dec)
    o, s_f, s_b = gla_bidirectional(q, k, v, la_f, la_b, s0_f, s0_b)
    o = rmsnorm(o, gla_norm_g).reshape(B, L, GLA_WIDTH) * jax.nn.silu(g)
    pooled = pool_mixer(p, w_pool, pool_scale, rows)
    out = jnp.concatenate([o, pooled.astype(o.dtype)], axis=-1) @ w_out
    return out, s_f, s_b

def context_states(h, w_in, w_dec, b_dec):
    B, L, _ = h.shape
    kv = h @ w_in[:, OFF_K:OFF_G]
    a_low = h @ w_in[:, OFF_A:OFF_P]
    k = kv[..., :K_COLS].reshape(B, L, GLA_HEADS, GLA_DK)
    v = kv[..., K_COLS:].reshape(B, L, GLA_HEADS, GLA_DV)
    la_f, la_b = log_decay(a_low, w_dec, b_dec)
    s0 = jnp.zeros((B, GLA_HEADS, GLA_DK, GLA_DV), jnp.float32)
    _, s_f, _ = gla_state(k, v, la_f, s0)
    _, s_b, _ = gla_state(flip(k), flip(v), flip(la_b), s0)
    return s_f, s_b

def hier_moe(h, w_rg, w_re, w_e_in, w_e_out):
    B, L, D = h.shape
    t = h.reshape(-1, D)
    pg = jax.nn.softmax((t @ w_rg).astype(jnp.float32), axis=-1)
    gp, gi = lax.top_k(pg, 1)
    le = (t @ w_re).astype(jnp.float32).reshape(-1, N_GROUPS, EXPERTS_PER_GROUP)
    le = jnp.take_along_axis(le, gi[:, :, None], axis=1)[:, 0]
    ew, ei = lax.top_k(jax.nn.softmax(le, axis=-1), TOP_K_INNER)
    ew = ew / jnp.sum(ew, axis=-1, keepdims=True)
    weights = gp * ew
    eid = gi * EXPERTS_PER_GROUP + ei
    gates = jnp.einsum('tk,tke->et', weights, jax.nn.one_hot(eid, N_EXPERTS, dtype=jnp.float32))

    def body(acc, inp):
        wi, wo, ge = inp
        a, u = jnp.split(t @ wi, 2, axis=-1)
        return acc + ((jax.nn.silu(a) * u) @ wo) * ge[:, None], None

    y, _ = lax.scan(body, jnp.zeros(t.shape, jnp.float32), (w_e_in, w_e_out, gates))
    return y.reshape(B, L, D).astype(h.dtype)

def first_inputs(seed: int = 0) -> dict:
    key = jax.random.key(seed)
    ks = jax.random.split(key, 24)
    f32 = jnp.float32

    def nrm(k, shape, s):
        return jax.random.normal(k, shape, f32) * s

    D = D_MODEL
    return {
        "x": nrm(ks[0], (BATCH, SEQ, D), 1.0),
        "c": nrm(ks[1], (BATCH, D), 1.0),
        "ctx": nrm(ks[2], (BATCH, CTX_LEN, D), 1.0),
        "c_ctx": nrm(ks[3], (D,), 1.0),
        "w_ada": nrm(ks[4], (DEPTH, D, 6 * D), D ** -0.5),
        "b_ada": nrm(ks[5], (DEPTH, 6 * D), 0.02),
        "norm1_g": 1.0 + nrm(ks[6], (DEPTH, D), 0.02),
        "w_in": nrm(ks[7], (DEPTH, D, IN_COLS), D ** -0.5),
        "w_decay": nrm(ks[8], (DEPTH, 2, GATE_RANK, GLA_HEADS * GLA_DK), GATE_RANK ** -0.5),
        "b_decay": nrm(ks[9], (DEPTH, 2, GLA_HEADS * GLA_DK), 0.1),
        "gla_norm_g": 1.0 + nrm(ks[10], (DEPTH, GLA_DV), 0.02),
        "w_pool": nrm(ks[11], (DEPTH, len(POOL_WINDOWS), POOL_GROUP, POOL_GROUP), POOL_GROUP ** -0.5),
        "pool_scale": 1.0 + nrm(ks[12], (DEPTH, POOL_WIDTH), 0.02),
        "w_out": nrm(ks[13], (DEPTH, MIX_WIDTH, D), MIX_WIDTH ** -0.5),
        "norm2_g": 1.0 + nrm(ks[14], (DEPTH, D), 0.02),
        "w_router_group": nrm(ks[15], (DEPTH, D, N_GROUPS), D ** -0.5),
        "w_router_expert": nrm(ks[16], (DEPTH, D, N_EXPERTS), D ** -0.5),
        "w_expert_in": nrm(ks[17], (DEPTH, N_EXPERTS, D, 2 * D_EXPERT), D ** -0.5),
        "w_expert_out": nrm(ks[18], (DEPTH, N_EXPERTS, D_EXPERT, D), D_EXPERT ** -0.5),
        "final_norm_g": 1.0 + nrm(ks[19], (D,), 0.02),
    }

def first_block(x, c, ctx, c_ctx, w_ada, b_ada, norm1_g, w_in, w_decay, b_decay, gla_norm_g, w_pool,
              pool_scale, w_out, norm2_g, w_router_group, w_router_expert, w_expert_in, w_expert_out,
              final_norm_g):
    rows = x.shape[1] // GRID_W
    xc = ctx
    for i in range(DEPTH):
        mod = jax.nn.silu(c) @ w_ada[i] + b_ada[i]
        sh_a, sc_a, gt_a, sh_m, sc_m, gt_m = jnp.split(mod[:, None, :], 6, axis=-1)
        mod_c = jax.nn.silu(c_ctx) @ w_ada[i] + b_ada[i]
        csh_a, csc_a, cgt_a, csh_m, csc_m, cgt_m = jnp.split(mod_c, 6, axis=-1)

        hc = modulate(rmsnorm(xc, norm1_g[i]), csh_a, csc_a)
        if i + 1 < DEPTH:
            zero_s = jnp.zeros((xc.shape[0], GLA_HEADS, GLA_DK, GLA_DV), jnp.float32)
            out_c, s_f, s_b = token_mixer(hc, w_in[i], w_decay[i], b_decay[i], gla_norm_g[i], w_pool[i],
                                          pool_scale[i], w_out[i], zero_s, zero_s, None)
            xc_next = xc + (cgt_a * out_c).astype(xc.dtype)
            hc2 = modulate(rmsnorm(xc_next, norm2_g[i]), csh_m, csc_m)
            xc_next = xc_next + (cgt_m * hier_moe(hc2, w_router_group[i], w_router_expert[i],
                                                  w_expert_in[i], w_expert_out[i])).astype(xc.dtype)
        else:
            s_f, s_b = context_states(hc, w_in[i], w_decay[i], b_decay[i])
            xc_next = xc

        h = modulate(rmsnorm(x, norm1_g[i]), sh_a, sc_a)
        out, _, _ = token_mixer(h, w_in[i], w_decay[i], b_decay[i], gla_norm_g[i], w_pool[i],
                                pool_scale[i], w_out[i], s_f, s_b, rows)
        x = x + (gt_a * out).astype(x.dtype)
        h2 = modulate(rmsnorm(x, norm2_g[i]), sh_m, sc_m)
        x = x + (gt_m * hier_moe(h2, w_router_group[i], w_router_expert[i],
                                 w_expert_in[i], w_expert_out[i])).astype(x.dtype)
        xc = xc_next
    return rmsnorm(x, final_norm_g)


Q_BLOCK = 128
ROPE_THETA = 10000.0
GN_EPS = 1e-5
NEG_BIG = -1e30
A_HEADS = 8
A_HEAD_DIM = 64
IDX_HEADS = 8
IDX_DIM = 64
TOPK_MAX = 256
A_WIDTH = A_HEADS * A_HEAD_DIM
R_HEADS = 4
R_QK_DIM = 128
R_V_DIM = 256
R_WIDTH = R_HEADS * R_V_DIM
D_FF = 2816
PLE_DIM = 256
IN_SPLITS = (
    A_HEADS * A_HEAD_DIM,
    A_HEAD_DIM,
    A_HEAD_DIM,
    IDX_HEADS * IDX_DIM,
    IDX_DIM,
    IDX_HEADS,
    R_HEADS * R_QK_DIM,
    R_HEADS * R_QK_DIM,
    R_HEADS * R_V_DIM,
    R_HEADS * R_V_DIM,
    D_MODEL,
    D_MODEL,
)
IN_WIDTH = sum(IN_SPLITS)


def rms_norm(x, g):
    xf = x.astype(jnp.float32)
    y = xf * lax.rsqrt(jnp.mean(xf * xf, axis=-1, keepdims=True) + EPS)
    return (y * g.astype(jnp.float32)).astype(x.dtype)

def swiglu(x, w_gate, w_up, w_down):
    return (jax.nn.silu(x @ w_gate) * (x @ w_up)) @ w_down

def rope(t, pos):
    half = t.shape[-1] // 2
    inv = ROPE_THETA ** (-jnp.arange(half, dtype=jnp.float32) / half)
    ang = pos.astype(jnp.float32)[..., None] * inv
    cos = jnp.cos(ang)[:, :, None, :]
    sin = jnp.sin(ang)[:, :, None, :]
    t1 = t[..., :half].astype(jnp.float32)
    t2 = t[..., half:].astype(jnp.float32)
    return jnp.concatenate([t1 * cos - t2 * sin, t2 * cos + t1 * sin], axis=-1).astype(t.dtype)

def dsa_attention(q, k, v, q_idx, k_idx, w_idx, n_sel):
    b, s = q.shape[0], q.shape[1]
    nb = s // Q_BLOCK
    key_pos = jnp.arange(s)
    k_idx32 = k_idx.astype(jnp.float32)

    def to_blocks(t):
        return jnp.moveaxis(t.reshape((b, nb, Q_BLOCK) + t.shape[2:]), 1, 0)

    def one_block(args):
        qb, qib, wb, blk = args
        qpos = blk * Q_BLOCK + jnp.arange(Q_BLOCK)
        visible_end = (qpos // CHUNK + 1) * CHUNK
        admissible = key_pos[None, :] < visible_end[:, None]
        rel = jax.nn.relu(jnp.einsum('bqhd,bsd->bqhs', qib.astype(jnp.float32), k_idx32))
        score = jnp.einsum('bqhs,bqh->bqs', rel, wb.astype(jnp.float32))
        score = jnp.where(admissible[None], score, NEG_BIG)
        top_val, top_pos = lax.top_k(score, n_sel)
        valid = top_val > 0.5 * NEG_BIG
        k_sel = jax.vmap(lambda kb, ib: kb[ib])(k, top_pos)
        v_sel = jax.vmap(lambda vb, ib: vb[ib])(v, top_pos)
        logits = jnp.einsum('bqhd,bqkd->bqhk', qb, k_sel).astype(jnp.float32) * (A_HEAD_DIM ** -0.5)
        logits = jnp.where(valid[:, :, None, :], logits, NEG_BIG)
        probs = jax.nn.softmax(logits, axis=-1).astype(v.dtype)
        return jnp.einsum('bqhk,bqkd->bqhd', probs, v_sel)

    out = lax.map(one_block, (to_blocks(q), to_blocks(q_idx), to_blocks(w_idx), jnp.arange(nb)))
    return jnp.moveaxis(out, 0, 1).reshape(b, s, -1)

def retention(q, k, v):
    b, s, h, dk = q.shape
    dv = v.shape[-1]
    n = s // CHUNK
    log_gamma = jnp.log1p(-jnp.exp2(-5.0 - jnp.arange(h, dtype=jnp.float32)))
    idx = jnp.arange(CHUNK, dtype=jnp.float32)
    decay_intra = jnp.exp(log_gamma[:, None, None] * jnp.abs(idx[:, None] - idx[None, :]))
    decay_q = jnp.exp(log_gamma[None, :] * (idx[:, None] + 1.0))
    decay_k = jnp.exp(log_gamma[None, :] * (CHUNK - 1.0 - idx[:, None]))
    decay_chunk = jnp.exp(log_gamma * CHUNK)
    qc = q.reshape(b, n, CHUNK, h, dk)
    kc = (k * (dk ** -0.5)).reshape(b, n, CHUNK, h, dk)
    vc = v.reshape(b, n, CHUNK, h, dv)
    scores = jnp.einsum('bnihd,bnjhd->bnhij', qc, kc) * decay_intra
    y_intra = jnp.einsum('bnhij,bnjhe->bnihe', scores, vc)
    kv = jnp.einsum('bnjhd,bnjhe,jh->nbhde', kc, vc, decay_k)

    def step(state, kv_n):
        return decay_chunk[None, :, None, None] * state + kv_n, state

    _, prev = lax.scan(step, jnp.zeros((b, h, dk, dv), jnp.float32), kv)
    y_cross = jnp.einsum('bnihd,nbhde->bnihe', qc, prev) * decay_q[None, None, :, :, None]
    return (y_intra + y_cross).reshape(b, s, h, dv)

def group_norm_heads(y, g):
    mean = jnp.mean(y, axis=-1, keepdims=True)
    var = jnp.mean(jnp.square(y - mean), axis=-1, keepdims=True)
    yn = (y - mean) * lax.rsqrt(var + GN_EPS)
    return yn.reshape(y.shape[0], y.shape[1], -1) * g.astype(jnp.float32)

def second_inputs(seed: int = 0) -> dict:
    key = jax.random.key(seed)
    ks = jax.random.split(key, 24)
    f32 = jnp.float32

    def w(k, shape, fan_in, scale=1.0):
        return jax.random.normal(k, shape, f32) * (scale * fan_in ** -0.5)

    def gain(k, shape):
        return 1.0 + 0.05 * jax.random.normal(k, shape, f32)

    offsets = jax.random.randint(ks[2], (BATCH, 1), 0, 4096)
    positions = (offsets + jnp.arange(SEQ)[None, :]).astype(jnp.int32)
    return {
        'x': jax.random.normal(ks[0], (BATCH, SEQ, D_MODEL), f32),
        'p': jax.random.normal(ks[1], (DEPTH, BATCH, SEQ, PLE_DIM), f32),
        'positions': positions,
        'ffn1_norm': gain(ks[3], (DEPTH, D_MODEL)),
        'ffn1_w_gate': w(ks[4], (DEPTH, D_MODEL, D_FF), D_MODEL),
        'ffn1_w_up': w(ks[5], (DEPTH, D_MODEL, D_FF), D_MODEL),
        'ffn1_w_down': w(ks[6], (DEPTH, D_FF, D_MODEL), D_FF, 0.5),
        'mix_norm': gain(ks[7], (DEPTH, D_MODEL)),
        'w_in': w(ks[8], (DEPTH, D_MODEL, IN_WIDTH), D_MODEL),
        'ret_gn': gain(ks[9], (DEPTH, R_WIDTH)),
        'w_branch_a': w(ks[10], (DEPTH, A_WIDTH, D_MODEL), A_WIDTH),
        'w_branch_b': w(ks[11], (DEPTH, R_WIDTH, D_MODEL), R_WIDTH),
        'w_out': w(ks[12], (DEPTH, D_MODEL, D_MODEL), D_MODEL, 0.5),
        'ffn2_norm': gain(ks[13], (DEPTH, D_MODEL)),
        'ffn2_w_gate': w(ks[14], (DEPTH, D_MODEL, D_FF), D_MODEL),
        'ffn2_w_up': w(ks[15], (DEPTH, D_MODEL, D_FF), D_MODEL),
        'ffn2_w_down': w(ks[16], (DEPTH, D_FF, D_MODEL), D_FF, 0.5),
        'ple_norm': gain(ks[17], (DEPTH, D_MODEL)),
        'w_ple_gate': w(ks[18], (DEPTH, D_MODEL, D_MODEL), D_MODEL),
        'w_ple_proj': w(ks[19], (DEPTH, PLE_DIM, D_MODEL), PLE_DIM, 0.5),
        'final_norm': gain(ks[20], (D_MODEL,)),
    }

def second_block(x, p, positions, ffn1_norm, ffn1_w_gate, ffn1_w_up, ffn1_w_down,
              mix_norm, w_in, ret_gn, w_branch_a, w_branch_b, w_out,
              ffn2_norm, ffn2_w_gate, ffn2_w_up, ffn2_w_down,
              ple_norm, w_ple_gate, w_ple_proj, final_norm):
    b, s, _ = x.shape
    n_sel = min(TOPK_MAX, s // 4)
    split_points = []
    acc = 0
    for sz in IN_SPLITS[:-1]:
        acc += sz
        split_points.append(acc)

    h = x
    for i in range(DEPTH):
        h = h + 0.5 * swiglu(rms_norm(h, ffn1_norm[i]), ffn1_w_gate[i], ffn1_w_up[i], ffn1_w_down[i])

        u = rms_norm(h, mix_norm[i])
        z = u @ w_in[i]
        (aq, ak, av, iq, ik, iw, rq, rk, rv, rg, ga, gb) = jnp.split(z, split_points, axis=-1)

        aq = rope(aq.reshape(b, s, A_HEADS, A_HEAD_DIM), positions)
        ak = rope(ak[:, :, None, :], positions)[:, :, 0, :]
        iq = rope(iq.reshape(b, s, IDX_HEADS, IDX_DIM), positions) * (IDX_DIM ** -0.5)
        ik = rope(ik[:, :, None, :], positions)[:, :, 0, :]
        iw = iw * (IDX_HEADS ** -0.5)
        y_a = dsa_attention(aq, ak, av, iq, ik, iw, n_sel)

        rq = rope(rq.reshape(b, s, R_HEADS, R_QK_DIM), positions).astype(jnp.float32)
        rk = rope(rk.reshape(b, s, R_HEADS, R_QK_DIM), positions).astype(jnp.float32)
        rv = rv.reshape(b, s, R_HEADS, R_V_DIM).astype(jnp.float32)
        y_r = group_norm_heads(retention(rq, rk, rv), ret_gn[i]).astype(x.dtype) * jax.nn.silu(rg)

        merged = jax.nn.sigmoid(ga) * (y_a @ w_branch_a[i]) + jax.nn.sigmoid(gb) * (y_r @ w_branch_b[i])
        h = h + merged @ w_out[i]

        h = h + 0.5 * swiglu(rms_norm(h, ffn2_norm[i]), ffn2_w_gate[i], ffn2_w_up[i], ffn2_w_down[i])

        gate = jax.nn.sigmoid(rms_norm(h, ple_norm[i]) @ w_ple_gate[i])
        h = h + gate * (p[i] @ w_ple_proj[i])

    return rms_norm(h, final_norm)


def setup_inputs(seed=0):
    out = dict(first_inputs(seed))
    for name, value in second_inputs(seed + 1).items():
        if name != "x":
            out[name + "_2"] = value
    return out


def reference(
    x, c, ctx, c_ctx, w_ada, b_ada, norm1_g, w_in, w_decay, b_decay, gla_norm_g, w_pool,
    pool_scale, w_out, norm2_g, w_router_group, w_router_expert, w_expert_in, w_expert_out,
    final_norm_g, p_2, positions_2, ffn1_norm_2, ffn1_w_gate_2, ffn1_w_up_2, ffn1_w_down_2,
    mix_norm_2, w_in_2, ret_gn_2, w_branch_a_2, w_branch_b_2, w_out_2, ffn2_norm_2,
    ffn2_w_gate_2, ffn2_w_up_2, ffn2_w_down_2, ple_norm_2, w_ple_gate_2, w_ple_proj_2,
    final_norm_2,
):
    x = first_block(
        x, c, ctx, c_ctx, w_ada, b_ada, norm1_g, w_in, w_decay, b_decay, gla_norm_g, w_pool,
        pool_scale, w_out, norm2_g, w_router_group, w_router_expert, w_expert_in, w_expert_out,
        final_norm_g,
    )
    return second_block(
        x, p_2, positions_2, ffn1_norm_2, ffn1_w_gate_2, ffn1_w_up_2, ffn1_w_down_2, mix_norm_2,
        w_in_2, ret_gn_2, w_branch_a_2, w_branch_b_2, w_out_2, ffn2_norm_2, ffn2_w_gate_2,
        ffn2_w_up_2, ffn2_w_down_2, ple_norm_2, w_ple_gate_2, w_ple_proj_2, final_norm_2,
    )


_drawn_inputs = setup_inputs


def setup_inputs(seed=0):
    import zlib

    import numpy as np

    out = dict(_drawn_inputs(seed))
    spreads = {}
    factors = {'gla_norm_g': 2.784,
     'pool_scale': 3.337,
     'ffn1_norm_2': 4.737,
     'mix_norm_2': 2.789,
     'ret_gn_2': 6.997,
     'ffn2_norm_2': 5.49,
     'ple_norm_2': 8.0}
    for name, (base, spread) in spreads.items():
        noise = np.random.default_rng([zlib.crc32(name.encode()), seed]).standard_normal(out[name].shape)
        drawn = base * np.exp(spread * noise) if base else spread * noise
        out[name] = __import__('jax').numpy.asarray(drawn.astype(out[name].dtype))
    for name, factor in factors.items():
        out[name] = (out[name] * factor).astype(out[name].dtype)
    return out
```

```python
import numpy as np

EPS = 1e-6
GN_EPS = 1e-5
PAR = ["norm1", "bada", "bdec", "glag", "pscale", "norm2", "final1", "ffn1n", "mixn", "retgn", "ffn2n", "plen", "final2"]
PARN = [8, 48, 4, 1, 4, 8, 8, 8, 8, 8, 8, 8, 8]
CON = [("ident", 128), ("ones", 128), ("ra", 128), ("rr", 128), ("inv", 2), ("idxw", 8), ("scanm", 512),
       ("glam", 256), ("pool", 2048), ("dec", 1536)]


def offsets(pairs):
    at, out = 0, {}
    for n, k in pairs:
        out[n] = (at, at + k)
        at += k
    return out, at


def program(nc, D, out):
    import concourse.bass as bass
    from concourse import mybir
    from contextlib import ExitStack

    f32, f32r, i32 = mybir.dt.float32, mybir.dt.float32r, mybir.dt.int32
    ALU, ACT, AX = mybir.AluOpType, mybir.ActivationFunctionType, mybir.AxisListType
    cx = ExitStack()

    with cx:
        def sb(name, shape, dt=f32):
            return cx.enter_context(nc.sbuf_tensor(name, shape, dt))

        def sem(name):
            return cx.enter_context(nc.semaphore(name))

        class Lane:
            def __init__(self, name):
                self.sem, self.n, self.q, self.seen = sem("s_" + name), 0, [], {}

            def wait(self, *toks):
                for t in toks:
                    if t is None:
                        continue
                    if isinstance(t, list):
                        self.wait(*t)
                        continue
                    s, v = t
                    if self.seen.get(id(s), 0) < v:
                        self.seen[id(s)] = v
                        self.q.append(lambda e, s=s, v=v: e.wait_ge(s, v))

            def run(self, fn, *toks):
                self.wait(*toks)
                self.n += 1
                self.q.append(lambda e, f=fn, s=self.sem: f(e).then_inc(s, 1))
                return (self.sem, self.n)

            def plain(self, fn, *toks):
                self.wait(*toks)
                self.q.append(fn)

            def last(self):
                return (self.sem, self.n) if self.n else None

        PE, DV, AC, GP, SY = Lane("pe"), Lane("dve"), Lane("act"), Lane("pool"), Lane("sp")

        class Dma:
            def __init__(self, name):
                self.sem, self.n = sem(name), 0

            def go(self, lane, dst, src, *toks):
                self.n += 16
                lane.plain(lambda e, s=self.sem: e.dma_start(dst, src).then_inc(s, 16), *toks)
                return (self.sem, self.n)

        def tt(o, a, b, op, *toks):
            return DV.run(lambda e: e.tensor_tensor(o, a, b, op), *toks)

        def ts(o, a, s1, s2, op0, op1, *toks):
            if op1 is None:
                return DV.run(lambda e: e.tensor_scalar(o, a, s1, None, op0), *toks)
            return DV.run(lambda e: e.tensor_scalar(o, a, s1, s2, op0, op1), *toks)

        def stt(o, a, s, b, op0, op1, *toks):
            return DV.run(lambda e: e.scalar_tensor_tensor(o, a, s, b, op0, op1), *toks)

        def vcopy(o, a, *toks):
            return DV.run(lambda e: e.tensor_copy(o, a), *toks)

        def rmax(o, a, *toks):
            return DV.run(lambda e: e.tensor_reduce(o, a, AX.X, ALU.max), *toks)

        def rsum(o, a, *toks):
            return DV.run(lambda e: e.tensor_reduce(o, a, AX.X, ALU.add), *toks)

        def recip(o, a, *toks):
            return DV.run(lambda e: e.reciprocal(o, a), *toks)

        def act(o, a, fn, *toks, **kw):
            return AC.run(lambda e: e.activation(o, a, fn, **kw), *toks)

        def mm(o, l, r, start, stop, *toks, inc=False):
            f = lambda e: e.matmul(o, l, r, start=start, stop=stop, skip_group_check=True)
            if inc:
                return PE.run(f, *toks)
            PE.plain(f, *toks)

        def mm3(o, lh, ll, rh, rl, start, stop, *toks, inc=False):
            PE.wait(*toks)
            mm(o, lh, rh, start, False)
            mm(o, lh, rl, False, False)
            return mm(o, ll, rh, False, stop, inc=inc)

        def transpose(o, a, idn, *toks):
            return PE.run(lambda e: e.transpose(o, a, idn), *toks)

        co, ncon = offsets(CON)
        po, npar = offsets(list(zip(PAR, PARN)))
        NR, NS = 4, 3
        RAW = [sb(f"raw{i}", [128, 2048]) for i in range(NR)]
        WH = [sb(f"wh{i}", [128, 2048], f32r) for i in range(NS)]
        WL = [sb(f"wl{i}", [128, 2048], f32r) for i in range(NS)]
        XTt = sb("xt", [128, 2048])
        XT = XTt[:, :].rearrange("p (k t) -> p k t", k=8)
        HHt, HLt = sb("hh", [128, 4096], f32r), sb("hl", [128, 4096], f32r)
        YHt, YLt = sb("yh", [128, 3072], f32r), sb("yl", [128, 3072], f32r)
        wide = lambda T: T[:, :].rearrange("p (k t) -> p k t", k=8)
        half = lambda T, i: T[:, 2048 * i:2048 * i + 2048].rearrange("p (k t) -> p k t", k=8)
        YH = YHt[:, :].rearrange("p (k t) -> p k t", k=12)
        YL = YLt[:, :].rearrange("p (k t) -> p k t", k=12)
        CS = sb("csts", [128, co["scanm"][0]])
        PR = sb("par", [128, npar])
        cst = lambda n: CS[:, co[n][0]:co[n][1]]
        par = lambda n: PR[:, po[n][0]:po[n][1]]
        ident, ones = cst("ident"), cst("ones")
        SMt = sb("small", [128, 512])
        AR = 13312
        ARt = sb("arena", [128, AR])
        small_at, arena_at, arena_free = [0], [0], [[]]

        def small(n):
            small_at[0] += n
            assert small_at[0] <= 512
            return SMt[:, small_at[0] - n:small_at[0]]

        def ar(n, k=None):
            arena_at[0] += n
            assert arena_at[0] <= AR, arena_at[0]
            v = ARt[:, arena_at[0] - n:arena_at[0]]
            return v if k is None else v.rearrange("p (k t) -> p k t", k=k)

        def everyone():
            return [t for t in (PE.last(), DV.last(), AC.last()) if t]

        class Bank:
            def __init__(self, i):
                self.t = cx.enter_context(nc.psum_tensor(f"bank{i}", [128, 512], f32))
                self.free = []

            def __getitem__(self, k):
                return self.t[k]

            def two(self):
                return self.t[:, :].rearrange("p (k t) -> p k t", k=2)

        BK = [Bank(i) for i in range(8)]
        AUX, YB = BK[3], BK[4:8]
        rot = {"l": BK[0:3], "i": 0}

        def rotate(banks):
            rot["l"], rot["i"] = banks, 0

        def bank():
            b = rot["l"][rot["i"] % len(rot["l"])]
            rot["i"] += 1
            PE.wait(b.free)
            b.free = []
            return b

        chunks = []

        def add(name, i, split=True):
            a = D[name]
            chunks.append((a[i], a.shape[2], split))

        for i in range(8):
            add("w_ada", i, False)
        ada = list(range(8, 24))
        for n, i in [("p", 0), ("p", 1), ("a", 0), ("k", 0), ("q", 0), ("v", 0), ("v", 1), ("g", 0), ("g", 1)]:
            add("w1" + n, i)
            for _ in range(2):
                if ada:
                    add("w_ada", ada.pop(0), False)
        for i in range(4):
            add("w_out", i)
        add("w_r", 0)

        def ffn_chunks(g, u, d, n):
            for i in range(n):
                add(g, i)
                add(u, i)
                if i:
                    add(d, i - 1)
            add(d, n - 1)

        ffn_chunks("eg", "eu", "ed", 32)
        ffn_chunks("f1g", "f1u", "f1d", 11)
        for n, k in [("ik", 1), ("iq", 2), ("rq", 2), ("rk", 2), ("rv", 4), ("aq", 2), ("kv", 1), ("rg", 4)]:
            for i in range(k):
                add("w2" + n, i)
        for j in range(4):
            for n in ("w2ga", "wba", "w2gb", "wbb"):
                add(n, j)
        for i in range(4):
            add("w_out2", i)
        ffn_chunks("f2g", "f2u", "f2d", 11)
        for j in range(4):
            add("wpg", j)
            add("wpp", j)

        RD = [Dma(f"d_raw{i}") for i in range(NR)]
        released = {}
        sfree = [[] for _ in range(NS)]
        st = {"f": 0, "s": 0, "g": 0, "k": 0, "held": None}
        loaded, parts = {}, {}

        def fetch():
            while st["f"] < len(chunks) and (st["f"] < NR or st["f"] - NR in released):
                i = st["f"]
                st["f"] += 1
                src, n, _ = chunks[i]
                loaded[i] = RD[i % NR].go(SY, RAW[i % NR][:, 0:n], src, released.get(i - NR))

        def split():
            i = st["s"]
            if i >= len(chunks):
                return
            st["s"] += 1
            _, n, sp = chunks[i]
            r = RAW[i % NR][:, 0:n]
            if not sp:
                parts[i] = (r, None, [loaded[i]], None)
                return
            s = st["k"] % NS
            st["k"] += 1
            h, l = WH[s][:, 0:n], WL[s][:, 0:n]
            th = act(h, r, ACT.Copy, loaded[i], sfree[s])
            tl = tt(l, r, h.bitcast(f32), ALU.subtract, th, loaded[i], sfree[s])
            parts[i] = (h, l, [th, tl], s)
            released[i] = [tl, th]
            fetch()

        def get():
            i = st["g"]
            st["g"] += 1
            while st["s"] <= min(i + 2, len(chunks) - 1):
                split()
            st["held"] = i
            return parts[i]

        def done(tok):
            i = st["held"]
            if chunks[i][2]:
                sfree[parts[i][3]] = [tok]
            else:
                released[i] = [tok]
                fetch()

        def blocks(part, nk):
            h, l, toks, _ = part
            v = lambda a: a if a is None else a.rearrange("p (k n) -> p k n", k=nk)
            return v(h), v(l), toks

        def lin_fm(xh, xl, xtoks, nk=8, ncols=256, N=256, width=128):
            h, l, wt = blocks(get(), nk)
            outs = []
            nb = ncols // width
            per = 512 // N
            tok = None
            for m in range(nb):
                if m % per == 0:
                    b = bank()
                    outs.append(b)
                o = b[:, (m % per) * N:(m % per) * N + N]
                for k in range(nk):
                    tok = mm3(o, h[:, k, m * width:(m + 1) * width], l[:, k, m * width:(m + 1) * width],
                              xh[:, k, :], xl[:, k, :], k == 0, k == nk - 1, wt, xtoks[k], inc=(k == nk - 1))
            done(tok)
            return outs, tok

        def split_into(h, l, src, *toks):
            th = act(h, src, ACT.Copy, *toks)
            tl = tt(l, src, h.bitcast(f32), ALU.subtract, th, *toks)
            return [th, tl]

        SQ = [sb("sq0", [128, 256]), sb("sq1", [128, 256])]
        sqfree = [[], []]
        RS = sb("rstd", [128, 256])
        rsfree = [[]]
        sqn = [0]

        def stat_step(src, b, k, n, *toks):
            i = sqn[0] % 2
            sqn[0] += 1
            a = act(SQ[i][:, :], src, ACT.Square, sqfree[i], *toks)
            t = mm(b[:, 0:256], ones, SQ[i][:, :], k == 0, k == n - 1, a, inc=True)
            sqfree[i] = [t]
            return t

        def rstd(b, tok, scale, eps_ap):
            a = act(RS[:, :], b[:, 0:256], ACT.Sqrt, tok, rsfree[0], scale=scale, bias=eps_ap)
            b.free = [a]
            return recip(RS[:, :], RS[:, :], a)

        TN = [sb("tn0", [128, 256]), sb("tn1", [128, 256])]
        tnfree = [[], []]

        def norm(b, tok, gain, shift, H, L, free):
            t = rstd(b, tok, 1.0 / 1024, EPSA)
            out_t = []
            for k in range(8):
                i = k % 2
                u = stt(TN[i][:, :], norm.src[:, k, :], gain[:, k:k + 1], RS[:, :], ALU.mult, ALU.mult, t, tnfree[i])
                if shift is None:
                    th = act(H[:, k, :], TN[i][:, :], ACT.Copy, u, free)
                    tl = tt(L[:, k, :], TN[i][:, :], H[:, k, :].bitcast(f32), ALU.subtract, th, free)
                else:
                    th = act(H[:, k, :], TN[i][:, :], ACT.Identity, u, free, bias=shift[:, k:k + 1])
                    tl = stt(L[:, k, :], TN[i][:, :], shift[:, k:k + 1], H[:, k, :].bitcast(f32),
                             ALU.add, ALU.subtract, th, free)
                tnfree[i] = [tl]
                out_t.append([th, tl])
            rsfree[0] = [u]
            return out_t

        d_c, d_x, d_ct, d_p, d_a0, d_m = (Dma(n) for n in ("d_c", "d_x", "d_ct", "d_p", "d_a0", "d_m"))
        EPSA = small(1)
        EPSG = small(1)
        te = DV.run(lambda e: e.memset(EPSA, EPS))
        te = DV.run(lambda e: e.memset(EPSG, GN_EPS))
        AC.wait(te)
        cv = small(16)
        CT = ar(2048, 8)
        POOLM = ar(2048).rearrange("p (a g t) -> p a g t", a=2, g=4)
        t_cv = d_c.go(AC, cv, D["cvec"])
        t_par = d_p.go(AC, PR[:, :], D["par"])
        t_cs = d_p.go(AC, CS[:, :], D["cst"][:, 0:co["scanm"][0]])
        t_par = t_cs
        t_x = d_x.go(AC, XTt[:, :], D["x"])
        t_ct = d_ct.go(AC, CT.rearrange("p k t -> p (k t)"), D["ctx"])
        WPOOL = ar(512).rearrange("p (g d) -> p g d", g=4)
        t_pm = d_a0.go(AC, POOLM.rearrange("p a g t -> p (a g t)"), D["cst"][:, co["pool"][0]:co["pool"][1]])
        t_pm = d_a0.go(AC, WPOOL.rearrange("p g d -> p (g d)"), D["w_pool"])
        PTM = ar(1024).rearrange("p (a c) -> p a c", a=2)
        PY = ar(1024, 4)
        fetch()

        SC = small(16)
        t_sc = act(SC, cv, ACT.Silu, t_cv)
        SC3 = SC.rearrange("p (k c) -> p k c", k=8)
        MOD = small(96)
        MOD3 = MOD.rearrange("p (n c) -> p n c", c=2)

        def ada_chunk(c):
            h, _, wt = blocks(get(), 8)
            for m in range(2):
                n = 2 * c + m
                for k in range(8):
                    tok = mm(AUX[:, 2 * n:2 * n + 2], h[:, k, m * 128:(m + 1) * 128], SC3[:, k, :], k == 0, k == 7,
                             wt, t_sc, inc=(k == 7))
            done(tok)
            return tok

        bx, bc = BK[4], BK[5]
        for k in range(8):
            tsx = stat_step(XT[:, k, :], bx, k, 8, t_x, t_cs)
        for k in range(8):
            tsc = stat_step(CT[:, k, :], bc, k, 8, t_ct)
        for c in range(8):
            tm = ada_chunk(c)
        BA = par("bada").unsqueeze(2)
        t1 = tt(MOD3[:, 0:16, :], AUX[:, 0:32].rearrange("p (n c) -> p n c", c=2), BA[:, 0:16, :].broadcast_to([128, 16, 2]),
                ALU.add, tm, t_par)
        AUX.free = [t1]
        A1, B1 = small(16).rearrange("p (c k) -> p c k", c=2), small(16).rearrange("p (c k) -> p c k", c=2)
        for c in range(2):
            t2 = stt(A1[:, c, :], MOD3[:, 8:16, c], 1.0, par("norm1"), ALU.add, ALU.mult, t1)
            t3 = vcopy(B1[:, c, :], MOD3[:, 0:8, c], t1)
        DV.wait(t2, t3)
        AC.wait(t3)
        HW, LW = wide(HHt), wide(HLt)
        norm.src = XT
        hx = norm(bx, tsx, A1[:, 0, :], B1[:, 0, :], HW[:, :, 0:256], LW[:, :, 0:256], [])
        norm.src = CT
        hc = norm(bc, tsc, A1[:, 1, :], B1[:, 1, :], HW[:, :, 256:512], LW[:, :, 256:512], [])
        hb = [hx[k] + hc[k] for k in range(8)]
        HX, LX = HW[:, :, 0:256], LW[:, :, 0:256]

        rotate(BK[0:3] + BK[4:8])
        adan = [8]

        def two_ada():
            for _ in range(2):
                if adan[0] < 24:
                    PE.wait(AUX.free)
                    t = ada_chunk(adan[0])
                    adan[0] += 1
                    two_ada.tok = t

        def lin_tm(ntt, nk=8, ncols=256, c0=0, H=HW, L=LW, toks=hb):
            h, l, wt = blocks(get(), nk)
            outs = []
            for a in range(ntt):
                if a % 2 == 0:
                    b = bank()
                o = b[:, (a % 2) * 256:(a % 2) * 256 + ncols]
                for k in range(nk):
                    xs = slice(a * 128, a * 128 + 128)
                    tok = mm3(o, H[:, k, xs], L[:, k, xs], h[:, k, c0:c0 + ncols], l[:, k, c0:c0 + ncols],
                              k == 0, k == nk - 1, wt, toks[k], inc=(k == nk - 1))
                if a % 2 == 1:
                    outs.append((b, tok))
            done(tok)
            return outs

        for i in range(2):
            (b, t), = lin_tm(2, toks=hx)
            tp = act(PTM[:, :, i * 256:i * 256 + 256], b.two(), ACT.Copy, t)
            b.free = [tp]
            two_ada()
        pool_free = []
        for gp in range(2):
            b = bank()
            for g in (2 * gp, 2 * gp + 1):
                for a in range(2):
                    t = mm(b[:, (g % 2) * 256:(g % 2) * 256 + 256], PTM[:, a, g * 128:(g + 1) * 128], POOLM[:, a, g, :],
                           a == 0, a == 1, tp, t_pm, inc=(a == 1))
            tpy = act(PY[:, 2 * gp:2 * gp + 2, :], b.two(), ACT.Copy, t)
            b.free = [tpy]
        for gp in range(2):
            b = bank()
            for g in (2 * gp, 2 * gp + 1):
                t = mm(b[:, (g % 2) * 256:(g % 2) * 256 + 256], WPOOL[:, g, :], PY[:, g, :], True, True, tpy, inc=True)
            for g in (2 * gp, 2 * gp + 1):
                u = ts(PY[:, g, :], b[:, (g % 2) * 256:(g % 2) * 256 + 256], par("pscale")[:, g:g + 1], None, ALU.mult, None, t)
                b.free = [u]
                ypool = split_into(YH[:, 4 + g, :], YL[:, 4 + g, :], PY[:, g, :], u)
        ytoks = [None] * 12
        for g in range(4):
            ytoks[4 + g] = ypool

        arena_at[0] = 0
        ph = everyone()
        SCM, GLM = ar(512), ar(256, 2)
        d_s = Dma("d_s")
        t_sm = d_s.go(SY, SCM, D["cst"][:, co["scanm"][0]:co["scanm"][1]], ph)
        t_sm = d_s.go(SY, GLM.rearrange("p a t -> p (a t)"), D["cst"][:, co["glam"][0]:co["glam"][1]], ph)
        WDEC = ar(512)
        t_wd = d_s.go(SY, WDEC[0:32, :], D["w_dec"], ph)
        t_sm = t_wd
        WDEC3 = WDEC.rearrange("p (d c) -> p d c", d=2)
        VT = ar(2048, 4)
        KS, QS, GS = ar(1024, 2), ar(512, 2), ar(1024, 4)
        QB, KB = ar(1024, 4), ar(1024, 4)
        KST = ar(2048).rearrange("p (j a d) -> p j a d", j=4, a=4)
        DV.wait(ph)
        AC.wait(ph)
        base = arena_at[0]
        ASB = ar(512)
        (b,), t = lin_fm(HW, LW, hb, ncols=128, N=512)
        ta = act(ASB[0:32, :], b[0:32, :], ACT.Copy, t)
        b.free = [ta]
        two_ada()
        (b0, b1), t = lin_fm(HW, LW, hb, ncols=256, N=512)
        tk = act(KS[:, 0, :], b0[:, :], ACT.Copy, t)
        b0.free = [tk]
        tk = act(KS[:, 1, :], b1[:, :], ACT.Copy, t)
        b1.free = [tk]
        two_ada()
        (b,), t = lin_fm(HX, LX, hx)
        tq = act(QS, b.two(), ACT.Copy, t)
        b.free = [tq]
        two_ada()
        LA, MN, CU, E1 = ar(512), ar(512), ar(512), ar(256)
        X1, E2 = ar(256), ar(256)
        DEC = small(16).rearrange("p (j n) -> p j n", j=4)
        tr = {"la": [], "kst": []}

        def decay(j):
            d, m = j // 2, j % 2
            b = bank()
            t = mm(b[:, :], WDEC3[0:32, d, m * 128:(m + 1) * 128], ASB[0:32, :], True, True, ta, t_wd, inc=True)
            bd = par("bdec")[:, j:j + 1]
            t1 = act(LA, b[:, :], ACT.Abs, t, tr["la"], bias=bd)
            t1 = act(LA, LA, ACT.Exp, t1, scale=-1.0)
            t1 = act(LA, LA, ACT.Ln, t1, bias=1.0)
            t2 = ts(MN, b[:, :], bd, 0.0, ALU.add, ALU.min, t, t1)
            b.free = [t2]
            t3 = tt(LA, MN, LA, ALU.subtract, t1, t2)
            t4 = DV.run(lambda e: e.tensor_tensor_scan(CU, SCM, LA, 0.0, ALU.mult, ALU.add), t3, t_sm)
            seg = lambda v: v[:, 0:256].rearrange("p (n c) -> p n c", n=4)
            tot = seg(CU)[:, :, 63:64]
            t5 = act(DEC[:, j, :].unsqueeze(2), tot, ACT.Exp, t4, scale=1.0 / 16)
            totb = tot.broadcast_to([128, 4, 64])
            if d == 0:
                t6 = tt(seg(MN), totb, seg(CU), ALU.subtract, t4)
                t6 = ts(MN[:, 256:512], CU[:, 256:512], CU[:, 511:512], -1.0, ALU.subtract, ALU.mult, t6)
                xx = CU[:, 0:256]
            else:
                t6 = tt(MN, CU, LA, ALU.subtract, t4)
                t6 = tt(seg(X1), totb, seg(MN), ALU.subtract, t6)
                xx = X1
            t7 = act(E1, xx, ACT.Exp, t6, scale=1.0 / 16)
            t8 = act(E2, xx, ACT.Exp, t6, scale=-1.0 / 16)
            t9 = act(LA, MN, ACT.Exp, t6, scale=1.0 / 16)
            u = stt(QB[:, j, :], E1, 0.125, QS[:, m, :], ALU.mult, ALU.mult, t7, tq)
            u = tt(KB[:, j, :], E2, KS[:, m, 0:256], ALU.mult, t8, tk)
            u = tt(LA, LA, KS[:, m, :], ALU.mult, t9)
            bt = bank()
            for a in range(4):
                v = transpose(bt[:, a * 128:(a + 1) * 128], LA[:, a * 128:(a + 1) * 128], ident, u)
            w = act(KST[:, j, :, :], bt[:, :].rearrange("p (a d) -> p a d", a=4), ACT.Copy, v)
            bt.free = [w]
            tr["la"] = [w, v]
            AC.wait(w)
            DV.wait(w)
            return u, w

        qk, ks = [], []
        vtok = []
        for i in range(2):
            for (a, (b, t)) in enumerate(lin_tm(4)):
                w = act(VT[:, 2 * a:2 * a + 2, i * 256:i * 256 + 256], b.two(), ACT.Copy, t)
                b.free = [w]
                vtok.append(w)
            two_ada()
            for j in (2 * i, 2 * i + 1):
                u, w = decay(j)
                qk.append(u)
                ks.append(w)
        for i in range(2):
            (b,), t = lin_fm(HX, LX, hx)
            tg = act(GS[:, 2 * i:2 * i + 2, :], b.two(), ACT.Silu, t)
            b.free = [tg]
            two_ada()
        PE.wait(vtok)
        ph = everyone()
        DV.wait(ph)
        AC.wait(ph)
        arena_at[0] = base
        ST = ar(2048).rearrange("p (j n d) -> p j n d", j=4, n=4)
        SM = [ar(512), ar(512)]
        for j in range(4):
            m = j % 2
            d = j // 2
            b = bank()
            for a in (2, 3):
                t = mm(b[:, 0:256], KST[:, j, a, :], VT[:, a, m * 256:m * 256 + 256], a == 2, a == 3, ks, inc=(a == 3))
            order_n = [0, 1, 2, 3] if d == 0 else [3, 2, 1, 0]
            prev = None
            for r in range(2):
                p = slice(64 * r, 64 * r + 64)
                u = vcopy(ST[p, j, order_n[0], :], b[p, r * 128:r * 128 + 128], t)
            b.free = [u]
            for s in range(3):
                n, nn = order_n[s], order_n[s + 1]
                p = slice(64 * (n % 2), 64 * (n % 2) + 64)
                b = bank()
                t = mm(b[:, 0:256], KST[p, j, n // 2, :], VT[p, n // 2, m * 256:m * 256 + 256], True, True, inc=True)
                for r in range(2):
                    p = slice(64 * r, 64 * r + 64)
                    v = stt(ST[p, j, nn, :], ST[p, j, n, :], DEC[p, j, n:n + 1], b[p, r * 128:r * 128 + 128],
                            ALU.mult, ALU.add, t, u)
                u = v
                b.free = [u]
        st_tok = u
        OTT = KS.rearrange("p k t -> p (k t)").rearrange("p (k t) -> p k t", k=4)
        sqt = QS.rearrange("p k t -> p (k t)")
        rst = SCM
        smfree = [[], []]
        otok = []
        for h in range(4):
            m, p = h // 2, slice(64 * (h % 2), 64 * (h % 2) + 64)
            b = bank()
            for d in range(2):
                for a in range(2):
                    c = slice(a * 128, a * 128 + 128)
                    t = mm(b[:, (d * 2 + a) * 128:(d * 2 + a) * 128 + 128], KB[p, 2 * d + m, c], QB[p, 2 * d + m, c],
                           True, True, qk, inc=True)
            s = SM[h % 2].rearrange("p (d a i) -> p d a i", d=2, a=2)
            for d in range(2):
                u = tt(s[:, d, :, :], b[:, d * 256:d * 256 + 256].rearrange("p (a i) -> p a i", a=2),
                       GLM[:, d, :].unsqueeze(1).broadcast_to([128, 2, 128]), ALU.mult, t, smfree[h % 2])
            b.free = [u]
            b = bank()
            for a in range(2):
                o = b[:, a * 128:a * 128 + 128]
                for d in range(2):
                    mm(o, VT[:, a, h * 128:h * 128 + 128], s[:, d, a, :], a == 0 and d == 0, False, u)
                    for n in (2 * a, 2 * a + 1):
                        t = mm(b[:, n * 64:n * 64 + 64], ST[p, 2 * d + m, n, :], QB[p, 2 * d + m, n * 64:n * 64 + 64],
                               False, d == 1, st_tok, inc=True)
            smfree[h % 2] = [t]
            w = act(OTT[:, h, :], b[:, 0:256], ACT.Copy, t)
            b.free = [w]
            otok.append(w)
        for hp in range(2):
            o2 = OTT[:, 2 * hp:2 * hp + 2, :].rearrange("p a t -> p (a t)")
            a = act(sqt, o2, ACT.Square, otok, PE.last())
            b = bank()
            t = mm(b[:, :], ones, sqt, True, True, a, inc=True)
            a = act(rst, b[:, :], ACT.Sqrt, t, DV.last(), scale=1.0 / 128, bias=EPSA)
            b.free = [a]
            r = recip(rst, rst, a)
            u = stt(o2, o2, par("glag"), rst, ALU.mult, ALU.mult, r)
            u = tt(o2, o2, GS[:, 2 * hp:2 * hp + 2, :].rearrange("p a t -> p (a t)"), ALU.mult, u, tg)
            y = split_into(YH[:, 2 * hp:2 * hp + 2, :], YL[:, 2 * hp:2 * hp + 2, :], OTT[:, 2 * hp:2 * hp + 2, :], u)
            ytoks[2 * hp] = ytoks[2 * hp + 1] = y
        while adan[0] < 24:
            two_ada()
        t1 = tt(MOD3[:, 16:48, :], AUX[:, 32:96].rearrange("p (n c) -> p n c", c=2), BA[:, 16:48, :].broadcast_to([128, 32, 2]),
                ALU.add, two_ada.tok)
        AUX.free = [t1]
        GTA, SHM, GTM = (MOD3[:, a:a + 8, 0] for a in (16, 24, 40))
        A2, B2, G2, G3 = small(8), small(8), small(8), small(8)
        vcopy(B2, SHM, t1)
        vcopy(G2, GTA, t1)
        vcopy(G3, GTM, t1)
        t_mod = stt(A2, MOD3[:, 32:40, 0], 1.0, par("norm2"), ALU.add, ALU.mult, t1)
        DV.wait(t_mod)
        AC.wait(t_mod)

        def add_out(b, i, t, gate):
            for r in range(2):
                k = 2 * i + r
                s = gate if isinstance(gate, float) else gate[:, k:k + 1]
                u = stt(XT[:, k, :], b[:, r * 256:r * 256 + 256], s, XT[:, k, :], ALU.mult, ALU.add, t)
            b.free = [u]
            return u

        def stats(b, i, u):
            for k in (2 * i, 2 * i + 1):
                s = stat_step(XT[:, k, :], b, k, 8, u)
            return s

        def project(yh, yl, toks, gate, rots):
            rotate(rots)
            PE.wait(AUX.free)
            for i in range(4):
                (b,), t = lin_fm(yh, yl, toks)
                u = add_out(b, i, t, gate)
                s = stats(AUX, i, u)
            return s

        s = project(YH, YL, ytoks, G2, BK[0:3] + BK[4:8])
        norm.src = XT
        H0, L0 = half(HHt, 0), half(HLt, 0)
        ht = norm(AUX, s, A2, B2, H0, L0, PE.last())

        arena_at[0] = 0
        ph = everyone()
        DV.wait(ph)
        AC.wait(ph)
        rotate(BK[0:3])
        LG = ar(72).rearrange("p (a e) -> p a e", a=2)
        h, l, wt = blocks(get(), 8)
        b = bank()
        for a in range(2):
            for k in range(8):
                xs = slice(a * 128, a * 128 + 128)
                t = mm3(b[:, a * 64:a * 64 + 36], H0[:, k, xs], L0[:, k, xs], h[:, k, 0:36], l[:, k, 0:36],
                        k == 0, k == 7, wt, ht[k], inc=(k == 7))
        done(t)
        u = vcopy(LG, b[:, 0:128].rearrange("p (a e) -> p a e", a=2)[:, :, 0:36], t)
        b.free = [u]
        mg, e4, sg, gp = ar(2).unsqueeze(2), ar(8).rearrange("p (a g) -> p a g", a=2), ar(2).unsqueeze(2), ar(2).unsqueeze(2)
        L4, L32 = LG[:, :, 0:4], LG[:, :, 4:36].rearrange("p a (g j) -> p a g j", g=4)
        v1 = rmax(mg, L4, u)
        u = tt(e4, L4, mg.broadcast_to([128, 2, 4]), ALU.subtract, v1)
        w = act(e4, e4, ACT.Exp, u)
        u = rsum(sg, e4, w)
        u = recip(gp, sg, u)
        IW = cst("idxw")

        def first_max(x, mx, n, *toks):
            key, oh, km = ar(2 * n).rearrange("p (a j) -> p a j", a=2), ar(2 * n).rearrange("p (a j) -> p a j", a=2), ar(2).unsqueeze(2)
            u = tt(key, x, mx.broadcast_to([128, 2, n]), ALU.is_equal, *toks)
            u = tt(key, key, IW[:, 0:n].unsqueeze(1).broadcast_to([128, 2, n]), ALU.mult, u)
            u = rmax(km, key, u)
            u = tt(oh, key, km.broadcast_to([128, 2, n]), ALU.is_equal, u)
            return oh, u

        ohg, ug = first_max(L4, mg, 4, v1)
        sel = ar(64).rearrange("p (a g j) -> p a g j", a=2, g=4)
        ug2 = None
        for a in range(2):
            ug2 = tt(sel[:, a], L32[:, a], ohg[:, a, :].unsqueeze(2).broadcast_to([128, 4, 8]), ALU.mult, ug)
        le = ar(16).rearrange("p (a j) -> p a j", a=2)
        for a in range(2):
            u = rsum(le[:, a, :].unsqueeze(2), sel[:, a].rearrange("p g j -> p j g"), ug2)
        m1, m2 = ar(2).unsqueeze(2), ar(2).unsqueeze(2)
        u1 = rmax(m1, le, u)
        oh1, u = first_max(le, m1, 8, u1)
        le2 = ar(16).rearrange("p (a j) -> p a j", a=2)
        u = stt(le2, oh1, -3e38, le, ALU.mult, ALU.add, u)
        u2 = rmax(m2, le2, u)
        oh2, u = first_max(le2, m2, 8, u2)
        ex, w1, w2, sd = ar(2).unsqueeze(2), ar(2).unsqueeze(2), ar(2).unsqueeze(2), ar(2).unsqueeze(2)
        u = tt(ex, m2, m1, ALU.subtract, u)
        w = act(ex, ex, ACT.Exp, u)
        u = ts(sd, ex, 1.0, None, ALU.add, None, w)
        u = recip(sd, sd, u)
        u = tt(w1, sd, gp, ALU.mult, u)
        u = tt(w2, w1, ex, ALU.mult, u)
        u = tt(oh1, oh1, w1.broadcast_to([128, 2, 8]), ALU.mult, u)
        u = tt(oh2, oh2, w2.broadcast_to([128, 2, 8]), ALU.mult, u)
        u = tt(oh1, oh1, oh2, ALU.add, u)
        G32 = ar(64).rearrange("p (a g j) -> p a g j", a=2, g=4)
        for a in range(2):
            ug = tt(G32[:, a], ohg[:, a, :].unsqueeze(2).broadcast_to([128, 4, 8]), oh1[:, a, :].unsqueeze(1).broadcast_to([128, 4, 8]),
                    ALU.mult, u)
        GT = ar(256)
        b = bank()
        for a in range(2):
            t = transpose(b[0:32, a * 128:a * 128 + 128], G32[:, a].rearrange("p g j -> p (g j)"), ident, ug)
        t_gt = act(GT[0:32, :], b[0:32, 0:256], ACT.Copy, t)
        b.free = [t_gt]

        def swiglu(n, ht, H, L, gated, scale, SB, TB):
            rotate(BK[0:3])
            ahl = [None, None]
            pend = None
            sfr, tfr, afr = [[], []], [[], []], [[PE.last()], [PE.last()]]

            def down(i, toks):
                h, l, wt = blocks(get(), 2)
                y = 4 * (i % 2)
                res = []
                for nb in range(8):
                    bb = YB[nb // 2]
                    if i == 0 and nb % 2 == 0:
                        PE.wait(bb.free)
                    for k in range(2):
                        t = mm3(bb[:, (nb % 2) * 256:(nb % 2) * 256 + 256], h[:, k, nb * 128:nb * 128 + 128],
                                l[:, k, nb * 128:nb * 128 + 128], YH[:, y + k, :], YL[:, y + k, :],
                                i == 0 and nb % 2 == 0 and k == 0, i == n - 1 and k == 1, wt, toks, inc=(k == 1))
                    res.append(t)
                done(t)
                afr[i % 2] = [t]
                return res

            for i in range(n):
                (bg,), tg = lin_fm(H, L, ht)
                if gated:
                    PE.wait(AUX.free)
                    ta = mm(AUX[:, 0:256], ident[0:32, i:i + 1].broadcast_to([32, 128]), GT[0:32, :], True, True, t_gt, inc=True)
                (bu,), tu = lin_fm(H, L, ht)
                S, T = SB[i % 2], TB[i % 2]
                u = act(S, bg.two(), ACT.Silu, tg, sfr[i % 2])
                bg.free = [u]
                if gated:
                    u = tt(S, S, AUX[:, 0:256].unsqueeze(1).broadcast_to([128, 2, 256]), ALU.mult, u, ta)
                    AUX.free = [u]
                u = tt(T, S, bu.two(), ALU.mult, u, tu, tfr[i % 2])
                bu.free = [u]
                sfr[i % 2] = [u]
                y = 4 * (i % 2)
                toks = split_into(YH[:, y:y + 2, :], YL[:, y:y + 2, :], T, u, afr[i % 2])
                tfr[i % 2] = toks
                if pend is not None:
                    down(*pend)
                pend = (i, toks)
            res = down(*pend)
            PE.wait(AUX.free)
            for i in range(4):
                u = add_out(YB[i], i, res[2 * i + 1], scale)
                s = stats(AUX, i, u)
            return s

        SB, TB = [ar(512, 2), ar(512, 2)], [ar(512, 2), ar(512, 2)]
        s = swiglu(32, ht, H0, L0, True, G3, SB, TB)
        t = rstd(AUX, s, 1.0 / 1024, EPSA)
        for k in range(8):
            u = stt(XT[:, k, :], XT[:, k, :], par("final1")[:, k:k + 1], RS[:, :], ALU.mult, ALU.mult, t, AC.last())
            if k % 2:
                s = stats(AUX, k // 2, u) if k > 1 else (PE.wait(AUX.free), stats(AUX, 0, u))[1]
        rsfree[0] = [u]
        norm.src = XT
        ht = norm(AUX, s, par("ffn1n"), None, H0, L0, PE.last())
        s = swiglu(11, ht, H0, L0, False, 0.5, SB, TB)
        ht = norm(AUX, s, par("mixn"), None, H0, L0, PE.last())

        ph = everyone()
        DV.wait(ph)
        AC.wait(ph)
        arena_at[0] = 0
        rotate(BK)
        COS, SIN = ar(512, 2), ar(512, 2)
        DECM = ar(1536).rearrange("p (h c) -> p h c", h=4)
        d_q = Dma("d_q")
        t_dec = d_q.go(SY, DECM.rearrange("p h c -> p (h c)"), D["cst"][:, co["dec"][0]:co["dec"][1]], ph)
        POSI = sb("posi", [128, 256], i32)
        d_pos = Dma("d_pos")
        t_pos = d_pos.go(SY, POSI[:, :], D["pos"].broadcast_to([128, 256]))
        mark = arena_at[0]
        ANG, KK, RR = ar(512, 2), ar(512, 2), ar(512, 2)
        PF = ar(256)
        u = vcopy(PF, POSI[:, :], t_pos)
        for i in range(2):
            u = ts(ANG[:, i, :], PF, cst("inv")[:, i:i + 1], None, ALU.mult, None, u)
        MAGIC = 12582912.0
        C1, C2 = 6.28125, float(np.float32(0.0019340515136718750))
        C3 = float(2 * np.pi - 6.28125 - np.float64(C2))
        u = ts(KK, ANG, float(1 / (2 * np.pi)), MAGIC, ALU.mult, ALU.add, u)
        u = ts(KK, KK, -MAGIC, None, ALU.add, None, u)
        u = stt(RR, KK, -C1, ANG, ALU.mult, ALU.add, u)
        u = stt(RR, KK, -C2, RR, ALU.mult, ALU.add, u)
        u = stt(RR, KK, -C3, RR, ALU.mult, ALU.add, u)
        PI = 3.1415925
        v = ts(ANG, RR, PI, -PI, ALU.min, ALU.max, u)
        w = act(SIN, ANG, ACT.Sin, v)
        u = ts(RR, RR, float(np.pi / 2), None, ALU.add, None, v)
        u = ts(KK, RR, float(np.pi), float(-2 * np.pi), ALU.is_gt, ALU.mult, u)
        u = tt(RR, RR, KK, ALU.add, u)
        u = ts(RR, RR, PI, -PI, ALU.min, ALU.max, u)
        t_rope = [act(COS, RR, ACT.Sin, u), w]
        AC.wait(t_rope)
        DV.wait(t_rope)
        arena_at[0] = mark
        TR = [ar(512, 2), ar(512, 2)]
        TA = ar(512, 2)
        trf = [[], []]
        trn = [0]

        def rope(b, n, t, kind, dst):
            i = trn[0] % 2
            trn[0] += 1
            T = TR[i][:, 0:n, :]
            w = act(T, b.two()[:, 0:n, :], ACT.Copy, t, trf[i])
            b.free = [w]
            b2 = bank()
            t = mm(b2[:, 0:n * 256], cst("rr" if kind else "ra"), T.rearrange("p k t -> p (k t)"), True, True, w, inc=True)
            c = COS[:, kind, :].unsqueeze(1).broadcast_to([128, n, 256])
            s = SIN[:, kind, :].unsqueeze(1).broadcast_to([128, n, 256])
            A = TA[:, 0:n, :]
            u = tt(A, T, c, ALU.mult, w, DV.last())
            u2 = tt(T, b2.two()[:, 0:n, :], s, ALU.mult, t, u)
            b2.free = [u2]
            u = tt(dst, A, T, ALU.add, u, u2)
            trf[i] = [u]
            return u

        IK, IWT = ar(256), small(16).rearrange("p (a h) -> p a h", a=2)
        yn_at = arena_at[0]
        IQ, SCO, WK = ar(1024, 4), ar(512, 2), ar(512, 2)
        MB = ar(512, 2)
        free_at = arena_at[0]
        h, l, wt = blocks(get(), 8)
        b = bank()
        b2 = bank()
        for k in range(8):
            t = mm3(b[:, 0:256], h[:, k, 0:128], l[:, k, 0:128], H0[:, k, :], L0[:, k, :], k == 0, k == 7, wt, ht[k], inc=(k == 7))
        for a in range(2):
            for k in range(8):
                xs = slice(a * 128, a * 128 + 128)
                t2 = mm3(b2[:, a * 8:a * 8 + 8], H0[:, k, xs], L0[:, k, xs], h[:, k, 128:136], l[:, k, 128:136],
                         k == 0, k == 7, inc=(k == 7))
        done(t2)
        w_iw = ts(IWT, b2[:, 0:16].rearrange("p (a h) -> p a h", a=2), float(np.float32(8 ** -0.5)), 0.125, ALU.mult, ALU.mult, t2)
        b2.free = [w_iw]
        t_ik = rope(b, 1, t, 0, IK.unsqueeze(1))
        for i in range(2):
            (b,), t = lin_fm(H0, L0, ht)
            t_iq = rope(b, 2, t, 0, IQ[:, 2 * i:2 * i + 2, :])
        RL = [ar(512, 2), ar(512, 2)]
        rlf = [[], []]
        M8 = small(16).rearrange("p (a h) -> p a h", a=2)

        def indexer():
            n = 0
            ut = None
            for a in range(2):
                for hp in range(4):
                    b = bank()
                    for r in range(2):
                        p = slice(64 * r, 64 * r + 64)
                        t = mm(b[:, r * 256:r * 256 + 256], IQ[p, hp, a * 128:a * 128 + 128], IK[p, :], True, True,
                               t_ik, t_iq, PE.last(), inc=True)
                    R = RL[n % 2]
                    w = act(R, b.two(), ACT.Relu, t, rlf[n % 2])
                    b.free = [w]
                    for r in range(2):
                        hh = 2 * hp + r
                        if hh == 0:
                            ut = ts(SCO[:, a, :], R[:, r, :], IWT[:, a, hh:hh + 1], None, ALU.mult, None, w)
                        else:
                            ut = stt(SCO[:, a, :], R[:, r, :], IWT[:, a, hh:hh + 1], SCO[:, a, :], ALU.mult, ALU.add, w, ut)
                    rlf[n % 2] = [ut]
                    n += 1
                yield
            for p0, p1, a, c in ((0, 64, 0, 64), (64, 128, 0, 128), (0, 64, 1, 192)):
                v = DV.run(lambda e, p0=p0, p1=p1, a=a, c=c: e.memset(SCO[p0:p1, a, c:256], -1e30), ut)
            src = [SCO[:, 0, :], SCO[:, 1, :]]
            prev = [v, v]
            for r in range(8):
                for a in range(2):
                    u = DV.run(lambda e, a=a, s=src[a]: e.max(M8[:, a, :], s), prev[a])
                    prev[a] = DV.run(lambda e, a=a, s=src[a]: e.match_replace(WK[:, a, :], M8[:, a, :], s, -3e38), u)
                    src[a] = WK[:, a, :]
                if r % 2:
                    yield
            u = ts(MB, WK, -3e38, -1e30, ALU.is_gt, ALU.mult, prev)
            indexer.tok = u
            yield

        RQ, RK, RV = ar(1024, 4), ar(1024, 4), ar(2048).rearrange("p (a c) -> p a c", a=2)
        gen = indexer()
        next(gen, None)
        for dst in (RQ, RK):
            for i in range(2):
                (b,), t = lin_fm(H0, L0, ht)
                t_r = rope(b, 2, t, 1, dst[:, 2 * i:2 * i + 2, :])
                next(gen, None)
        for i in range(4):
            (b, t), = lin_tm(2, H=H0, L=L0, toks=ht)
            t_rv = act(RV[:, :, i * 256:i * 256 + 256], b.two(), ACT.Copy, t)
            b.free = [t_rv]
            next(gen, None)
        for _ in gen:
            pass
        YN = ARt[:, yn_at:yn_at + 2048].rearrange("p (k t) -> p k t", k=8)
        AC.wait(indexer.tok, PE.last())
        SR = TR
        srf = [[], []]
        for h4 in range(4):
            b = bank()
            mm(b[:, 0:256], RK[:, h4, 0:128], RQ[:, h4, :], True, True, t_r)
            t = mm(b[:, 256:384], RK[:, h4, 128:256], RQ[:, h4, 128:256], True, True, inc=True)
            S = SR[h4 % 2].rearrange("p k t -> p (k t)")
            u = tt(S[:, 0:384], b[:, 0:384], DECM[:, h4, :], ALU.mult, t, t_dec, srf[h4 % 2], DV.last())
            b.free = [u]
            b = bank()
            for e in range(2):
                c = slice(h4 * 256 + e * 128, h4 * 256 + e * 128 + 128)
                mm(b[:, e * 256:e * 256 + 256], RV[:, 0, c], S[:, 0:256], e == 0, False, u, t_rv)
                t = mm(b[:, e * 256 + 128:e * 256 + 256], RV[:, 1, c], S[:, 256:384], False, True, inc=True)
            srf[h4 % 2] = [t]
            Y2 = YN[:, 2 * h4:2 * h4 + 2, :]
            w = act(Y2, b.two(), ACT.Copy, t)
            b.free = [w]
            b = bank()
            for e in range(2):
                t = mm(b[:, 0:256], ones, Y2[:, e, :], e == 0, e == 1, w, inc=(e == 1))
            u = stt(Y2, b[:, 0:256].unsqueeze(1).broadcast_to([128, 2, 256]), -1.0 / 256, Y2, ALU.mult, ALU.add, t)
            b.free = [u]
            b = bank()
            for e in range(2):
                i = sqn[0] % 2
                sqn[0] += 1
                w = act(SQ[i][:, :], Y2[:, e, :], ACT.Square, u, sqfree[i])
                t = mm(b[:, 0:256], ones, SQ[i][:, :], e == 0, e == 1, w, inc=True)
                sqfree[i] = [t]
            v = rstd(b, t, 1.0 / 256, EPSG)
            for e in range(2):
                k = 2 * h4 + e
                u = stt(YN[:, k, :], YN[:, k, :], par("retgn")[:, k:k + 1], RS[:, :], ALU.mult, ALU.mult, v)
            rsfree[0] = [u]
        t_yn = u
        ph = everyone()
        DV.wait(ph)
        AC.wait(ph)
        arena_at[0] = free_at
        AQ = ar(1024, 4)
        AK, AV = ar(256), ar(256).rearrange("p (a c) -> p a c", a=2)
        P2 = [ar(512, 2), ar(512, 2)]
        PT = ar(1024).rearrange("p (h s q) -> p h s q", h=2, s=2)
        NM, SS = small(4), small(4)
        for i in range(2):
            (b,), t = lin_fm(H0, L0, ht)
            t_aq = rope(b, 2, t, 0, AQ[:, 2 * i:2 * i + 2, :])
        h, l, wt = blocks(get(), 8)
        b = bank()
        b2 = bank()
        for k in range(8):
            t = mm3(b[:, 0:256], h[:, k, 0:128], l[:, k, 0:128], H0[:, k, :], L0[:, k, :], k == 0, k == 7, wt, inc=(k == 7))
        for a in range(2):
            for k in range(8):
                xs = slice(a * 128, a * 128 + 128)
                t2 = mm3(b2[:, a * 64:a * 64 + 64], H0[:, k, xs], L0[:, k, xs], h[:, k, 128:192], l[:, k, 128:192],
                         k == 0, k == 7, inc=(k == 7))
        done(t2)
        v2 = b2[:, 0:128].rearrange("p (a c) -> p a c", a=2)
        act(AV[:, :, 0:64], v2, ACT.Copy, t2)
        t_av = act(AV[:, :, 64:128], v2, ACT.Copy, t2)
        b2.free = [t_av]
        t_ak = rope(b, 1, t, 0, AK.unsqueeze(1))

        def attention():
            pf = [[], []]
            ptf = []
            n = 0
            for hp in range(4):
                for a in range(2):
                    b = bank()
                    for r in range(2):
                        p = slice(64 * r, 64 * r + 64)
                        t = mm(b[:, r * 256:r * 256 + 256], AQ[p, hp, a * 128:a * 128 + 128], AK[p, :], True, True,
                               t_aq, t_ak, PE.last(), inc=True)
                    P = P2[n % 2]
                    u = stt(P, b.two(), 0.125, MB[:, a, :].unsqueeze(1).broadcast_to([128, 2, 256]), ALU.mult, ALU.add,
                            t, indexer.tok, pf[n % 2])
                    b.free = [u]
                    u = DV.run(lambda e, P=P: e.tensor_reduce(NM[:, 0:2].unsqueeze(2), P, AX.X, ALU.max), u, AC.last())
                    u = ts(NM[:, 2:4], NM[:, 0:2], -1.0, None, ALU.mult, None, u)
                    for r in range(2):
                        w = act(P[:, r, :], P[:, r, :], ACT.Exp, u, DV.last(), bias=NM[:, 2 + r:3 + r], accum_out=SS[:, r:r + 1])
                    u = recip(SS[:, 2:4], SS[:, 0:2], w)
                    for r in range(2):
                        u2 = ts(P[:, r, :], P[:, r, :], SS[:, 2 + r:3 + r], None, ALU.mult, None, u)
                    b = bank()
                    for r in range(2):
                        for s in range(2):
                            t = transpose(b[:, (r * 2 + s) * 128:(r * 2 + s) * 128 + 128], P[:, r, s * 128:s * 128 + 128],
                                          ident, u2)
                    pf[n % 2] = [t]
                    w = act(PT[:, :, :, a * 128:a * 128 + 128], b[:, :].rearrange("p (h s q) -> p h s q", h=2, s=2),
                            ACT.Copy, t, ptf)
                    b.free = [w]
                    n += 1
                    if a == 0:
                        yield
                b = bank()
                for r in range(2):
                    for s in range(2):
                        t = mm(b[:, r * 256:r * 256 + 256], AV[:, s, :], PT[:, r, s, :], s == 0, s == 1, w, t_av, inc=(s == 1))
                ptf = [t]
                for r in range(2):
                    p = slice(64 * r, 64 * r + 64)
                    th = act(YH[p, hp, :], b[p, r * 256:r * 256 + 256], ACT.Copy, t)
                    tl = tt(YL[p, hp, :], b[p, r * 256:r * 256 + 256], YH[p, hp, :].bitcast(f32), ALU.subtract, th)
                    AC.wait(tl)
                b.free = [tl, th]
                ytoks[hp] = [tl, th]
                yield

        gen = attention()
        SG = TR
        sgf = [[], []]
        for h4 in range(4):
            (b,), t = lin_fm(H0, L0, ht)
            S = SG[h4 % 2]
            w = act(S, b.two(), ACT.Silu, t, sgf[h4 % 2], DV.last())
            b.free = [w]
            Y2 = YN[:, 2 * h4:2 * h4 + 2, :]
            u = tt(Y2, Y2, S, ALU.mult, w, t_yn)
            sgf[h4 % 2] = [u]
            y = split_into(YH[:, 4 + 2 * h4:6 + 2 * h4, :], YL[:, 4 + 2 * h4:6 + 2 * h4, :], Y2, u)
            ytoks[4 + 2 * h4] = ytoks[5 + 2 * h4] = y
            next(gen, None)
            next(gen, None)
        for _ in gen:
            pass
        H1, L1 = half(HHt, 1), half(HLt, 1)
        mtoks = [None] * 8
        S1, S2 = TR
        free1 = DV.last()
        for j in range(4):
            (b,), t = lin_fm(H0, L0, ht)
            w1_ = act(S1, b.two(), ACT.Sigmoid, t, DV.last(), AC.last())
            b.free = [w1_]
            (b,), t = lin_fm(YH[:, 0:4, :], YL[:, 0:4, :], ytoks[0:4], nk=4)
            u = tt(S1, S1, b.two(), ALU.mult, w1_, t)
            b.free = [u]
            (b,), t = lin_fm(H0, L0, ht)
            w2_ = act(S2, b.two(), ACT.Sigmoid, t, DV.last(), AC.last())
            b.free = [w2_]
            (b,), t = lin_fm(YH[:, 4:12, :], YL[:, 4:12, :], ytoks[4:12])
            u2 = tt(S2, S2, b.two(), ALU.mult, w2_, t)
            b.free = [u2]
            u = tt(TA, S1, S2, ALU.add, u, u2, AC.last())
            y = split_into(H1[:, 2 * j:2 * j + 2, :], L1[:, 2 * j:2 * j + 2, :], TA, u)
            mtoks[2 * j] = mtoks[2 * j + 1] = y
        s = project(H1, L1, mtoks, 1.0, BK[0:3] + BK[4:8])
        ht = norm(AUX, s, par("ffn2n"), None, H0, L0, PE.last())
        ph = everyone()
        DV.wait(ph)
        AC.wait(ph)
        arena_at[0] = 0
        SB, TB = [ar(512, 2), ar(512, 2)], [ar(512, 2), ar(512, 2)]
        PL = ar(512, 2)
        d_l = Dma("d_l")
        t_pl = d_l.go(SY, PL.rearrange("p k t -> p (k t)"), D["ple"], ph)
        s = swiglu(11, ht, H0, L0, False, 0.5, SB, TB)
        PH, PLO = half(HHt, 1)[:, 0:2, :], half(HLt, 1)[:, 0:2, :]
        t_ph = split_into(PH, PLO, PL, t_pl, PE.last())
        ht = norm(AUX, s, par("plen"), None, H0, L0, PE.last())
        rotate(BK[0:3] + BK[4:8])
        PE.wait(AUX.free)
        S1, S2 = SB
        for j in range(4):
            (b,), t = lin_fm(H0, L0, ht)
            w = act(S1, b.two(), ACT.Sigmoid, t, DV.last())
            b.free = [w]
            (b,), t = lin_fm(PH, PLO, [t_ph, t_ph], nk=2)
            u = tt(S2, S1, b.two(), ALU.mult, w, t)
            b.free = [u]
            xs = XT[:, 2 * j:2 * j + 2, :]
            u = tt(xs, xs, S2, ALU.add, u)
            s = stats(AUX, j, u)
        t = rstd(AUX, s, 1.0 / 1024, EPSA)
        d_o = Dma("d_out")
        for k in range(8):
            u = stt(XT[:, k, :], XT[:, k, :], par("final2")[:, k:k + 1], RS[:, :], ALU.mult, ALU.mult, t, AC.last())
            if k % 2:
                to = d_o.go(SY, out[:, (k - 1) * 256:(k + 1) * 256], XTt[:, (k - 1) * 256:(k + 1) * 256], u)
        SY.wait(to)
        assert st["g"] == len(chunks), (st["g"], len(chunks))

        block = cx.enter_context(nc.Block())

        def play(lane):
            def body(e):
                for f in lane.q:
                    f(e)
            return body

        block.sync(play(SY))
        block.scalar(play(AC))
        block.vector(play(DV))
        block.tensor(play(PE))


def constants():
    f = np.float32
    parts = {}
    parts["ident"] = np.eye(128, dtype=f)
    parts["ones"] = np.ones((128, 128), f)
    for name, half in (("ra", 32), ("rr", 64)):
        R = np.zeros((128, 128), f)
        for m in range(128):
            b, i = m // (2 * half) * 2 * half, m % (2 * half)
            if i < half:
                R[b + i + half, m] = -1
            else:
                R[b + i - half, m] = 1
        parts[name] = R
    inv = np.zeros((128, 2), f)
    for c, half in enumerate((32, 64)):
        t = f(10000.0) ** (-np.arange(half, dtype=f) / f(half))
        inv[:, c] = t[np.arange(128) % half]
    parts["inv"] = inv
    parts["idxw"] = np.tile(np.arange(8, 0, -1, dtype=f), (128, 1))
    sm = np.ones((128, 512), f)
    sm[:, [0, 64, 128, 192, 256]] = 0
    parts["scanm"] = sm
    j, i = np.arange(128)[:, None], np.arange(128)[None, :]
    same = j // 64 == i // 64
    parts["glam"] = np.concatenate([same & (j <= i), same & (j >= i)], 1).astype(f)

    def win(n, w):
        lo = w // 2
        hi = w - 1 - lo
        M = np.zeros((n, n))
        for t in range(n):
            s, e = max(t - lo, 0), min(t + hi + 1, n)
            M[t, s:e] = 1.0 / (e - s)
        return M

    pool = np.zeros((128, 2, 4, 256), f)
    for g, w in enumerate((2, 4, 8, 16)):
        M = np.kron(win(4, w), win(64, w)) - np.eye(256)
        pool[:, :, g, :] = M.T.reshape(2, 128, 256).transpose(1, 0, 2)
    parts["pool"] = pool.reshape(128, -1)
    dec = np.zeros((128, 4, 384))
    for h in range(4):
        lg = np.log1p(-(2.0 ** (-5.0 - h)))
        a, b = np.arange(256)[:, None], np.arange(256)[None, :]
        M = np.exp(lg * np.abs(a - b)) * (a // 64 <= b // 64) * 128 ** -0.5
        dec[:, h, 0:256] = M[0:128]
        dec[:, h, 256:384] = M[128:, 128:]
    parts["dec"] = dec.reshape(128, -1).astype(f)
    return np.ascontiguousarray(np.concatenate([parts[n] for n, _ in CON], 1))


def kernel(**I):
    import concourse.bacc as bacc
    from concourse import mybir
    from concourse.bass_utils import run_bass_kernel_spmd as run

    I = {k: np.asarray(v) for k, v in I.items()}

    def cols(w, lists):
        K = w.shape[0]
        r = w.reshape(K // 128, 128, -1)
        return np.ascontiguousarray(np.stack([r[:, :, c].transpose(1, 0, 2).reshape(128, -1) for c in lists]))

    def even(w, a, b, step=256):
        return cols(w, [np.arange(s, s + step) for s in range(a, b, step)])

    def rows(w):
        K, n = w.shape
        return np.ascontiguousarray(w.reshape(K // 256, 2, 128, n).transpose(0, 2, 1, 3).reshape(K // 256, 128, 2 * n))

    def fm(x):
        t, n = x.shape
        return np.ascontiguousarray(x.T.reshape(n // 128, 128, t).transpose(1, 0, 2).reshape(128, -1))

    col = lambda v: v.reshape(-1, 128).T
    w1 = I["w_in"][0]
    w2 = I["w_in_2"][0]
    A = {}
    A["w_ada"] = even(I["w_ada"][0], 0, 6144)
    w1a = np.zeros((1024, 128), w1.dtype)
    w1a[:, 0:32] = w1[:, 1536:1568]
    A["w1p"] = even(w1, 1568, 2080)
    A["w1a"] = even(w1a, 0, 128, 128)
    A["w1k"] = even(w1, 256, 512)
    A["w1q"] = even(w1, 0, 256)
    A["w1v"] = even(w1, 512, 1024)
    A["w1g"] = even(w1, 1024, 1536)
    A["w_out"] = even(I["w_out"][0], 0, 1024)
    A["w_r"] = even(np.concatenate([I["w_router_group"][0], I["w_router_expert"][0]], 1), 0, 36, 36)
    we = I["w_expert_in"][0]
    e4 = we.reshape(32, 8, 128, 2, 256).transpose(3, 0, 2, 1, 4).reshape(2, 32, 128, 2048)
    A["eg"], A["eu"] = np.ascontiguousarray(e4[0]), np.ascontiguousarray(e4[1])
    A["ed"] = rows(I["w_expert_out"][0].reshape(8192, 1024))
    for n in "12":
        A[f"f{n}g"] = even(I[f"ffn{n}_w_gate_2"][0], 0, 2816)
        A[f"f{n}u"] = even(I[f"ffn{n}_w_up_2"][0], 0, 2816)
        A[f"f{n}d"] = rows(I[f"ffn{n}_w_down_2"][0])
    ra = np.arange
    A["w2ik"] = cols(w2, [np.concatenate([ra(1152, 1216), ra(1152, 1216), ra(1216, 1224)])])
    A["w2iq"] = even(w2, 640, 1152)
    A["w2rq"] = even(w2, 1224, 1736)
    A["w2rk"] = even(w2, 1736, 2248)
    A["w2rv"] = even(w2, 2248, 3272)
    A["w2aq"] = even(w2, 0, 512)
    A["w2kv"] = cols(w2, [np.concatenate([ra(512, 576), ra(512, 576), ra(576, 640)])])
    A["w2rg"] = even(w2, 3272, 4296)
    A["w2ga"] = even(w2, 4296, 5320)
    A["w2gb"] = even(w2, 5320, 6344)
    A["wba"] = even(I["w_branch_a_2"][0], 0, 1024)
    A["wbb"] = even(I["w_branch_b_2"][0], 0, 1024)
    A["w_out2"] = even(I["w_out_2"][0], 0, 1024)
    A["wpg"] = even(I["w_ple_gate_2"][0], 0, 1024)
    A["wpp"] = even(I["w_ple_proj_2"][0], 0, 1024)
    A["x"] = fm(I["x"][0])
    A["ctx"] = fm(I["ctx"][0])
    A["ple"] = fm(I["p_2"][0, 0])
    A["cvec"] = fm(np.stack([I["c"][0], I["c_ctx"]]))
    A["pos"] = np.ascontiguousarray(I["positions_2"])
    A["par"] = np.ascontiguousarray(np.concatenate([
        col(I["norm1_g"]), col(I["b_ada"]), col(I["b_decay"]), col(I["gla_norm_g"]), col(I["pool_scale"]),
        col(I["norm2_g"]), col(I["final_norm_g"]), col(I["ffn1_norm_2"]), col(I["mix_norm_2"]), col(I["ret_gn_2"]),
        col(I["ffn2_norm_2"]), col(I["ple_norm_2"]), col(I["final_norm_2"])], 1))
    A["cst"] = constants()
    A["w_pool"] = np.ascontiguousarray(I["w_pool"][0].transpose(1, 0, 2).reshape(128, 512))
    wd = np.zeros((32, 2, 256), np.float32)
    wd[0:16, 0], wd[16:32, 1] = I["w_decay"][0, 0], I["w_decay"][0, 1]
    A["w_dec"] = wd.reshape(32, 512)

    nc = bacc.Bacc("TRN2", target_bir_lowering=False, num_devices=1)
    D = {n: nc.dram_tensor("in_" + n, a.shape, mybir.dt.from_np(a.dtype), kind="ExternalInput").ap() for n, a in A.items()}
    o = nc.dram_tensor("out0", (128, 2048), mybir.dt.float32, kind="ExternalOutput").ap()
    program(nc, D, o)
    r = run(nc, [{"in_" + n: a for n, a in A.items()}], core_ids=[0])
    y = r.results[0]["out0"].reshape(128, 8, 256).transpose(2, 1, 0).reshape(1, 256, 1024)
    return np.ascontiguousarray(y)
```

```python
import numpy as np

EPS = 1e-6
GN_EPS = 1e-5
PAR = ["norm1", "bada", "bdec", "glag", "pscale", "norm2", "final1", "ffn1n", "mixn", "retgn", "ffn2n", "plen", "final2"]
PARN = [8, 48, 4, 1, 4, 8, 8, 8, 8, 8, 8, 8, 8]
CON = [("ident", 128), ("sel", 2), ("ones", 128), ("ra", 128), ("rr", 128), ("inv", 2), ("idxw", 8), ("scanm", 512),
       ("glam", 256), ("pool", 2048), ("dec", 1536), ("tri", 128), ("iota", 128)]


def offsets(pairs):
    at, out = 0, {}
    for n, k in pairs:
        out[n] = (at, at + k)
        at += k
    return out, at


def program(nc, D, out):
    import concourse.bass as bass
    from concourse import mybir
    from contextlib import ExitStack

    f32, f32r, i32 = mybir.dt.float32, mybir.dt.float32r, mybir.dt.int32
    ALU, ACT, AX = mybir.AluOpType, mybir.ActivationFunctionType, mybir.AxisListType
    cx = ExitStack()

    with cx:
        def sb(name, shape, dt=f32):
            return cx.enter_context(nc.sbuf_tensor(name, shape, dt))

        def sem(name):
            return cx.enter_context(nc.semaphore(name))

        class Lane:
            def __init__(self, name):
                self.sem, self.n, self.q, self.seen = sem("s_" + name), 0, [], {}

            def wait(self, *toks):
                for t in toks:
                    if t is None:
                        continue
                    if isinstance(t, list):
                        self.wait(*t)
                        continue
                    s, v = t
                    if self.seen.get(id(s), 0) < v:
                        self.seen[id(s)] = v
                        self.q.append(lambda e, s=s, v=v: e.wait_ge(s, v))

            def run(self, fn, *toks):
                self.wait(*toks)
                self.n += 1
                self.q.append(lambda e, f=fn, s=self.sem: f(e).then_inc(s, 1))
                return (self.sem, self.n)

            def plain(self, fn, *toks):
                self.wait(*toks)
                self.q.append(fn)

            def last(self):
                return (self.sem, self.n) if self.n else None

        PE, DV, AC, GP, SY = Lane("pe"), Lane("dve"), Lane("act"), Lane("pool"), Lane("sp")

        class Dma:
            def __init__(self, name):
                self.sem, self.n = sem(name), 0

            def go(self, lane, dst, src, *toks):
                self.n += 16
                lane.plain(lambda e, s=self.sem: e.dma_start(dst, src).then_inc(s, 16), *toks)
                return (self.sem, self.n)

        def tt(o, a, b, op, *toks):
            return DV.run(lambda e: e.tensor_tensor(o, a, b, op), *toks)

        def ts(o, a, s1, s2, op0, op1, *toks):
            if op1 is None:
                return DV.run(lambda e: e.tensor_scalar(o, a, s1, None, op0), *toks)
            return DV.run(lambda e: e.tensor_scalar(o, a, s1, s2, op0, op1), *toks)

        def stt(o, a, s, b, op0, op1, *toks):
            return DV.run(lambda e: e.scalar_tensor_tensor(o, a, s, b, op0, op1), *toks)

        def vcopy(o, a, *toks):
            return DV.run(lambda e: e.tensor_copy(o, a), *toks)

        def rmax(o, a, *toks):
            return DV.run(lambda e: e.tensor_reduce(o, a, AX.X, ALU.max), *toks)

        def rsum(o, a, *toks):
            return DV.run(lambda e: e.tensor_reduce(o, a, AX.X, ALU.add), *toks)

        def recip(o, a, *toks):
            return DV.run(lambda e: e.reciprocal(o, a), *toks)

        def act(o, a, fn, *toks, **kw):
            return AC.run(lambda e: e.activation(o, a, fn, **kw), *toks)

        def mm(o, l, r, start, stop, *toks, inc=False):
            f = lambda e: e.matmul(o, l, r, start=start, stop=stop, skip_group_check=True)
            if inc:
                return PE.run(f, *toks)
            PE.plain(f, *toks)

        def mm3(o, lh, ll, rh, rl, start, stop, *toks, inc=False):
            PE.wait(*toks)
            mm(o, lh, rh, start, False)
            mm(o, lh, rl, False, False)
            return mm(o, ll, rh, False, stop, inc=inc)

        def transpose(o, a, idn, *toks):
            return PE.run(lambda e: e.transpose(o, a, idn), *toks)

        co, ncon = offsets(CON)
        po, npar = offsets(list(zip(PAR, PARN)))
        NR, NS = 4, 3
        RAW = [sb(f"raw{i}", [128, 2048]) for i in range(NR)]
        WH = [sb(f"wh{i}", [128, 2048], f32r) for i in range(NS)]
        WL = [sb(f"wl{i}", [128, 2048], f32r) for i in range(NS)]
        XTt = sb("xt", [128, 2048])
        XT = XTt[:, :].rearrange("p (k t) -> p k t", k=8)
        HHt, HLt = sb("hh", [128, 4096], f32r), sb("hl", [128, 4096], f32r)
        YHt, YLt = sb("yh", [128, 3072], f32r), sb("yl", [128, 3072], f32r)
        wide = lambda T: T[:, :].rearrange("p (k t) -> p k t", k=8)
        half = lambda T, i: T[:, 2048 * i:2048 * i + 2048].rearrange("p (k t) -> p k t", k=8)
        YH = YHt[:, :].rearrange("p (k t) -> p k t", k=12)
        YL = YLt[:, :].rearrange("p (k t) -> p k t", k=12)
        CS = sb("csts", [128, co["scanm"][0]])
        PR = sb("par", [128, npar])
        cst = lambda n: CS[:, co[n][0]:co[n][1]]
        par = lambda n: PR[:, po[n][0]:po[n][1]]
        ident, ones = cst("ident"), cst("ones")
        SMt = sb("small", [128, 512])
        ROWt = sb("row", [4, 512])
        AR = 13312
        ARt = sb("arena", [128, AR])
        small_at, arena_at, arena_free = [0], [0], [[]]

        def small(n):
            small_at[0] += n
            assert small_at[0] <= 512
            return SMt[:, small_at[0] - n:small_at[0]]

        def ar(n, k=None):
            arena_at[0] += n
            assert arena_at[0] <= AR, arena_at[0]
            v = ARt[:, arena_at[0] - n:arena_at[0]]
            return v if k is None else v.rearrange("p (k t) -> p k t", k=k)

        def everyone():
            return [t for t in (PE.last(), DV.last(), AC.last()) if t]

        class Bank:
            def __init__(self, i):
                self.t = cx.enter_context(nc.psum_tensor(f"bank{i}", [128, 512], f32))
                self.free = []

            def __getitem__(self, k):
                return self.t[k]

            def two(self):
                return self.t[:, :].rearrange("p (k t) -> p k t", k=2)

        BK = [Bank(i) for i in range(8)]
        AUX, YB = BK[3], BK[4:8]
        rot = {"l": BK[0:3], "i": 0}

        def rotate(banks):
            rot["l"], rot["i"] = banks, 0

        def bank():
            b = rot["l"][rot["i"] % len(rot["l"])]
            rot["i"] += 1
            PE.wait(b.free)
            b.free = []
            return b

        chunks = []

        def add(name, i, split=True):
            a = D[name]
            chunks.append((a[i], a.shape[2], split))

        for i in range(8):
            add("w_ada", i)
        ada = list(range(8, 24))
        FIRST = [("p", 0, 1), ("p", 1, 1), ("a", 0, 1), ("k", 0, 1), ("q", 0, 1), ("v", 0, 1), ("v", 1, 1), ("g", 0, 4), ("g", 1, 5)]
        for n, i, m in FIRST:
            add("w1" + n, i)
            for _ in range(m):
                add("w_ada", ada.pop(0))
        for i in range(4):
            add("w_out", i)
        add("w_r", 0)

        def ffn_chunks(g, u, d, n):
            for i in range(n):
                add(g, i)
                add(u, i)
                if i:
                    add(d, i - 1)
            add(d, n - 1)

        ffn_chunks("eg", "eu", "ed", 32)
        ffn_chunks("f1g", "f1u", "f1d", 11)
        for n, k in [("ik", 1), ("iq", 2), ("rq", 2), ("rk", 2), ("rv", 4), ("aq", 2), ("kv", 1), ("rg", 4)]:
            for i in range(k):
                add("w2" + n, i)
        for j in range(4):
            for n in ("w2ga", "wba", "w2gb", "wbb"):
                add(n, j)
        for i in range(4):
            add("w_out2", i)
        ffn_chunks("f2g", "f2u", "f2d", 11)
        for j in range(4):
            add("wpg", j)
            add("wpp", j)

        RD = [Dma(f"d_raw{i}") for i in range(NR)]
        released = {}
        sfree = [[] for _ in range(NS)]
        st = {"f": 0, "s": 0, "g": 0, "k": 0, "held": None}
        loaded, parts = {}, {}

        def fetch():
            while st["f"] < len(chunks) and (st["f"] < NR or st["f"] - NR in released):
                i = st["f"]
                st["f"] += 1
                src, n, _ = chunks[i]
                loaded[i] = RD[i % NR].go(SY, RAW[i % NR][:, 0:n], src, released.get(i - NR))

        def split():
            i = st["s"]
            if i >= len(chunks):
                return
            st["s"] += 1
            _, n, sp = chunks[i]
            r = RAW[i % NR][:, 0:n]
            if not sp:
                parts[i] = (r, None, [loaded[i]], None)
                return
            s = st["k"] % NS
            st["k"] += 1
            h, l = WH[s][:, 0:n], WL[s][:, 0:n]
            th = act(h, r, ACT.Copy, loaded[i], sfree[s])
            tl = tt(l, r, h.bitcast(f32), ALU.subtract, th, loaded[i], sfree[s])
            parts[i] = (h, l, [th, tl], s)
            released[i] = [tl, th]
            fetch()

        def get():
            i = st["g"]
            st["g"] += 1
            while st["s"] <= min(i + 2, len(chunks) - 1):
                split()
            st["held"] = i
            return parts[i]

        def done(tok):
            i = st["held"]
            if chunks[i][2]:
                sfree[parts[i][3]] = [tok]
            else:
                released[i] = [tok]
                fetch()

        def blocks(part, nk):
            h, l, toks, _ = part
            v = lambda a: a if a is None else a.rearrange("p (k n) -> p k n", k=nk)
            return v(h), v(l), toks

        def lin_fm(xh, xl, xtoks, nk=8, ncols=256, N=256, width=128):
            h, l, wt = blocks(get(), nk)
            outs = []
            nb = ncols // width
            per = 512 // N
            tok = None
            for m in range(nb):
                if m % per == 0:
                    b = bank()
                    outs.append(b)
                o = b[:, (m % per) * N:(m % per) * N + N]
                for k in range(nk):
                    tok = mm3(o, h[:, k, m * width:(m + 1) * width], l[:, k, m * width:(m + 1) * width],
                              xh[:, k, :], xl[:, k, :], k == 0, k == nk - 1, wt, xtoks[k], inc=(k == nk - 1))
            done(tok)
            return outs, tok

        def split_into(h, l, src, *toks):
            th = act(h, src, ACT.Copy, *toks)
            tl = tt(l, src, h.bitcast(f32), ALU.subtract, th, *toks)
            return [th, tl]

        SQ = [sb("sq0", [128, 256]), sb("sq1", [128, 256])]
        sqfree = [[], []]
        RS = sb("rstd", [128, 256])
        rsfree = [[]]
        sqn = [0]

        def stat_step(src, b, k, n, *toks):
            i = sqn[0] % 2
            sqn[0] += 1
            a = act(SQ[i][:, :], src, ACT.Square, sqfree[i], *toks)
            t = mm(b[:, 0:256], ones, SQ[i][:, :], k == 0, k == n - 1, a, inc=True)
            sqfree[i] = [t]
            return t

        def rstd(b, tok, scale, eps_ap):
            a = act(RS[:, :], b[:, 0:256], ACT.Sqrt, tok, rsfree[0], scale=scale, bias=eps_ap)
            b.free = [a]
            return recip(RS[:, :], RS[:, :], a)

        TN = [sb("tn0", [128, 256]), sb("tn1", [128, 256])]
        tnfree = [[], []]

        def norm(b, tok, gain, shift, H, L, free):
            t = rstd(b, tok, 1.0 / 1024, EPSA)
            out_t = []
            for k in range(8):
                i = k % 2
                u = stt(TN[i][:, :], norm.src[:, k, :], gain[:, k:k + 1], RS[:, :], ALU.mult, ALU.mult, t, tnfree[i])
                if shift is None:
                    th = act(H[:, k, :], TN[i][:, :], ACT.Copy, u, free)
                    tl = tt(L[:, k, :], TN[i][:, :], H[:, k, :].bitcast(f32), ALU.subtract, th, free)
                else:
                    th = act(H[:, k, :], TN[i][:, :], ACT.Identity, u, free, bias=shift[:, k:k + 1])
                    tl = stt(L[:, k, :], TN[i][:, :], shift[:, k:k + 1], H[:, k, :].bitcast(f32),
                             ALU.add, ALU.subtract, th, free)
                tnfree[i] = [tl]
                out_t.append([th, tl])
            rsfree[0] = [u]
            return out_t

        d_c, d_x, d_ct, d_p, d_a0, d_m = (Dma(n) for n in ("d_c", "d_x", "d_ct", "d_p", "d_a0", "d_m"))
        EPSA = small(1)
        EPSG = small(1)
        te = DV.run(lambda e: e.memset(EPSA, EPS))
        te = DV.run(lambda e: e.memset(EPSG, GN_EPS))
        AC.wait(te)
        cv = small(16)
        CT = ar(2048, 8)
        POOLM = ar(2048).rearrange("p (a g t) -> p a g t", a=2, g=4)
        t_cv = d_c.go(AC, cv, D["cvec"])
        t_par = d_p.go(AC, PR[:, :], D["par"])
        t_cs = d_p.go(AC, CS[:, :], D["cst"][:, 0:co["scanm"][0]])
        t_par = t_cs
        t_x = d_x.go(AC, XTt[:, :], D["x"])
        t_ct = d_ct.go(AC, CT.rearrange("p k t -> p (k t)"), D["ctx"])
        WPOOL = ar(512).rearrange("p (g d) -> p g d", g=4)
        t_pm = d_a0.go(AC, POOLM.rearrange("p a g t -> p (a g t)"), D["cst"][:, co["pool"][0]:co["pool"][1]])
        t_pm = d_a0.go(AC, WPOOL.rearrange("p g d -> p (g d)"), D["w_pool"])
        PTM = ar(1024).rearrange("p (a c) -> p a c", a=2)
        PY = ar(1024, 4)
        fetch()

        SC = small(16)
        CV4 = YHt[:, 2048:3072].rearrange("p (k c) -> p k c", k=8)
        CV3 = CV4[:, :, 0:4].rearrange("p k (s c) -> p k s c", s=2)
        AC.wait(DV.run(lambda e: e.memset(YHt[:, 2048:3072].bitcast(f32), 0.0)))
        ROW = [ROWt[:, 0:256], ROWt[:, 256:512]]
        rowfree = [[], []]
        t_sc = act(SC, cv, ACT.Silu, t_cv)
        SC3 = SC.rearrange("p (k c) -> p k c", k=8)
        t_sc = split_into(CV3[:, :, 0, :], CV3[:, :, 1, :], SC3, t_sc)
        MOD = small(96)
        MOD3 = MOD.rearrange("p (n c) -> p n c", c=2)

        ada_pend = []

        def ada_turn():
            if ada_pend:
                c, w = ada_pend.pop()
                for m in range(2):
                    n = 2 * c + m
                    t = mm(AUX[:, 2 * n:2 * n + 2], ROW[c % 2][:, m * 128:(m + 1) * 128], cst("sel")[0:4, :], True, True,
                           w, inc=True)
                rowfree[c % 2] = [t]
                ada_turn.tok = t

        def ada_chunk(c):
            h, l, wt = blocks(get(), 8)
            b = bank()
            for k in range(8):
                mm(b[:, 0:256], CV4[:, k, :], h[:, k, :], k == 0, False, wt[0], t_sc)
                tok = mm(b[:, 0:256], CV4[:, k, :], l[:, k, :], False, k == 7, wt[1], inc=(k == 7))
            done(tok)
            ada_turn()
            w = act(ROW[c % 2], b[0:4, 0:256], ACT.Copy, tok, rowfree[c % 2])
            b.free = [w]
            ada_pend.append((c, w))

        def mod_rows(a, z, tok):
            v = AUX[:, 2 * a:2 * z].rearrange("p (n c) -> p n c", c=2)
            t = tt(MOD3[:, a:z, :], v, BA[:, a:z, :].broadcast_to([128, z - a, 2]), ALU.add, tok, t_par)
            AUX.free = [t]
            return t

        bx, bc = BK[4], BK[5]
        for k in range(8):
            tsx = stat_step(XT[:, k, :], bx, k, 8, t_x, t_cs)
        for k in range(8):
            tsc = stat_step(CT[:, k, :], bc, k, 8, t_ct)
        for c in range(8):
            ada_chunk(c)
        ada_turn()
        tm = ada_turn.tok
        BA = par("bada").unsqueeze(2)
        t1 = mod_rows(0, 16, tm)
        A1, B1 = small(16).rearrange("p (c k) -> p c k", c=2), small(16).rearrange("p (c k) -> p c k", c=2)
        for c in range(2):
            t2 = stt(A1[:, c, :], MOD3[:, 8:16, c], 1.0, par("norm1"), ALU.add, ALU.mult, t1)
            t3 = vcopy(B1[:, c, :], MOD3[:, 0:8, c], t1)
        DV.wait(t2, t3)
        AC.wait(t3)
        HW, LW = wide(HHt), wide(HLt)
        norm.src = XT
        hx = norm(bx, tsx, A1[:, 0, :], B1[:, 0, :], HW[:, :, 0:256], LW[:, :, 0:256], [])
        norm.src = CT
        hc = norm(bc, tsc, A1[:, 1, :], B1[:, 1, :], HW[:, :, 256:512], LW[:, :, 256:512], [])
        hb = [hx[k] + hc[k] for k in range(8)]
        HX, LX = HW[:, :, 0:256], LW[:, :, 0:256]

        rotate(BK[0:3] + BK[4:8])
        adan = [8]
        gens = []

        def tick(n=1):
            for _ in range(n):
                while gens:
                    if next(gens[0], "end") == "end":
                        gens.pop(0)
                    else:
                        break

        def drain():
            while gens:
                tick()

        def some_ada(n):
            for _ in range(n):
                PE.wait(AUX.free)
                ada_chunk(adan[0])
                adan[0] += 1
                tick()

        def lin_tm(ntt, nk=8, ncols=256, c0=0, H=HW, L=LW, toks=hb):
            h, l, wt = blocks(get(), nk)
            outs = []
            for a in range(ntt):
                if a % 2 == 0:
                    b = bank()
                o = b[:, (a % 2) * 256:(a % 2) * 256 + ncols]
                for k in range(nk):
                    xs = slice(a * 128, a * 128 + 128)
                    tok = mm3(o, H[:, k, xs], L[:, k, xs], h[:, k, c0:c0 + ncols], l[:, k, c0:c0 + ncols],
                              k == 0, k == nk - 1, wt, toks[k], inc=(k == nk - 1))
                if a % 2 == 1:
                    outs.append((b, tok))
            done(tok)
            return outs

        for i in range(2):
            (b, t), = lin_tm(2, toks=hx)
            tp = act(PTM[:, :, i * 256:i * 256 + 256], b.two(), ACT.Copy, t)
            b.free = [tp]
            some_ada(1)
        ytoks = [None] * 12

        def pooling():
            tpy = [None, None]
            for gp in range(2):
                b = bank()
                for g in (2 * gp, 2 * gp + 1):
                    for a in range(2):
                        t = mm(b[:, (g % 2) * 256:(g % 2) * 256 + 256], PTM[:, a, g * 128:(g + 1) * 128], POOLM[:, a, g, :],
                               a == 0, a == 1, tp, t_pm, inc=(a == 1))
                tpy[gp] = act(PY[:, 2 * gp:2 * gp + 2, :], b.two(), ACT.Copy, t)
                b.free = [tpy[gp]]
            yield
            for gp in range(2):
                b = bank()
                for g in (2 * gp, 2 * gp + 1):
                    t = mm(b[:, (g % 2) * 256:(g % 2) * 256 + 256], WPOOL[:, g, :], PY[:, g, :], True, True, tpy[gp], inc=True)
                for g in (2 * gp, 2 * gp + 1):
                    u = ts(PY[:, g, :], b[:, (g % 2) * 256:(g % 2) * 256 + 256], par("pscale")[:, g:g + 1], None, ALU.mult, None, t)
                b.free = [u]
                y = split_into(YH[:, 4 + 2 * gp:6 + 2 * gp, :], YL[:, 4 + 2 * gp:6 + 2 * gp, :], PY[:, 2 * gp:2 * gp + 2, :], u)
                ytoks[4 + 2 * gp] = ytoks[5 + 2 * gp] = y

        gens.append(pooling())
        (b,), t_a = lin_fm(HW, LW, hb, ncols=128, N=512)
        bank_a = b
        drain()

        arena_at[0] = 0
        ph = everyone()
        SCM, GLM = ar(512), ar(256, 2)
        d_s = Dma("d_s")
        t_sm = d_s.go(SY, SCM, D["cst"][:, co["scanm"][0]:co["scanm"][1]], ph)
        t_sm = d_s.go(SY, GLM.rearrange("p a t -> p (a t)"), D["cst"][:, co["glam"][0]:co["glam"][1]], ph)
        WDEC = ar(512)
        t_wd = d_s.go(SY, WDEC[0:32, :], D["w_dec"], ph)
        t_sm = t_wd
        WDEC3 = WDEC.rearrange("p (d c) -> p d c", d=2)
        VT = ar(2048, 4)
        KS, QS = ar(1024, 2), ar(512, 2)
        QB, KB = ar(1024, 4), ar(1024, 4)
        LA4 = ar(2048, 4)
        KST = LA4.rearrange("p j (a d) -> p j a d", a=4)
        base = arena_at[0]
        ASB = ar(512)
        MNs, CUs, X1s = [ar(512), ar(512)], [ar(512), ar(512)], [ar(256), ar(256)]
        GS = ar(1024, 4)
        DV.wait(ph)
        AC.wait(ph)
        ta = act(ASB[0:32, :], bank_a[0:32, :], ACT.Copy, t_a)
        bank_a.free = [ta]
        DEC = small(16).rearrange("p (j n) -> p j n", j=4)
        qk, kst_t, vtok, kk = [None] * 4, [None] * 4, [], {}
        trf = [[], []]

        def decays():
            zb, te = [], []
            for j in range(4):
                d, m = j // 2, j % 2
                b = bank()
                t = mm(b[:, :], WDEC3[0:32, d, m * 128:(m + 1) * 128], ASB[0:32, :], True, True, ta, t_wd, inc=True)
                bd = par("bdec")[:, j:j + 1]
                i = j % 2
                t1 = act(LA4[:, j, :], b[:, :], ACT.Abs, t, bias=bd)
                zb.append((b, t1, bd))
            for j in range(4):
                te.append(act(LA4[:, j, :], LA4[:, j, :], ACT.Exp, zb[j][1], scale=-1.0))
            for j in range(4):
                te[j] = act(LA4[:, j, :], LA4[:, j, :], ACT.Ln, te[j], bias=1.0)
            yield
            seg = lambda v: v[:, 0:256].rearrange("p (n c) -> p n c", n=4)

            def first(j):
                d, i = j // 2, j % 2
                MN, CU, X1, LA = MNs[i], CUs[i], X1s[i], LA4[:, j, :]
                b, t1, bd = zb[j]
                t2 = ts(MN, b[:, :], bd, 0.0, ALU.add, ALU.min, t1, trf[i])
                b.free = [t2]
                t3 = tt(LA, MN, LA, ALU.subtract, te[j], t2)
                t4 = DV.run(lambda e: e.tensor_tensor_scan(CU, SCM, LA, 0.0, ALU.mult, ALU.add), t3, t_sm)
                tot = seg(CU)[:, :, 63:64]
                t5 = act(DEC[:, j, :].unsqueeze(2), tot, ACT.Exp, t4, scale=1.0 / 16)
                totb = tot.broadcast_to([128, 4, 64])
                if d == 0:
                    tt(seg(MN), totb, seg(CU), ALU.subtract, t4)
                    t6 = ts(MN[:, 256:512], CU[:, 256:512], CU[:, 511:512], -1.0, ALU.subtract, ALU.mult, t4)
                    xx = CU[:, 0:256]
                else:
                    t6 = tt(MN, CU, LA, ALU.subtract, t4)
                    t6 = tt(seg(X1), totb, seg(MN), ALU.subtract, t6)
                    xx = X1
                t7 = act(QB[:, j, :], xx, ACT.Exp, t6, scale=1.0 / 16)
                t8 = act(KB[:, j, :], xx, ACT.Exp, t6, scale=-1.0 / 16)
                t9 = act(LA, MN, ACT.Exp, t6, scale=1.0 / 16)
                trf[i] = [t9, t5, t8]
                return t7, t8, t9

            def second(j, tk):
                m, LA = j % 2, LA4[:, j, :]
                stt(QB[:, j, :], QB[:, j, :], 0.125, QS[:, m, :], ALU.mult, ALU.mult, tk[0], kk["q"])
                qk[j] = tt(KB[:, j, :], KB[:, j, :], KS[:, m, 0:256], ALU.mult, tk[1], kk["k"])
                return tt(LA, LA, KS[:, m, :], ALU.mult, tk[2])

            def third(j, u):
                bt = bank()
                for a in range(4):
                    v = transpose(bt[:, a * 128:(a + 1) * 128], LA4[:, j, a * 128:(a + 1) * 128], ident, u)
                w = act(KST[:, j, :, :], bt[:, :].rearrange("p (a d) -> p a d", a=4), ACT.Copy, v)
                bt.free = [w]
                kst_t[j] = w

            f, g = {}, {}
            for j in range(6):
                if j < 4:
                    f[j] = first(j)
                if j >= 2:
                    third(j - 2, g[j - 2])
                if 1 <= j < 5:
                    g[j - 1] = second(j - 1, f[j - 1])
                yield

        (some_ada(1))
        (b0, b1), t = lin_fm(HW, LW, hb, ncols=256, N=512)
        tk = act(KS[:, 0, :], b0[:, :], ACT.Copy, t)
        b0.free = [tk]
        kk["k"] = act(KS[:, 1, :], b1[:, :], ACT.Copy, t)
        b1.free = [kk["k"]]
        gens.append(decays())
        tick()
        some_ada(1)
        (b,), t = lin_fm(HX, LX, hx)
        kk["q"] = act(QS, b.two(), ACT.Copy, t)
        b.free = [kk["q"]]
        tick()
        some_ada(1)
        for i in range(2):
            for (a, (b, t)) in enumerate(lin_tm(4)):
                w = act(VT[:, 2 * a:2 * a + 2, i * 256:i * 256 + 256], b.two(), ACT.Copy, t)
                b.free = [w]
                vtok.append(w)
            tick()
            some_ada(1)
        (b,), t = lin_fm(HX, LX, hx)
        tg = act(GS[:, 0:2, :], b.two(), ACT.Silu, t)
        b.free = [tg]
        tick()
        drain()
        ph = everyone()
        arena_at[0] = base
        ST = ar(2048).rearrange("p (j n d) -> p j n d", j=4, n=4)
        SM = [ar(512), ar(512)]
        OTT = KS.rearrange("p k t -> p (k t)").rearrange("p (k t) -> p k t", k=4)
        sqt = QS.rearrange("p k t -> p (k t)")
        rst = SCM
        st_tok, otok = [None] * 4, [None] * 4

        def heads():
            def scores(h):
                m, p = h // 2, slice(64 * (h % 2), 64 * (h % 2) + 64)
                b = bank()
                for d in range(2):
                    for a in range(2):
                        c = slice(a * 128, a * 128 + 128)
                        t = mm(b[:, (d * 2 + a) * 128:(d * 2 + a) * 128 + 128], KB[p, 2 * d + m, c], QB[p, 2 * d + m, c],
                               True, True, qk, inc=True)
                s = SM[h % 2].rearrange("p (d a i) -> p d a i", d=2, a=2)
                for d in range(2):
                    u = tt(s[:, d, :, :], b[:, d * 256:d * 256 + 256].rearrange("p (a i) -> p a i", a=2),
                           GLM[:, d, :].unsqueeze(1).broadcast_to([128, 2, 128]), ALU.mult, t, smfree[h % 2], ph)
                b.free = [u]
                return u

            def states(j):
                d, m = j // 2, j % 2
                b = bank()
                for a in (2, 3):
                    t = mm(b[:, 0:256], KST[:, j, a, :], VT[:, a, m * 256:m * 256 + 256], a == 2, a == 3, kst_t, vtok,
                           inc=(a == 3))
                order_n = [0, 1, 2, 3] if d == 0 else [3, 2, 1, 0]
                for r in range(2):
                    p = slice(64 * r, 64 * r + 64)
                    u = vcopy(ST[p, j, order_n[0], :], b[p, r * 128:r * 128 + 128], t, ph)
                b.free = [u]
                for s in range(3):
                    n, nn = order_n[s], order_n[s + 1]
                    p = slice(64 * (n % 2), 64 * (n % 2) + 64)
                    b = bank()
                    t = mm(b[:, 0:256], KST[p, j, n // 2, :], VT[p, n // 2, m * 256:m * 256 + 256], True, True, inc=True)
                    for r in range(2):
                        p = slice(64 * r, 64 * r + 64)
                        v = stt(ST[p, j, nn, :], ST[p, j, n, :], DEC[p, j, n:n + 1], b[p, r * 128:r * 128 + 128],
                                ALU.mult, ALU.add, t, u)
                    u = v
                    b.free = [u]
                st_tok[j] = u

            def outs(h, u):
                m, p = h // 2, slice(64 * (h % 2), 64 * (h % 2) + 64)
                s = SM[h % 2].rearrange("p (d a i) -> p d a i", d=2, a=2)
                b = bank()
                for a in range(2):
                    o = b[:, a * 128:a * 128 + 128]
                    for d in range(2):
                        mm(o, VT[:, a, h * 128:h * 128 + 128], s[:, d, a, :], a == 0 and d == 0, False, u)
                        for n in (2 * a, 2 * a + 1):
                            t = mm(b[:, n * 64:n * 64 + 64], ST[p, 2 * d + m, n, :], QB[p, 2 * d + m, n * 64:n * 64 + 64],
                                   False, d == 1, st_tok[m], st_tok[2 + m], inc=True)
                smfree[h % 2] = [t]
                w = act(OTT[:, h, :], b[:, 0:256], ACT.Copy, t, ph)
                b.free = [w]
                otok[h] = w

            def gated(hp):
                o2 = OTT[:, 2 * hp:2 * hp + 2, :].rearrange("p a t -> p (a t)")
                a = act(sqt, o2, ACT.Square, otok[2 * hp:2 * hp + 2], gated.free)
                b = bank()
                t = mm(b[:, :], ones, sqt, True, True, a, inc=True)
                a = act(rst, b[:, :], ACT.Sqrt, t, gated.free, scale=1.0 / 128, bias=EPSA)
                b.free = [a]
                r = recip(rst, rst, a)
                u = stt(o2, o2, par("glag"), rst, ALU.mult, ALU.mult, r)
                gated.free = [t, u]
                u = tt(o2, o2, GS[:, 2 * hp:2 * hp + 2, :].rearrange("p a t -> p (a t)"), ALU.mult, u, gtok[hp])
                y = split_into(YH[:, 2 * hp:2 * hp + 2, :], YL[:, 2 * hp:2 * hp + 2, :], OTT[:, 2 * hp:2 * hp + 2, :], u)
                ytoks[2 * hp] = ytoks[2 * hp + 1] = y

            gated.free = [ph]
            smfree = [[], []]
            states(0)
            u0 = scores(0)
            yield
            states(2)
            u1 = scores(1)
            yield
            outs(0, u0)
            states(1)
            u0 = scores(2)
            yield
            outs(1, u1)
            states(3)
            u1 = scores(3)
            yield
            gated(0)
            outs(2, u0)
            yield
            outs(3, u1)
            yield
            gated(1)
            yield

        gtok = [tg, None]
        gens.append(heads())
        some_ada(4)
        (b,), t = lin_fm(HX, LX, hx)
        gtok[1] = tg = act(GS[:, 2:4, :], b.two(), ACT.Silu, t)
        b.free = [tg]
        tick()
        some_ada(5)
        drain()
        ada_turn()
        t1 = mod_rows(16, 48, ada_turn.tok)
        GTA, SHM, GTM = (MOD3[:, a:a + 8, 0] for a in (16, 24, 40))
        A2, B2, G2, G3 = small(8), small(8), small(8), small(8)
        vcopy(B2, SHM, t1)
        vcopy(G2, GTA, t1)
        vcopy(G3, GTM, t1)
        t_mod = stt(A2, MOD3[:, 32:40, 0], 1.0, par("norm2"), ALU.add, ALU.mult, t1)
        DV.wait(t_mod)
        AC.wait(t_mod)

        def add_out(b, i, t, gate):
            for r in range(2):
                k = 2 * i + r
                s = gate if isinstance(gate, float) else gate[:, k:k + 1]
                u = stt(XT[:, k, :], b[:, r * 256:r * 256 + 256], s, XT[:, k, :], ALU.mult, ALU.add, t)
            b.free = [u]
            return u

        def stats(b, i, u):
            for k in (2 * i, 2 * i + 1):
                s = stat_step(XT[:, k, :], b, k, 8, u)
            return s

        def project(yh, yl, toks, gate, rots):
            rotate(rots)
            PE.wait(AUX.free)
            for i in range(4):
                (b,), t = lin_fm(yh, yl, toks)
                u = add_out(b, i, t, gate)
                s = stats(AUX, i, u)
            return s

        s = project(YH, YL, ytoks, G2, BK[0:3] + BK[4:8])
        norm.src = XT
        H0, L0 = half(HHt, 0), half(HLt, 0)
        ht = norm(AUX, s, A2, B2, H0, L0, PE.last())

        arena_at[0] = 0
        ph = everyone()
        DV.wait(ph)
        AC.wait(ph)
        rotate(BK[0:3] + BK[4:8])
        CAP = 128
        TRI, IOTA = ar(128), ar(128)
        d_t = Dma("d_t")
        t_tri = d_t.go(SY, TRI, D["cst"][:, co["tri"][0]:co["tri"][1]], ph)
        t_tri = d_t.go(SY, IOTA, D["cst"][:, co["iota"][0]:co["iota"][1]])
        LG = ar(72).rearrange("p (a e) -> p a e", a=2)
        h, l, wt = blocks(get(), 8)
        b = bank()
        for a in range(2):
            for k in range(8):
                xs = slice(a * 128, a * 128 + 128)
                t = mm3(b[:, a * 64:a * 64 + 36], H0[:, k, xs], L0[:, k, xs], h[:, k, 0:36], l[:, k, 0:36],
                        k == 0, k == 7, wt, ht[k], inc=(k == 7))
        done(t)
        u = vcopy(LG, b[:, 0:128].rearrange("p (a e) -> p a e", a=2)[:, :, 0:36], t)
        b.free = [u]
        TH = HHt[:, 2048:4096].rearrange("p (a f) -> p a f", a=2)
        TL = HLt[:, 2048:4096].rearrange("p (a f) -> p a f", a=2)
        t_tm = []
        free_half = PE.last()
        for src, dst in ((H0, TH), (L0, TL)):
            for a in range(2):
                for kq in range(2):
                    bt = bank()
                    for k in range(4):
                        t = transpose(bt[:, k * 128:(k + 1) * 128], src[:, 4 * kq + k, a * 128:a * 128 + 128].bitcast(f32),
                                      ident, ht)
                    w = act(dst[:, a, kq * 512:kq * 512 + 512], bt[:, :], ACT.Copy, t, free_half)
                    bt.free = [w]
                    t_tm.append(w)
        mg, e4, sg, gp = ar(2).unsqueeze(2), ar(8).rearrange("p (a g) -> p a g", a=2), ar(2).unsqueeze(2), ar(2).unsqueeze(2)
        L4, L32 = LG[:, :, 0:4], LG[:, :, 4:36].rearrange("p a (g j) -> p a g j", g=4)
        v1 = rmax(mg, L4, u)
        u = tt(e4, L4, mg.broadcast_to([128, 2, 4]), ALU.subtract, v1)
        w = act(e4, e4, ACT.Exp, u)
        u = rsum(sg, e4, w)
        u = recip(gp, sg, u)
        IW = cst("idxw")

        def first_max(x, mx, n, *toks):
            key, oh, km = ar(2 * n).rearrange("p (a j) -> p a j", a=2), ar(2 * n).rearrange("p (a j) -> p a j", a=2), ar(2).unsqueeze(2)
            u = tt(key, x, mx.broadcast_to([128, 2, n]), ALU.is_equal, *toks)
            u = tt(key, key, IW[:, 0:n].unsqueeze(1).broadcast_to([128, 2, n]), ALU.mult, u)
            u = rmax(km, key, u)
            u = tt(oh, key, km.broadcast_to([128, 2, n]), ALU.is_equal, u)
            return oh, u

        ohg, ug = first_max(L4, mg, 4, v1)
        b = bank()
        t = mm(b[:, 0:4], TRI, ohg[:, 0, :], True, True, ug, t_tri, inc=True)
        mm(b[:, 8:12], ones, ohg[:, 0, :], True, False)
        t = mm(b[:, 8:12], TRI, ohg[:, 1, :], False, True, inc=True)
        mm(b[:, 16:20], ones, ohg[:, 0, :], True, False)
        t = mm(b[:, 16:20], ones, ohg[:, 1, :], False, True, inc=True)
        RANK = ar(16).rearrange("p (a g) -> p a g", a=2)
        vr = vcopy(RANK, b[:, 0:16].rearrange("p (a g) -> p a g", a=2), t)
        MX, FLAG = ar(1), ar(1).bitcast(i32)
        vf = rmax(MX, b[:, 16:20], t)
        b.free = [vr, vf]
        t_flag = ts(FLAG, MX, CAP + 0.5, None, ALU.is_gt, None, vf)
        sel = ar(64).rearrange("p (a g j) -> p a g j", a=2, g=4)
        ug2 = None
        for a in range(2):
            ug2 = tt(sel[:, a], L32[:, a], ohg[:, a, :].unsqueeze(2).broadcast_to([128, 4, 8]), ALU.mult, ug)
        le = ar(16).rearrange("p (a j) -> p a j", a=2)
        for a in range(2):
            u = rsum(le[:, a, :].unsqueeze(2), sel[:, a].rearrange("p g j -> p j g"), ug2)
        m1, m2 = ar(2).unsqueeze(2), ar(2).unsqueeze(2)
        u1 = rmax(m1, le, u)
        oh1, u = first_max(le, m1, 8, u1)
        le2 = ar(16).rearrange("p (a j) -> p a j", a=2)
        u = stt(le2, oh1, -3e38, le, ALU.mult, ALU.add, u)
        u2 = rmax(m2, le2, u)
        oh2, u = first_max(le2, m2, 8, u2)
        ex, w1, w2, sd = ar(2).unsqueeze(2), ar(2).unsqueeze(2), ar(2).unsqueeze(2), ar(2).unsqueeze(2)
        u = tt(ex, m2, m1, ALU.subtract, u)
        w = act(ex, ex, ACT.Exp, u)
        u = ts(sd, ex, 1.0, None, ALU.add, None, w)
        u = recip(sd, sd, u)
        u = tt(w1, sd, gp, ALU.mult, u)
        u = tt(w2, w1, ex, ALU.mult, u)
        u = tt(oh1, oh1, w1.broadcast_to([128, 2, 8]), ALU.mult, u)
        u = tt(oh2, oh2, w2.broadcast_to([128, 2, 8]), ALU.mult, u)
        u = tt(oh1, oh1, oh2, ALU.add, u)
        G32 = ar(64).rearrange("p (a g j) -> p a g j", a=2, g=4)
        for a in range(2):
            ug = tt(G32[:, a], ohg[:, a, :].unsqueeze(2).broadcast_to([128, 4, 8]), oh1[:, a, :].unsqueeze(1).broadcast_to([128, 4, 8]),
                    ALU.mult, u)
        def fork(fast, general, flag, t_flag):
            lanes = [PE, DV, AC, SY]
            for L in lanes:
                L.wait(t_flag)
            lists = lambda: [x[:] for x in (sfree, sqfree, rsfree, tnfree)]
            keep = ([(L.q, L.n, dict(L.seen)) for L in lanes], dict(st), dict(released), dict(loaded), dict(parts), lists(),
                    [b.free for b in BK], dict(rot), sqn[0], arena_at[0], [d.n for d in RD])
            bodies, counts, dmas = [], [], []
            for body in (fast, general):
                for L, (q, n, seen) in zip(lanes, keep[0]):
                    L.q, L.n, L.seen = [], n, dict(seen)
                st.update(keep[1])
                for d, k in zip((released, loaded, parts), keep[2:5]):
                    d.clear()
                    d.update(k)
                for x, k in zip((sfree, sqfree, rsfree, tnfree), keep[5]):
                    x[:] = k
                for b, f in zip(BK, keep[6]):
                    b.free = f
                rot.update(keep[7])
                sqn[0], arena_at[0] = keep[8], keep[9]
                for d, n in zip(RD, keep[10]):
                    d.n = n
                body()
                bodies.append([L.q for L in lanes])
                counts.append([L.n for L in lanes])
                dmas.append(([d.n for d in RD], dict(st)))
            assert dmas[0] == dmas[1]
            for x, L in enumerate(lanes):
                top = max(c[x] for c in counts) + 1
                if L is not SY:
                    for c, bd in zip(counts, bodies):
                        bd[x].append(lambda e, L=L, n=c[x]: e.wait_ge(L.sem, n))
                        bd[x].append(lambda e, L=L, d=top - c[x]: e.sem_inc(L.sem, d))
                    L.n = top
                L.q, L.seen = keep[0][x][0], keep[0][x][2]
                L.q.append((flag, bodies[0][x], bodies[1][x]))
            for L in lanes:
                L.wait(everyone())
            return PE.last()

        def swiglu(n, ht, H, L, gated, scale, SB, TB, t_gt=None):
            rotate(BK[0:3])
            ahl = [None, None]
            pend = None
            sfr, tfr, afr = [[], []], [[], []], [[PE.last()], [PE.last()]]

            def down(i, toks):
                h, l, wt = blocks(get(), 2)
                y = 4 * (i % 2)
                res = []
                for nb in range(8):
                    bb = YB[nb // 2]
                    if i == 0 and nb % 2 == 0:
                        PE.wait(bb.free)
                    for k in range(2):
                        t = mm3(bb[:, (nb % 2) * 256:(nb % 2) * 256 + 256], h[:, k, nb * 128:nb * 128 + 128],
                                l[:, k, nb * 128:nb * 128 + 128], YH[:, y + k, :], YL[:, y + k, :],
                                i == 0 and nb % 2 == 0 and k == 0, i == n - 1 and k == 1, wt, toks, inc=(k == 1))
                    res.append(t)
                done(t)
                afr[i % 2] = [t]
                return res

            for i in range(n):
                (bg,), tg = lin_fm(H, L, ht)
                if gated:
                    PE.wait(AUX.free)
                    ta = mm(AUX[:, 0:256], ident[0:32, i:i + 1].broadcast_to([32, 128]), GT[0:32, :], True, True, t_gt, inc=True)
                (bu,), tu = lin_fm(H, L, ht)
                S, T = SB[i % 2], TB[i % 2]
                u = act(S, bg.two(), ACT.Silu, tg, sfr[i % 2])
                bg.free = [u]
                if gated:
                    u = tt(S, S, AUX[:, 0:256].unsqueeze(1).broadcast_to([128, 2, 256]), ALU.mult, u, ta)
                    AUX.free = [u]
                u = tt(T, S, bu.two(), ALU.mult, u, tu, tfr[i % 2])
                bu.free = [u]
                sfr[i % 2] = [u]
                y = 4 * (i % 2)
                toks = split_into(YH[:, y:y + 2, :], YL[:, y:y + 2, :], T, u, afr[i % 2])
                tfr[i % 2] = toks
                if pend is not None:
                    down(*pend)
                pend = (i, toks)
            res = down(*pend)
            PE.wait(AUX.free)
            for i in range(4):
                u = add_out(YB[i], i, res[2 * i + 1], scale)
                s = stats(AUX, i, u)
            return s

        SB, TB = [ar(512, 2), ar(512, 2)], [ar(512, 2), ar(512, 2)]
        GT = ar(256)

        def dense():
            b = bank()
            for a in range(2):
                t = transpose(b[0:32, a * 128:a * 128 + 128], G32[:, a].rearrange("p g j -> p (g j)"), ident, ug)
            t_gt = act(GT[0:32, :], b[0:32, 0:256], ACT.Copy, t)
            b.free = [t_gt]
            swiglu(32, ht, H0, L0, True, G3, SB, TB, t_gt)

        def grouped():
            rotate(BK[0:3])
            PG = YHt[:, 1024:2048].rearrange("p (g a s) -> p g a s", g=4, a=2)
            PT = YLt[:, 1024:2048].rearrange("p (g t) -> p g t", g=4)
            YGH, YGL = YHt[:, 2048:3072], YLt[:, 2048:3072]
            fr = [PE.last()]
            for g in range(4):
                for a in range(2):
                    tp = ts(PG[:, g, a, :], IOTA, RANK[:, a, g:g + 1], ohg[:, a, g:g + 1], ALU.is_equal, ALU.mult,
                            vr, t_tri, fr)
            gx = [[], []]
            gfree = [[], []]

            def gather(g):
                toks = []
                for src, dst in ((TH, HHt), (TL, HLt)):
                    for kq in range(2):
                        b = bank()
                        for k in range(4):
                            c = slice((4 * kq + k) * 128, (4 * kq + k) * 128 + 128)
                            o = b[:, k * 128:k * 128 + 128]
                            mm(o, src[:, 0, c], PG[:, g, 0, :], True, False, tp, t_tm)
                            t = mm(o, src[:, 1, c], PG[:, g, 1, :], False, True, inc=True)
                        w = act(dst[:, 1024 * (g % 2) + 512 * kq:1024 * (g % 2) + 512 * kq + 512], b[:, :], ACT.Copy, t,
                                gfree[g % 2], fr)
                        b.free = [w]
                        toks.append(w)
                gx[g % 2] = [toks] * 8

            gather(0)
            GC = ar(32).rearrange("p (g j) -> p g j", g=4)
            b = bank()
            for g in range(4):
                for a in range(2):
                    t = mm(b[:, 8 * g:8 * g + 8], PG[:, g, a, :].bitcast(f32), G32[:, a, g, :], a == 0, a == 1, ug, tp,
                           inc=(a == 1))
            t_gc = vcopy(GC, b[:, 0:32].rearrange("p (g j) -> p g j", g=4), t)
            b.free = [t_gc]
            for gq in range(2):
                b = bank()
                for g in (2 * gq, 2 * gq + 1):
                    for a in range(2):
                        t = transpose(b[:, (g % 2) * 256 + a * 128:(g % 2) * 256 + a * 128 + 128],
                                      PG[:, g, a, :].bitcast(f32), ident, tp)
                t_pt = act(PT[:, 2 * gq:2 * gq + 2, :], b.two(), ACT.Copy, t, fr)
                b.free = [t_pt]
            sfr, tfr, afr = [[], []], [[], []], [[], []]
            sc = {"y": fr, "x": None}

            def down(i, toks):
                h, l, wt = blocks(get(), 2)
                g, y = i // 8, 256 * (i % 2)
                ah = YHt[:, y:y + 256].rearrange("p (k s) -> p k s", k=2)
                al = YLt[:, y:y + 256].rearrange("p (k s) -> p k s", k=2)
                res = []
                for q in range(2):
                    b = YB[2 * (g % 2) + q]
                    if i % 8 == 0:
                        PE.wait(b.free)
                    for k in range(2):
                        t = mm3(b[:, :], ah[:, k, :], al[:, k, :], h[:, k, q * 512:q * 512 + 512], l[:, k, q * 512:q * 512 + 512],
                                i % 8 == 0 and k == 0, i % 8 == 7 and k == 1, wt, toks, inc=(k == 1))
                    res.append(t)
                done(t)
                afr[i % 2] = [t]
                return res

            def lin_slots(X, XL, toks):
                h, l, wt = blocks(get(), 8)
                b = bank()
                for k in range(8):
                    t = mm3(b[:, 0:256], X[:, k, :], XL[:, k, :], h[:, k, :], l[:, k, :], k == 0, k == 7, wt, toks[k],
                            inc=(k == 7))
                done(t)
                return b, t

            def scatter(g, res, last):
                for q in range(2):
                    b = YB[2 * (g % 2) + q]
                    c = slice(512 * q, 512 * q + 512)
                    th = act(YGH[:, c], b[:, :], ACT.Copy, res[q], sc["y"])
                    tl = tt(YGL[:, c], b[:, :], YGH[:, c].bitcast(f32), ALU.subtract, th, sc["y"])
                    b.free = [tl]
                for i in range(4):
                    b = bank()
                    for r in range(2):
                        k = 2 * i + r
                        o = b[:, r * 256:r * 256 + 256]
                        mm(o, YGH[:, k * 128:k * 128 + 128], PT[:, g, :], True, False, th, tl, t_pt)
                        t = mm(o, YGL[:, k * 128:k * 128 + 128], PT[:, g, :], False, True, inc=True)
                    u = add_out(b, i, [t, sc["x"]], G3)
                    if last:
                        stats(AUX, i, u)
                sc["x"] = u
                sc["y"] = [t]

            pend = None
            for i in range(32):
                g = i // 8
                X, XL = (T[:, 1024 * (g % 2):1024 * (g % 2) + 1024].rearrange("p (k s) -> p k s", k=8) for T in (HHt, HLt))
                bg, tg = lin_slots(X, XL, gx[g % 2])
                bu, tu = lin_slots(X, XL, gx[g % 2])
                if i % 8 == 7:
                    gfree[g % 2] = [tu]
                S, T = (v[i % 2].rearrange("p k t -> p (k t)")[:, 0:256] for v in (SB, TB))
                u = act(S, bg[:, 0:256], ACT.Silu, tg, sfr[i % 2])
                bg.free = [u]
                u = stt(T, S, GC[:, g, i % 8:i % 8 + 1], bu[:, 0:256], ALU.mult, ALU.mult, u, tu, tfr[i % 2], t_gc)
                bu.free = [u]
                sfr[i % 2] = [u]
                if pend is not None:
                    res = down(*pend)
                    if i % 8 == 0:
                        scatter(g - 1, res, False)
                PE.wait(AUX.free)
                for k in range(2):
                    t = transpose(AUX[:, k * 128:k * 128 + 128], T[:, k * 128:k * 128 + 128], ident, u)
                tfr[i % 2] = [t]
                y = 256 * (i % 2)
                toks = split_into(YHt[:, y:y + 256], YLt[:, y:y + 256], AUX[:, 0:256], t, afr[i % 2])
                AUX.free = toks
                pend = (i, toks)
                if i % 8 == 5 and g < 3:
                    gather(g + 1)
            res = down(*pend)
            PE.wait(AUX.free)
            scatter(3, res, True)

        s = fork(grouped, dense, FLAG, t_flag)
        t = rstd(AUX, s, 1.0 / 1024, EPSA)
        for k in range(8):
            u = stt(XT[:, k, :], XT[:, k, :], par("final1")[:, k:k + 1], RS[:, :], ALU.mult, ALU.mult, t, AC.last())
            if k % 2:
                s = stats(AUX, k // 2, u) if k > 1 else (PE.wait(AUX.free), stats(AUX, 0, u))[1]
        rsfree[0] = [u]
        norm.src = XT
        ht = norm(AUX, s, par("ffn1n"), None, H0, L0, PE.last())
        s = swiglu(11, ht, H0, L0, False, 0.5, SB, TB)
        ht = norm(AUX, s, par("mixn"), None, H0, L0, PE.last())

        ph = everyone()
        DV.wait(ph)
        AC.wait(ph)
        arena_at[0] = 0
        rotate(BK)
        COS, SIN = ar(512, 2), ar(512, 2)
        DECM = ar(1536).rearrange("p (h c) -> p h c", h=4)
        d_q = Dma("d_q")
        t_dec = d_q.go(SY, DECM.rearrange("p h c -> p (h c)"), D["cst"][:, co["dec"][0]:co["dec"][1]], ph)
        mark = arena_at[0]
        POSI = ar(256).bitcast(i32)
        d_pos = Dma("d_pos")
        t_pos = d_pos.go(SY, POSI, D["pos"].broadcast_to([128, 256]), ph)
        ANG, KK, RR = ar(512, 2), ar(512, 2), ar(512, 2)
        PF = ar(256)
        u = vcopy(PF, POSI, t_pos)
        for i in range(2):
            u = ts(ANG[:, i, :], PF, cst("inv")[:, i:i + 1], None, ALU.mult, None, u)
        MAGIC = 12582912.0
        C1, C2 = 6.28125, float(np.float32(0.0019340515136718750))
        C3 = float(2 * np.pi - 6.28125 - np.float64(C2))
        u = ts(KK, ANG, float(1 / (2 * np.pi)), MAGIC, ALU.mult, ALU.add, u)
        u = ts(KK, KK, -MAGIC, None, ALU.add, None, u)
        u = stt(RR, KK, -C1, ANG, ALU.mult, ALU.add, u)
        u = stt(RR, KK, -C2, RR, ALU.mult, ALU.add, u)
        u = stt(RR, KK, -C3, RR, ALU.mult, ALU.add, u)
        PI = 3.1415925
        v = ts(ANG, RR, PI, -PI, ALU.min, ALU.max, u)
        w = act(SIN, ANG, ACT.Sin, v)
        u = ts(RR, RR, float(np.pi / 2), None, ALU.add, None, v)
        u = ts(KK, RR, float(np.pi), float(-2 * np.pi), ALU.is_gt, ALU.mult, u)
        u = tt(RR, RR, KK, ALU.add, u)
        u = ts(RR, RR, PI, -PI, ALU.min, ALU.max, u)
        t_rope = [act(COS, RR, ACT.Sin, u), w]
        AC.wait(t_rope)
        DV.wait(t_rope)
        arena_at[0] = mark
        TR = [ar(512, 2), ar(512, 2)]
        TA = ar(512, 2)
        trf = [[], []]
        trn = [0]

        def rope(b, n, t, kind, dst):
            i = trn[0] % 2
            trn[0] += 1
            T = TR[i][:, 0:n, :]
            w = act(T, b.two()[:, 0:n, :], ACT.Copy, t, trf[i])
            b.free = [w]
            b2 = bank()
            t = mm(b2[:, 0:n * 256], cst("rr" if kind else "ra"), T.rearrange("p k t -> p (k t)"), True, True, w, inc=True)
            c = COS[:, kind, :].unsqueeze(1).broadcast_to([128, n, 256])
            s = SIN[:, kind, :].unsqueeze(1).broadcast_to([128, n, 256])
            A = TA[:, 0:n, :]
            u = tt(A, T, c, ALU.mult, w, DV.last())
            u2 = tt(T, b2.two()[:, 0:n, :], s, ALU.mult, t, u)
            b2.free = [u2]
            u = tt(dst, A, T, ALU.add, u, u2)
            trf[i] = [u]
            return u

        IK, IWT = ar(256), small(16).rearrange("p (a h) -> p a h", a=2)
        yn_at = arena_at[0]
        IQ, SCO, WK = ar(1024, 4), ar(512, 2), ar(512, 2)
        MB = ar(512, 2)
        free_at = arena_at[0]
        h, l, wt = blocks(get(), 8)
        b = bank()
        b2 = bank()
        for k in range(8):
            t = mm3(b[:, 0:256], h[:, k, 0:128], l[:, k, 0:128], H0[:, k, :], L0[:, k, :], k == 0, k == 7, wt, ht[k], inc=(k == 7))
        for a in range(2):
            for k in range(8):
                xs = slice(a * 128, a * 128 + 128)
                t2 = mm3(b2[:, a * 8:a * 8 + 8], H0[:, k, xs], L0[:, k, xs], h[:, k, 128:136], l[:, k, 128:136],
                         k == 0, k == 7, inc=(k == 7))
        done(t2)
        w_iw = ts(IWT, b2[:, 0:16].rearrange("p (a h) -> p a h", a=2), float(np.float32(8 ** -0.5)), 0.125, ALU.mult, ALU.mult, t2)
        b2.free = [w_iw]
        t_ik = rope(b, 1, t, 0, IK.unsqueeze(1))
        for i in range(2):
            (b,), t = lin_fm(H0, L0, ht)
            t_iq = rope(b, 2, t, 0, IQ[:, 2 * i:2 * i + 2, :])
        RL = [ar(512, 2), ar(512, 2)]
        rlf = [[], []]
        M8 = small(16).rearrange("p (a h) -> p a h", a=2)

        def indexer():
            n = 0
            ut = None
            for a in range(2):
                for hp in range(4):
                    b = bank()
                    for r in range(2):
                        p = slice(64 * r, 64 * r + 64)
                        t = mm(b[:, r * 256:r * 256 + 256], IQ[p, hp, a * 128:a * 128 + 128], IK[p, :], True, True,
                               t_ik, t_iq, PE.last(), inc=True)
                    R = RL[n % 2]
                    w = act(R, b.two(), ACT.Relu, t, rlf[n % 2])
                    b.free = [w]
                    for r in range(2):
                        hh = 2 * hp + r
                        if hh == 0:
                            ut = ts(SCO[:, a, :], R[:, r, :], IWT[:, a, hh:hh + 1], None, ALU.mult, None, w)
                        else:
                            ut = stt(SCO[:, a, :], R[:, r, :], IWT[:, a, hh:hh + 1], SCO[:, a, :], ALU.mult, ALU.add, w, ut)
                    rlf[n % 2] = [ut]
                    n += 1
                yield
            for p0, p1, a, c in ((0, 64, 0, 64), (64, 128, 0, 128), (0, 64, 1, 192)):
                v = DV.run(lambda e, p0=p0, p1=p1, a=a, c=c: e.memset(SCO[p0:p1, a, c:256], -1e30), ut)
            src = [SCO[:, 0, :], SCO[:, 1, :]]
            prev = [v, v]
            for r in range(8):
                for a in range(2):
                    u = DV.run(lambda e, a=a, s=src[a]: e.max(M8[:, a, :], s), prev[a])
                    prev[a] = DV.run(lambda e, a=a, s=src[a]: e.match_replace(WK[:, a, :], M8[:, a, :], s, -3e38), u)
                    src[a] = WK[:, a, :]
                if r % 2:
                    yield
            u = ts(MB, WK, -3e38, -1e30, ALU.is_gt, ALU.mult, prev)
            indexer.tok = u
            yield

        RQ, RK, RV = ar(1024, 4), ar(1024, 4), ar(2048).rearrange("p (a c) -> p a c", a=2)
        gen = indexer()
        next(gen, None)
        for dst in (RQ, RK):
            for i in range(2):
                (b,), t = lin_fm(H0, L0, ht)
                t_r = rope(b, 2, t, 1, dst[:, 2 * i:2 * i + 2, :])
                next(gen, None)
        for i in range(4):
            (b, t), = lin_tm(2, H=H0, L=L0, toks=ht)
            t_rv = act(RV[:, :, i * 256:i * 256 + 256], b.two(), ACT.Copy, t)
            b.free = [t_rv]
            next(gen, None)
        for _ in gen:
            pass
        YN = ARt[:, yn_at:yn_at + 2048].rearrange("p (k t) -> p k t", k=8)
        AC.wait(indexer.tok, PE.last())
        SR = TR
        srf = [[], []]
        for h4 in range(4):
            b = bank()
            mm(b[:, 0:256], RK[:, h4, 0:128], RQ[:, h4, :], True, True, t_r)
            t = mm(b[:, 256:384], RK[:, h4, 128:256], RQ[:, h4, 128:256], True, True, inc=True)
            S = SR[h4 % 2].rearrange("p k t -> p (k t)")
            u = tt(S[:, 0:384], b[:, 0:384], DECM[:, h4, :], ALU.mult, t, t_dec, srf[h4 % 2], DV.last())
            b.free = [u]
            b = bank()
            for e in range(2):
                c = slice(h4 * 256 + e * 128, h4 * 256 + e * 128 + 128)
                mm(b[:, e * 256:e * 256 + 256], RV[:, 0, c], S[:, 0:256], e == 0, False, u, t_rv)
                t = mm(b[:, e * 256 + 128:e * 256 + 256], RV[:, 1, c], S[:, 256:384], False, True, inc=True)
            srf[h4 % 2] = [t]
            Y2 = YN[:, 2 * h4:2 * h4 + 2, :]
            w = act(Y2, b.two(), ACT.Copy, t)
            b.free = [w]
            b = bank()
            for e in range(2):
                t = mm(b[:, 0:256], ones, Y2[:, e, :], e == 0, e == 1, w, inc=(e == 1))
            u = stt(Y2, b[:, 0:256].unsqueeze(1).broadcast_to([128, 2, 256]), -1.0 / 256, Y2, ALU.mult, ALU.add, t)
            b.free = [u]
            b = bank()
            for e in range(2):
                i = sqn[0] % 2
                sqn[0] += 1
                w = act(SQ[i][:, :], Y2[:, e, :], ACT.Square, u, sqfree[i])
                t = mm(b[:, 0:256], ones, SQ[i][:, :], e == 0, e == 1, w, inc=True)
                sqfree[i] = [t]
            v = rstd(b, t, 1.0 / 256, EPSG)
            for e in range(2):
                k = 2 * h4 + e
                u = stt(YN[:, k, :], YN[:, k, :], par("retgn")[:, k:k + 1], RS[:, :], ALU.mult, ALU.mult, v)
            rsfree[0] = [u]
        t_yn = u
        ph = everyone()
        DV.wait(ph)
        AC.wait(ph)
        arena_at[0] = free_at
        AQ = ar(1024, 4)
        AK, AV = ar(256), ar(256).rearrange("p (a c) -> p a c", a=2)
        P2 = [ar(512, 2), ar(512, 2)]
        PT = ar(1024).rearrange("p (h s q) -> p h s q", h=2, s=2)
        NM, SS = small(4), small(4)
        for i in range(2):
            (b,), t = lin_fm(H0, L0, ht)
            t_aq = rope(b, 2, t, 0, AQ[:, 2 * i:2 * i + 2, :])
        h, l, wt = blocks(get(), 8)
        b = bank()
        b2 = bank()
        for k in range(8):
            t = mm3(b[:, 0:256], h[:, k, 0:128], l[:, k, 0:128], H0[:, k, :], L0[:, k, :], k == 0, k == 7, wt, inc=(k == 7))
        for a in range(2):
            for k in range(8):
                xs = slice(a * 128, a * 128 + 128)
                t2 = mm3(b2[:, a * 64:a * 64 + 64], H0[:, k, xs], L0[:, k, xs], h[:, k, 128:192], l[:, k, 128:192],
                         k == 0, k == 7, inc=(k == 7))
        done(t2)
        v2 = b2[:, 0:128].rearrange("p (a c) -> p a c", a=2)
        act(AV[:, :, 0:64], v2, ACT.Copy, t2)
        t_av = act(AV[:, :, 64:128], v2, ACT.Copy, t2)
        b2.free = [t_av]
        t_ak = rope(b, 1, t, 0, AK.unsqueeze(1))

        def attention():
            pf = [[], []]
            ptf = []
            n = 0
            for hp in range(4):
                for a in range(2):
                    b = bank()
                    for r in range(2):
                        p = slice(64 * r, 64 * r + 64)
                        t = mm(b[:, r * 256:r * 256 + 256], AQ[p, hp, a * 128:a * 128 + 128], AK[p, :], True, True,
                               t_aq, t_ak, PE.last(), inc=True)
                    P = P2[n % 2]
                    u = stt(P, b.two(), 0.125, MB[:, a, :].unsqueeze(1).broadcast_to([128, 2, 256]), ALU.mult, ALU.add,
                            t, indexer.tok, pf[n % 2])
                    b.free = [u]
                    u = DV.run(lambda e, P=P: e.tensor_reduce(NM[:, 0:2].unsqueeze(2), P, AX.X, ALU.max), u, AC.last())
                    u = ts(NM[:, 2:4], NM[:, 0:2], -1.0, None, ALU.mult, None, u)
                    for r in range(2):
                        w = act(P[:, r, :], P[:, r, :], ACT.Exp, u, DV.last(), bias=NM[:, 2 + r:3 + r], accum_out=SS[:, r:r + 1])
                    u = recip(SS[:, 2:4], SS[:, 0:2], w)
                    for r in range(2):
                        u2 = ts(P[:, r, :], P[:, r, :], SS[:, 2 + r:3 + r], None, ALU.mult, None, u)
                    b = bank()
                    for r in range(2):
                        for s in range(2):
                            t = transpose(b[:, (r * 2 + s) * 128:(r * 2 + s) * 128 + 128], P[:, r, s * 128:s * 128 + 128],
                                          ident, u2)
                    pf[n % 2] = [t]
                    w = act(PT[:, :, :, a * 128:a * 128 + 128], b[:, :].rearrange("p (h s q) -> p h s q", h=2, s=2),
                            ACT.Copy, t, ptf)
                    b.free = [w]
                    n += 1
                    if a == 0:
                        yield
                b = bank()
                for r in range(2):
                    for s in range(2):
                        t = mm(b[:, r * 256:r * 256 + 256], AV[:, s, :], PT[:, r, s, :], s == 0, s == 1, w, t_av, inc=(s == 1))
                ptf = [t]
                for r in range(2):
                    p = slice(64 * r, 64 * r + 64)
                    th = act(YH[p, hp, :], b[p, r * 256:r * 256 + 256], ACT.Copy, t)
                    tl = tt(YL[p, hp, :], b[p, r * 256:r * 256 + 256], YH[p, hp, :].bitcast(f32), ALU.subtract, th)
                    AC.wait(tl)
                b.free = [tl, th]
                ytoks[hp] = [tl, th]
                yield

        gen = attention()
        SG = TR
        sgf = [[], []]
        for h4 in range(4):
            (b,), t = lin_fm(H0, L0, ht)
            S = SG[h4 % 2]
            w = act(S, b.two(), ACT.Silu, t, sgf[h4 % 2], DV.last())
            b.free = [w]
            Y2 = YN[:, 2 * h4:2 * h4 + 2, :]
            u = tt(Y2, Y2, S, ALU.mult, w, t_yn)
            sgf[h4 % 2] = [u]
            y = split_into(YH[:, 4 + 2 * h4:6 + 2 * h4, :], YL[:, 4 + 2 * h4:6 + 2 * h4, :], Y2, u)
            ytoks[4 + 2 * h4] = ytoks[5 + 2 * h4] = y
            next(gen, None)
            next(gen, None)
        for _ in gen:
            pass
        H1, L1 = half(HHt, 1), half(HLt, 1)
        mtoks = [None] * 8
        S1, S2 = TR
        free1 = DV.last()
        for j in range(4):
            (b,), t = lin_fm(H0, L0, ht)
            w1_ = act(S1, b.two(), ACT.Sigmoid, t, DV.last(), AC.last())
            b.free = [w1_]
            (b,), t = lin_fm(YH[:, 0:4, :], YL[:, 0:4, :], ytoks[0:4], nk=4)
            u = tt(S1, S1, b.two(), ALU.mult, w1_, t)
            b.free = [u]
            (b,), t = lin_fm(H0, L0, ht)
            w2_ = act(S2, b.two(), ACT.Sigmoid, t, DV.last(), AC.last())
            b.free = [w2_]
            (b,), t = lin_fm(YH[:, 4:12, :], YL[:, 4:12, :], ytoks[4:12])
            u2 = tt(S2, S2, b.two(), ALU.mult, w2_, t)
            b.free = [u2]
            u = tt(TA, S1, S2, ALU.add, u, u2, AC.last())
            y = split_into(H1[:, 2 * j:2 * j + 2, :], L1[:, 2 * j:2 * j + 2, :], TA, u)
            mtoks[2 * j] = mtoks[2 * j + 1] = y
        s = project(H1, L1, mtoks, 1.0, BK[0:3] + BK[4:8])
        ht = norm(AUX, s, par("ffn2n"), None, H0, L0, PE.last())
        ph = everyone()
        DV.wait(ph)
        AC.wait(ph)
        arena_at[0] = 0
        SB, TB = [ar(512, 2), ar(512, 2)], [ar(512, 2), ar(512, 2)]
        PL = ar(512, 2)
        d_l = Dma("d_l")
        t_pl = d_l.go(SY, PL.rearrange("p k t -> p (k t)"), D["ple"], ph)
        s = swiglu(11, ht, H0, L0, False, 0.5, SB, TB)
        PH, PLO = half(HHt, 1)[:, 0:2, :], half(HLt, 1)[:, 0:2, :]
        t_ph = split_into(PH, PLO, PL, t_pl, PE.last())
        ht = norm(AUX, s, par("plen"), None, H0, L0, PE.last())
        rotate(BK[0:3] + BK[4:8])
        PE.wait(AUX.free)
        S1, S2 = SB
        for j in range(4):
            (b,), t = lin_fm(H0, L0, ht)
            w = act(S1, b.two(), ACT.Sigmoid, t, DV.last())
            b.free = [w]
            (b,), t = lin_fm(PH, PLO, [t_ph, t_ph], nk=2)
            u = tt(S2, S1, b.two(), ALU.mult, w, t)
            b.free = [u]
            xs = XT[:, 2 * j:2 * j + 2, :]
            u = tt(xs, xs, S2, ALU.add, u)
            s = stats(AUX, j, u)
        t = rstd(AUX, s, 1.0 / 1024, EPSA)
        d_o = Dma("d_out")
        for k in range(8):
            u = stt(XT[:, k, :], XT[:, k, :], par("final2")[:, k:k + 1], RS[:, :], ALU.mult, ALU.mult, t, AC.last())
            if k % 2:
                to = d_o.go(SY, out[:, (k - 1) * 256:(k + 1) * 256], XTt[:, (k - 1) * 256:(k + 1) * 256], u)
        SY.wait(to)
        assert st["g"] == len(chunks), (st["g"], len(chunks))

        block = cx.enter_context(nc.Block())

        def run_all(e, q):
            for f in q:
                if isinstance(f, tuple):
                    v = e.value_load(f[0][0:1, 0:1], min_val=0, max_val=1)
                    with e.If(v < 1):
                        run_all(e, f[1])
                    with e.Else():
                        run_all(e, f[2])
                else:
                    f(e)

        def play(lane):
            def body(e):
                run_all(e, lane.q)
            return body

        block.sync(play(SY))
        block.scalar(play(AC))
        block.vector(play(DV))
        block.tensor(play(PE))


def constants():
    f = np.float32
    parts = {}
    parts["ident"] = np.eye(128, dtype=f)
    parts["sel"] = np.zeros((128, 2), f)
    parts["sel"][0:4] = [[1, 0], [0, 1], [1, 0], [0, 1]]
    parts["ones"] = np.ones((128, 128), f)
    for name, half in (("ra", 32), ("rr", 64)):
        R = np.zeros((128, 128), f)
        for m in range(128):
            b, i = m // (2 * half) * 2 * half, m % (2 * half)
            if i < half:
                R[b + i + half, m] = -1
            else:
                R[b + i - half, m] = 1
        parts[name] = R
    inv = np.zeros((128, 2), f)
    for c, half in enumerate((32, 64)):
        t = f(10000.0) ** (-np.arange(half, dtype=f) / f(half))
        inv[:, c] = t[np.arange(128) % half]
    parts["inv"] = inv
    parts["idxw"] = np.tile(np.arange(8, 0, -1, dtype=f), (128, 1))
    sm = np.ones((128, 512), f)
    sm[:, [0, 64, 128, 192, 256]] = 0
    parts["scanm"] = sm
    j, i = np.arange(128)[:, None], np.arange(128)[None, :]
    same = j // 64 == i // 64
    parts["glam"] = np.concatenate([same & (j <= i), same & (j >= i)], 1).astype(f)

    def win(n, w):
        lo = w // 2
        hi = w - 1 - lo
        M = np.zeros((n, n))
        for t in range(n):
            s, e = max(t - lo, 0), min(t + hi + 1, n)
            M[t, s:e] = 1.0 / (e - s)
        return M

    pool = np.zeros((128, 2, 4, 256), f)
    for g, w in enumerate((2, 4, 8, 16)):
        M = np.kron(win(4, w), win(64, w)) - np.eye(256)
        pool[:, :, g, :] = M.T.reshape(2, 128, 256).transpose(1, 0, 2)
    parts["pool"] = pool.reshape(128, -1)
    dec = np.zeros((128, 4, 384))
    for h in range(4):
        lg = np.log1p(-(2.0 ** (-5.0 - h)))
        a, b = np.arange(256)[:, None], np.arange(256)[None, :]
        M = np.exp(lg * np.abs(a - b)) * (a // 64 <= b // 64) * 128 ** -0.5
        dec[:, h, 0:256] = M[0:128]
        dec[:, h, 256:384] = M[128:, 128:]
    parts["dec"] = dec.reshape(128, -1).astype(f)
    parts["tri"] = (np.arange(128)[:, None] < np.arange(128)[None, :]).astype(f)
    parts["iota"] = np.tile(np.arange(128, dtype=f), (128, 1))
    return np.ascontiguousarray(np.concatenate([parts[n] for n, _ in CON], 1))


def kernel(**I):
    import concourse.bacc as bacc
    from concourse import mybir
    from concourse.bass_utils import run_bass_kernel_spmd as run

    I = {k: np.asarray(v) for k, v in I.items()}

    def cols(w, lists):
        K = w.shape[0]
        r = w.reshape(K // 128, 128, -1)
        return np.ascontiguousarray(np.stack([r[:, :, c].transpose(1, 0, 2).reshape(128, -1) for c in lists]))

    def even(w, a, b, step=256):
        return cols(w, [np.arange(s, s + step) for s in range(a, b, step)])

    def rows(w):
        K, n = w.shape
        return np.ascontiguousarray(w.reshape(K // 256, 2, 128, n).transpose(0, 2, 1, 3).reshape(K // 256, 128, 2 * n))

    def fm(x):
        t, n = x.shape
        return np.ascontiguousarray(x.T.reshape(n // 128, 128, t).transpose(1, 0, 2).reshape(128, -1))

    col = lambda v: v.reshape(-1, 128).T
    w1 = I["w_in"][0]
    w2 = I["w_in_2"][0]
    A = {}
    A["w_ada"] = even(I["w_ada"][0], 0, 6144)
    w1a = np.zeros((1024, 128), w1.dtype)
    w1a[:, 0:32] = w1[:, 1536:1568]
    A["w1p"] = even(w1, 1568, 2080)
    A["w1a"] = even(w1a, 0, 128, 128)
    A["w1k"] = even(w1, 256, 512)
    A["w1q"] = even(w1, 0, 256)
    A["w1v"] = even(w1, 512, 1024)
    A["w1g"] = even(w1, 1024, 1536)
    A["w_out"] = even(I["w_out"][0], 0, 1024)
    A["w_r"] = even(np.concatenate([I["w_router_group"][0], I["w_router_expert"][0]], 1), 0, 36, 36)
    we = I["w_expert_in"][0]
    e4 = we.reshape(32, 8, 128, 2, 256).transpose(3, 0, 2, 1, 4).reshape(2, 32, 128, 2048)
    A["eg"], A["eu"] = np.ascontiguousarray(e4[0]), np.ascontiguousarray(e4[1])
    A["ed"] = rows(I["w_expert_out"][0].reshape(8192, 1024))
    for n in "12":
        A[f"f{n}g"] = even(I[f"ffn{n}_w_gate_2"][0], 0, 2816)
        A[f"f{n}u"] = even(I[f"ffn{n}_w_up_2"][0], 0, 2816)
        A[f"f{n}d"] = rows(I[f"ffn{n}_w_down_2"][0])
    ra = np.arange
    A["w2ik"] = cols(w2, [np.concatenate([ra(1152, 1216), ra(1152, 1216), ra(1216, 1224)])])
    A["w2iq"] = even(w2, 640, 1152)
    A["w2rq"] = even(w2, 1224, 1736)
    A["w2rk"] = even(w2, 1736, 2248)
    A["w2rv"] = even(w2, 2248, 3272)
    A["w2aq"] = even(w2, 0, 512)
    A["w2kv"] = cols(w2, [np.concatenate([ra(512, 576), ra(512, 576), ra(576, 640)])])
    A["w2rg"] = even(w2, 3272, 4296)
    A["w2ga"] = even(w2, 4296, 5320)
    A["w2gb"] = even(w2, 5320, 6344)
    A["wba"] = even(I["w_branch_a_2"][0], 0, 1024)
    A["wbb"] = even(I["w_branch_b_2"][0], 0, 1024)
    A["w_out2"] = even(I["w_out_2"][0], 0, 1024)
    A["wpg"] = even(I["w_ple_gate_2"][0], 0, 1024)
    A["wpp"] = even(I["w_ple_proj_2"][0], 0, 1024)
    A["x"] = fm(I["x"][0])
    A["ctx"] = fm(I["ctx"][0])
    A["ple"] = fm(I["p_2"][0, 0])
    A["cvec"] = fm(np.stack([I["c"][0], I["c_ctx"]]))
    A["pos"] = np.ascontiguousarray(I["positions_2"])
    A["par"] = np.ascontiguousarray(np.concatenate([
        col(I["norm1_g"]), col(I["b_ada"]), col(I["b_decay"]), col(I["gla_norm_g"]), col(I["pool_scale"]),
        col(I["norm2_g"]), col(I["final_norm_g"]), col(I["ffn1_norm_2"]), col(I["mix_norm_2"]), col(I["ret_gn_2"]),
        col(I["ffn2_norm_2"]), col(I["ple_norm_2"]), col(I["final_norm_2"])], 1))
    A["cst"] = constants()
    A["w_pool"] = np.ascontiguousarray(I["w_pool"][0].transpose(1, 0, 2).reshape(128, 512))
    wd = np.zeros((32, 2, 256), np.float32)
    wd[0:16, 0], wd[16:32, 1] = I["w_decay"][0, 0], I["w_decay"][0, 1]
    A["w_dec"] = wd.reshape(32, 512)

    nc = bacc.Bacc("TRN2", target_bir_lowering=False, num_devices=1)
    D = {n: nc.dram_tensor("in_" + n, a.shape, mybir.dt.from_np(a.dtype), kind="ExternalInput").ap() for n, a in A.items()}
    o = nc.dram_tensor("out0", (128, 2048), mybir.dt.float32, kind="ExternalOutput").ap()
    program(nc, D, o)
    r = run(nc, [{"in_" + n: a for n, a in A.items()}], core_ids=[0])
    y = r.results[0]["out0"].reshape(128, 8, 256).transpose(2, 1, 0).reshape(1, 256, 1024)
    return np.ascontiguousarray(y)
```

```python
import numpy as np

EPS = 1e-6
GN_EPS = 1e-5
PAR = ["norm1", "bada", "bdec", "glag", "pscale", "norm2", "final1", "ffn1n", "mixn", "retgn", "ffn2n", "plen", "final2"]
PARN = [8, 48, 4, 1, 4, 8, 8, 8, 8, 8, 8, 8, 8]
CON = [("ident", 128), ("sel", 2), ("ones", 128), ("ra", 128), ("rr", 128), ("inv", 2), ("idxw", 8), ("scanm", 512),
       ("glam", 256), ("pool", 2048), ("dec", 1536), ("tri", 128), ("iota", 128)]


def offsets(pairs):
    at, out = 0, {}
    for n, k in pairs:
        out[n] = (at, at + k)
        at += k
    return out, at


def program(nc, D, out):
    import concourse.bass as bass
    from concourse import mybir
    from contextlib import ExitStack

    f32, f32r, i32 = mybir.dt.float32, mybir.dt.float32r, mybir.dt.int32
    ALU, ACT, AX = mybir.AluOpType, mybir.ActivationFunctionType, mybir.AxisListType
    cx = ExitStack()

    with cx:
        def sb(name, shape, dt=f32):
            return cx.enter_context(nc.sbuf_tensor(name, shape, dt))

        def sem(name):
            return cx.enter_context(nc.semaphore(name))

        class Lane:
            def __init__(self, name):
                self.sem, self.n, self.q, self.seen = sem("s_" + name), 0, [], {}

            def wait(self, *toks):
                for t in toks:
                    if t is None:
                        continue
                    if isinstance(t, list):
                        self.wait(*t)
                        continue
                    s, v = t
                    if self.seen.get(id(s), 0) < v:
                        self.seen[id(s)] = v
                        self.q.append(lambda e, s=s, v=v: e.wait_ge(s, v))

            def run(self, fn, *toks):
                self.wait(*toks)
                self.n += 1
                self.q.append(lambda e, f=fn, s=self.sem: f(e).then_inc(s, 1))
                return (self.sem, self.n)

            def plain(self, fn, *toks):
                self.wait(*toks)
                self.q.append(fn)

            def last(self):
                return (self.sem, self.n) if self.n else None

        PE, DV, AC, GP, SY = Lane("pe"), Lane("dve"), Lane("act"), Lane("pool"), Lane("sp")

        class Dma:
            def __init__(self, name):
                self.sem, self.n = sem(name), 0

            def go(self, lane, dst, src, *toks):
                self.n += 16
                lane.plain(lambda e, s=self.sem: e.dma_start(dst, src).then_inc(s, 16), *toks)
                return (self.sem, self.n)

        def tt(o, a, b, op, *toks):
            return DV.run(lambda e: e.tensor_tensor(o, a, b, op), *toks)

        def ts(o, a, s1, s2, op0, op1, *toks):
            if op1 is None:
                return DV.run(lambda e: e.tensor_scalar(o, a, s1, None, op0), *toks)
            return DV.run(lambda e: e.tensor_scalar(o, a, s1, s2, op0, op1), *toks)

        def stt(o, a, s, b, op0, op1, *toks):
            return DV.run(lambda e: e.scalar_tensor_tensor(o, a, s, b, op0, op1), *toks)

        def vcopy(o, a, *toks):
            return DV.run(lambda e: e.tensor_copy(o, a), *toks)

        def rmax(o, a, *toks):
            return DV.run(lambda e: e.tensor_reduce(o, a, AX.X, ALU.max), *toks)

        def rsum(o, a, *toks):
            return DV.run(lambda e: e.tensor_reduce(o, a, AX.X, ALU.add), *toks)

        def recip(o, a, *toks):
            return DV.run(lambda e: e.reciprocal(o, a), *toks)

        def act(o, a, fn, *toks, **kw):
            return AC.run(lambda e: e.activation(o, a, fn, **kw), *toks)

        def mm(o, l, r, start, stop, *toks, inc=False):
            f = lambda e: e.matmul(o, l, r, start=start, stop=stop, skip_group_check=True)
            if inc:
                return PE.run(f, *toks)
            PE.plain(f, *toks)

        def mm3(o, lh, ll, rh, rl, start, stop, *toks, inc=False):
            PE.wait(*toks)
            mm(o, lh, rh, start, False)
            mm(o, lh, rl, False, False)
            return mm(o, ll, rh, False, stop, inc=inc)

        def transpose(o, a, idn, *toks):
            return PE.run(lambda e: e.transpose(o, a, idn), *toks)

        co, ncon = offsets(CON)
        po, npar = offsets(list(zip(PAR, PARN)))
        NR, NU, AHEAD = 4, 6, 4
        RAW = [sb(f"raw{i}", [128, 2048]) for i in range(NR)]
        WH = [sb(f"wh{i}", [128, 1024], f32r) for i in range(NU)]
        WL = [sb(f"wl{i}", [128, 1024], f32r) for i in range(NU)]
        XTt = sb("xt", [128, 2048])
        XT = XTt[:, :].rearrange("p (k t) -> p k t", k=8)
        HHt, HLt = sb("hh", [128, 4096], f32r), sb("hl", [128, 4096], f32r)
        YHt, YLt = sb("yh", [128, 3072], f32r), sb("yl", [128, 3072], f32r)
        wide = lambda T: T[:, :].rearrange("p (k t) -> p k t", k=8)
        half = lambda T, i: T[:, 2048 * i:2048 * i + 2048].rearrange("p (k t) -> p k t", k=8)
        YH = YHt[:, :].rearrange("p (k t) -> p k t", k=12)
        YL = YLt[:, :].rearrange("p (k t) -> p k t", k=12)
        CS = sb("csts", [128, co["scanm"][0]])
        PR = sb("par", [128, npar])
        cst = lambda n: CS[:, co[n][0]:co[n][1]]
        par = lambda n: PR[:, po[n][0]:po[n][1]]
        ident, ones = cst("ident"), cst("ones")
        SMt = sb("small", [128, 512])
        ROWt = sb("row", [4, 512])
        AR = 13312
        ARt = sb("arena", [128, AR])
        small_at, arena_at, arena_free = [0], [0], [[]]

        def small(n):
            small_at[0] += n
            assert small_at[0] <= 512
            return SMt[:, small_at[0] - n:small_at[0]]

        def ar(n, k=None):
            arena_at[0] += n
            assert arena_at[0] <= AR, arena_at[0]
            v = ARt[:, arena_at[0] - n:arena_at[0]]
            return v if k is None else v.rearrange("p (k t) -> p k t", k=k)

        def everyone():
            return [t for t in (PE.last(), DV.last(), AC.last()) if t]

        class Bank:
            def __init__(self, i):
                self.t = cx.enter_context(nc.psum_tensor(f"bank{i}", [128, 512], f32))
                self.free = []

            def __getitem__(self, k):
                return self.t[k]

            def two(self):
                return self.t[:, :].rearrange("p (k t) -> p k t", k=2)

        BK = [Bank(i) for i in range(8)]
        AUX, YB = BK[3], BK[4:8]
        rot = {"l": BK[0:3], "i": 0}

        def rotate(banks):
            rot["l"], rot["i"] = banks, 0

        def bank():
            b = rot["l"][rot["i"] % len(rot["l"])]
            rot["i"] += 1
            PE.wait(b.free)
            b.free = []
            return b

        chunks = []

        def add(name, i):
            a = D[name]
            chunks.append((a[i], a.shape[2]))

        for i in range(8):
            add("w_ada", i)
        ada = list(range(8, 24))
        FIRST = [("p", 0, 1), ("p", 1, 1), ("a", 0, 1), ("k", 0, 1), ("q", 0, 1), ("v", 0, 1), ("v", 1, 1), ("g", 0, 4), ("g", 1, 5)]
        for n, i, m in FIRST:
            add("w1" + n, i)
            for _ in range(m):
                add("w_ada", ada.pop(0))
        for i in range(4):
            add("w_out", i)
        add("w_r", 0)

        MERGE = [("w2gb", 0), ("w2gb", 1), ("wba", 0), ("wbb", 0), ("w2gb", 2), ("wba", 1), ("wbb", 1), ("w2gb", 3),
                 ("wba", 2), ("wbb", 2), ("wba", 3), ("wbb", 3)]

        def ffn_chunks(g, u, d, n):
            for i in range(n):
                add(g, i)
                add(u, i)
                if i:
                    add(d, i - 1)
            add(d, n - 1)

        ffn_chunks("eg", "eu", "ed", 32)
        ffn_chunks("f1g", "f1u", "f1d", 11)
        for n, k in [("iq", 2), ("ik", 1), ("rq", 2), ("rk", 2), ("rv", 4), ("aq", 2), ("kv", 1), ("rg", 4)]:
            for i in range(k):
                add("w2" + n, i)
        for i in range(4):
            add("w2ga", i)
        for n, j in MERGE:
            add(n, j)
        for i in range(4):
            add("w_out2", i)
        ffn_chunks("f2g", "f2u", "f2d", 11)
        for j in range(4):
            add("wpg", j)
            add("wpp", j)

        RD = [Dma(f"d_raw{i}") for i in range(NR)]
        released = {}
        sfree = [[] for _ in range(NU)]
        st = {"f": 0, "s": 0, "g": 0}
        loaded, parts = {}, {}

        def fetch():
            while st["f"] < len(chunks) and (st["f"] < NR or st["f"] - NR in released):
                i = st["f"]
                st["f"] += 1
                src, n = chunks[i]
                loaded[i] = RD[i % NR].go(SY, RAW[i % NR][:, 0:n], src, released.get(i - NR))

        def split():
            u = st["s"]
            st["s"] += 1
            i, n = u // 2, chunks[u // 2][1] // 2
            r = RAW[i % NR][:, (u % 2) * n:(u % 2) * n + n]
            s = u % NU
            h, l = WH[s][:, 0:n], WL[s][:, 0:n]
            th = act(h, r, ACT.Copy, loaded[i], sfree[s])
            tl = tt(l, r, h.bitcast(f32), ALU.subtract, th, loaded[i], sfree[s])
            parts[u] = (h, l, [th, tl])
            if u % 2:
                released[i] = [tl, th]
                fetch()

        def unit(nk):
            u = st["g"]
            st["g"] += 1
            while st["s"] <= min(u + AHEAD, 2 * len(chunks) - 1):
                split()
            h, l, toks = parts[u]
            v = lambda a: a.rearrange("p (k n) -> p k n", k=nk)
            return v(h), v(l), toks

        def done(tok):
            sfree[(st["g"] - 1) % NU] = [tok]

        def lin_fm(xh, xl, xtoks, nk=8, ncols=256, N=256):
            per = 512 // N
            nb = ncols // 128
            outs = [bank() for _ in range((nb + per - 1) // per)]
            hk = nk // 2
            for u in range(2):
                h, l, wt = unit(hk)
                for m in range(nb):
                    o = outs[m // per][:, (m % per) * N:(m % per) * N + N]
                    for k in range(hk):
                        c = u * hk + k
                        tok = mm3(o, h[:, k, m * 128:(m + 1) * 128], l[:, k, m * 128:(m + 1) * 128], xh[:, c, :], xl[:, c, :],
                                  c == 0 and m % per == 0, c == nk - 1, wt, xtoks[c], inc=(k == hk - 1))
                done(tok)
            return outs, tok

        def split_into(h, l, src, *toks):
            th = act(h, src, ACT.Copy, *toks)
            tl = tt(l, src, h.bitcast(f32), ALU.subtract, th, *toks)
            return [th, tl]

        SQ = [sb("sq0", [128, 256]), sb("sq1", [128, 256])]
        sqfree = [[], []]
        RS = sb("rstd", [128, 256])
        rsfree = [[]]
        sqn = [0]

        def stat_step(src, b, k, n, *toks):
            i = sqn[0] % 2
            sqn[0] += 1
            a = act(SQ[i][:, :], src, ACT.Square, sqfree[i], *toks)
            t = mm(b[:, 0:256], ones, SQ[i][:, :], k == 0, k == n - 1, a, inc=True)
            sqfree[i] = [t]
            return t

        def rstd(b, tok, scale, eps_ap):
            a = act(RS[:, :], b[:, 0:256], ACT.Sqrt, tok, rsfree[0], scale=scale, bias=eps_ap)
            b.free = [a]
            return recip(RS[:, :], RS[:, :], a)

        TN = [sb("tn0", [128, 256]), sb("tn1", [128, 256])]
        tnfree = [[], []]

        def norm(b, tok, gain, shift, H, L, free):
            t = rstd(b, tok, 1.0 / 1024, EPSA)
            out_t = []
            for k in range(8):
                i = k % 2
                u = stt(TN[i][:, :], norm.src[:, k, :], gain[:, k:k + 1], RS[:, :], ALU.mult, ALU.mult, t, tnfree[i])
                if shift is None:
                    th = act(H[:, k, :], TN[i][:, :], ACT.Copy, u, free)
                    tl = tt(L[:, k, :], TN[i][:, :], H[:, k, :].bitcast(f32), ALU.subtract, th, free)
                else:
                    th = act(H[:, k, :], TN[i][:, :], ACT.Identity, u, free, bias=shift[:, k:k + 1])
                    tl = stt(L[:, k, :], TN[i][:, :], shift[:, k:k + 1], H[:, k, :].bitcast(f32),
                             ALU.add, ALU.subtract, th, free)
                tnfree[i] = [tl]
                out_t.append([th, tl])
            rsfree[0] = [u]
            return out_t

        d_c, d_x, d_ct, d_p, d_a0, d_m = (Dma(n) for n in ("d_c", "d_x", "d_ct", "d_p", "d_a0", "d_m"))
        EPSA = small(1)
        EPSG = small(1)
        te = DV.run(lambda e: e.memset(EPSA, EPS))
        te = DV.run(lambda e: e.memset(EPSG, GN_EPS))
        AC.wait(te)
        cv = small(16)
        CT = ar(2048, 8)
        POOLM = ar(2048).rearrange("p (a g t) -> p a g t", a=2, g=4)
        t_cv = d_c.go(AC, cv, D["cvec"])
        t_par = d_p.go(AC, PR[:, :], D["par"])
        t_cs = d_p.go(AC, CS[:, :], D["cst"][:, 0:co["scanm"][0]])
        t_par = t_cs
        t_x = d_x.go(AC, XTt[:, :], D["x"])
        t_ct = d_ct.go(AC, CT.rearrange("p k t -> p (k t)"), D["ctx"])
        WPOOL = ar(512).rearrange("p (g d) -> p g d", g=4)
        t_pm = d_a0.go(AC, POOLM.rearrange("p a g t -> p (a g t)"), D["cst"][:, co["pool"][0]:co["pool"][1]])
        t_pm = d_a0.go(AC, WPOOL.rearrange("p g d -> p (g d)"), D["w_pool"])
        PTM = ar(1024).rearrange("p (a c) -> p a c", a=2)
        PY = ar(1024, 4)
        fetch()

        SC = small(16)
        CV4 = YHt[:, 2048:3072].rearrange("p (k c) -> p k c", k=8)
        CV3 = CV4[:, :, 0:4].rearrange("p k (s c) -> p k s c", s=2)
        AC.wait(DV.run(lambda e: e.memset(YHt[:, 2048:3072].bitcast(f32), 0.0)))
        ROW = [ROWt[:, 0:256], ROWt[:, 256:512]]
        rowfree = [[], []]
        t_sc = act(SC, cv, ACT.Silu, t_cv)
        SC3 = SC.rearrange("p (k c) -> p k c", k=8)
        t_sc = split_into(CV3[:, :, 0, :], CV3[:, :, 1, :], SC3, t_sc)
        MOD = small(96)
        MOD3 = MOD.rearrange("p (n c) -> p n c", c=2)

        ada_pend = []

        def ada_turn():
            if ada_pend:
                c, w = ada_pend.pop()
                for m in range(2):
                    n = 2 * c + m
                    t = mm(AUX[:, 2 * n:2 * n + 2], ROW[c % 2][:, m * 128:(m + 1) * 128], cst("sel")[0:4, :], True, True,
                           w, inc=True)
                rowfree[c % 2] = [t]
                ada_turn.tok = t

        def ada_chunk(c):
            b = bank()
            for u in range(2):
                h, l, wt = unit(4)
                for k in range(4):
                    x = CV4[:, 4 * u + k, :]
                    mm(b[:, 0:256], x, h[:, k, :], u + k == 0, False, wt[0], t_sc)
                    tok = mm(b[:, 0:256], x, l[:, k, :], False, u == 1 and k == 3, wt[1], inc=(k == 3))
                done(tok)
            ada_turn()
            w = act(ROW[c % 2], b[0:4, 0:256], ACT.Copy, tok, rowfree[c % 2])
            b.free = [w]
            ada_pend.append((c, w))

        def mod_rows(a, z, tok):
            v = AUX[:, 2 * a:2 * z].rearrange("p (n c) -> p n c", c=2)
            t = tt(MOD3[:, a:z, :], v, BA[:, a:z, :].broadcast_to([128, z - a, 2]), ALU.add, tok, t_par)
            AUX.free = [t]
            return t

        bx, bc = BK[4], BK[5]
        for k in range(8):
            tsx = stat_step(XT[:, k, :], bx, k, 8, t_x, t_cs)
        for k in range(8):
            tsc = stat_step(CT[:, k, :], bc, k, 8, t_ct)
        for c in range(8):
            ada_chunk(c)
        ada_turn()
        tm = ada_turn.tok
        BA = par("bada").unsqueeze(2)
        t1 = mod_rows(0, 16, tm)
        A1, B1 = small(16).rearrange("p (c k) -> p c k", c=2), small(16).rearrange("p (c k) -> p c k", c=2)
        for c in range(2):
            t2 = stt(A1[:, c, :], MOD3[:, 8:16, c], 1.0, par("norm1"), ALU.add, ALU.mult, t1)
            t3 = vcopy(B1[:, c, :], MOD3[:, 0:8, c], t1)
        DV.wait(t2, t3)
        AC.wait(t3)
        HW, LW = wide(HHt), wide(HLt)
        norm.src = XT
        hx = norm(bx, tsx, A1[:, 0, :], B1[:, 0, :], HW[:, :, 0:256], LW[:, :, 0:256], [])
        norm.src = CT
        hc = norm(bc, tsc, A1[:, 1, :], B1[:, 1, :], HW[:, :, 256:512], LW[:, :, 256:512], [])
        hb = [hx[k] + hc[k] for k in range(8)]
        HX, LX = HW[:, :, 0:256], LW[:, :, 0:256]

        rotate(BK[0:3] + BK[4:8])
        adan = [8]
        gens = []

        def tick(n=1):
            for _ in range(n):
                while gens:
                    if next(gens[0], "end") == "end":
                        gens.pop(0)
                    else:
                        break

        def drain():
            while gens:
                tick()

        def some_ada(n):
            for _ in range(n):
                PE.wait(AUX.free)
                ada_chunk(adan[0])
                adan[0] += 1
                tick()

        def lin_tm(ntt, H=HW, L=LW, toks=hb, ncols=256, bs=None):
            bs = bs or [bank() for _ in range(ntt // 2)]
            for u in range(2):
                h, l, wt = unit(4)
                ts_ = []
                for a in range(ntt):
                    o = bs[a // 2][:, (a % 2) * 256:(a % 2) * 256 + ncols]
                    for k in range(4):
                        c = 4 * u + k
                        xs = slice(a * 128, a * 128 + 128)
                        tok = mm3(o, H[:, c, xs], L[:, c, xs], h[:, k, 0:ncols], l[:, k, 0:ncols],
                                  c == 0 and a % 2 == 0, c == 7, wt, toks[c], inc=(k == 3))
                    ts_.append(tok)
                done(tok)
            return [(b, ts_[2 * i + 1]) for i, b in enumerate(bs)]

        def lin_mixed(w, H, L, toks):
            b, b2 = bank(), bank()
            for u in range(2):
                h, l, wt = unit(4)
                for k in range(4):
                    c = 4 * u + k
                    t = mm3(b[:, 0:256], h[:, k, 0:128], l[:, k, 0:128], H[:, c, :], L[:, c, :], c == 0, c == 7, wt, toks[c],
                            inc=(k == 3))
                for a in range(2):
                    for k in range(4):
                        c = 4 * u + k
                        xs = slice(a * 128, a * 128 + 128)
                        t2 = mm3(b2[:, a * w:a * w + w], H[:, c, xs], L[:, c, xs], h[:, k, 128:128 + w], l[:, k, 128:128 + w],
                                 c == 0 and a == 0, c == 7, inc=(k == 3))
                done(t2)
            return b, t, b2, t2

        for i in range(2):
            (b, t), = lin_tm(2, toks=hx)
            tp = act(PTM[:, :, i * 256:i * 256 + 256], b.two(), ACT.Copy, t)
            b.free = [tp]
            some_ada(1)
        ytoks = [None] * 12

        def pooling():
            tpy = [None, None]
            for gp in range(2):
                b = bank()
                for g in (2 * gp, 2 * gp + 1):
                    for a in range(2):
                        t = mm(b[:, (g % 2) * 256:(g % 2) * 256 + 256], PTM[:, a, g * 128:(g + 1) * 128], POOLM[:, a, g, :],
                               a == 0, a == 1, tp, t_pm, inc=(a == 1))
                tpy[gp] = act(PY[:, 2 * gp:2 * gp + 2, :], b.two(), ACT.Copy, t)
                b.free = [tpy[gp]]
            yield
            for gp in range(2):
                b = bank()
                for g in (2 * gp, 2 * gp + 1):
                    t = mm(b[:, (g % 2) * 256:(g % 2) * 256 + 256], WPOOL[:, g, :], PY[:, g, :], True, True, tpy[gp], inc=True)
                for g in (2 * gp, 2 * gp + 1):
                    u = ts(PY[:, g, :], b[:, (g % 2) * 256:(g % 2) * 256 + 256], par("pscale")[:, g:g + 1], None, ALU.mult, None, t)
                b.free = [u]
                y = split_into(YH[:, 4 + 2 * gp:6 + 2 * gp, :], YL[:, 4 + 2 * gp:6 + 2 * gp, :], PY[:, 2 * gp:2 * gp + 2, :], u)
                ytoks[4 + 2 * gp] = ytoks[5 + 2 * gp] = y

        gens.append(pooling())
        (b,), t_a = lin_fm(HW, LW, hb, ncols=128, N=512)
        bank_a = b
        drain()

        arena_at[0] = 0
        ph = everyone()
        SCM, GLM = ar(512), ar(256, 2)
        d_s = Dma("d_s")
        t_sm = d_s.go(SY, SCM, D["cst"][:, co["scanm"][0]:co["scanm"][1]], ph)
        t_sm = d_s.go(SY, GLM.rearrange("p a t -> p (a t)"), D["cst"][:, co["glam"][0]:co["glam"][1]], ph)
        WDEC = ar(512)
        t_wd = d_s.go(SY, WDEC[0:32, :], D["w_dec"], ph)
        t_sm = t_wd
        WDEC3 = WDEC.rearrange("p (d c) -> p d c", d=2)
        VT = ar(2048, 4)
        KS, QS = ar(1024, 2), ar(512, 2)
        QB, KB = ar(1024, 4), ar(1024, 4)
        LA4 = ar(2048, 4)
        KST = LA4.rearrange("p j (a d) -> p j a d", a=4)
        base = arena_at[0]
        ASB = ar(512)
        MNs, CUs, X1s = [ar(512), ar(512)], [ar(512), ar(512)], [ar(256), ar(256)]
        GS = ar(1024, 4)
        DV.wait(ph)
        AC.wait(ph)
        ta = act(ASB[0:32, :], bank_a[0:32, :], ACT.Copy, t_a)
        bank_a.free = [ta]
        DEC = small(16).rearrange("p (j n) -> p j n", j=4)
        qk, kst_t, vtok, kk = [None] * 4, [None] * 4, [], {}
        trf = [[], []]

        def decays():
            zb, te = [], []
            for j in range(4):
                d, m = j // 2, j % 2
                b = bank()
                t = mm(b[:, :], WDEC3[0:32, d, m * 128:(m + 1) * 128], ASB[0:32, :], True, True, ta, t_wd, inc=True)
                bd = par("bdec")[:, j:j + 1]
                i = j % 2
                t1 = act(LA4[:, j, :], b[:, :], ACT.Abs, t, bias=bd)
                zb.append((b, t1, bd))
            for j in range(4):
                te.append(act(LA4[:, j, :], LA4[:, j, :], ACT.Exp, zb[j][1], scale=-1.0))
            for j in range(4):
                te[j] = act(LA4[:, j, :], LA4[:, j, :], ACT.Ln, te[j], bias=1.0)
            yield
            seg = lambda v: v[:, 0:256].rearrange("p (n c) -> p n c", n=4)

            def first(j):
                d, i = j // 2, j % 2
                MN, CU, X1, LA = MNs[i], CUs[i], X1s[i], LA4[:, j, :]
                b, t1, bd = zb[j]
                t2 = ts(MN, b[:, :], bd, 0.0, ALU.add, ALU.min, t1, trf[i])
                b.free = [t2]
                t3 = tt(LA, MN, LA, ALU.subtract, te[j], t2)
                t4 = DV.run(lambda e: e.tensor_tensor_scan(CU, SCM, LA, 0.0, ALU.mult, ALU.add), t3, t_sm)
                tot = seg(CU)[:, :, 63:64]
                t5 = act(DEC[:, j, :].unsqueeze(2), tot, ACT.Exp, t4, scale=1.0 / 16)
                totb = tot.broadcast_to([128, 4, 64])
                if d == 0:
                    tt(seg(MN), totb, seg(CU), ALU.subtract, t4)
                    t6 = ts(MN[:, 256:512], CU[:, 256:512], CU[:, 511:512], -1.0, ALU.subtract, ALU.mult, t4)
                    xx = CU[:, 0:256]
                else:
                    t6 = tt(MN, CU, LA, ALU.subtract, t4)
                    t6 = tt(seg(X1), totb, seg(MN), ALU.subtract, t6)
                    xx = X1
                t7 = act(QB[:, j, :], xx, ACT.Exp, t6, scale=1.0 / 16)
                t8 = act(KB[:, j, :], xx, ACT.Exp, t6, scale=-1.0 / 16)
                t9 = act(LA, MN, ACT.Exp, t6, scale=1.0 / 16)
                trf[i] = [t9, t5, t8]
                return t7, t8, t9

            def second(j, tk):
                m, LA = j % 2, LA4[:, j, :]
                stt(QB[:, j, :], QB[:, j, :], 0.125, QS[:, m, :], ALU.mult, ALU.mult, tk[0], kk["q"])
                qk[j] = tt(KB[:, j, :], KB[:, j, :], KS[:, m, 0:256], ALU.mult, tk[1], kk["k"])
                return tt(LA, LA, KS[:, m, :], ALU.mult, tk[2])

            def third(j, u):
                bt = bank()
                for a in range(4):
                    v = transpose(bt[:, a * 128:(a + 1) * 128], LA4[:, j, a * 128:(a + 1) * 128], ident, u)
                w = act(KST[:, j, :, :], bt[:, :].rearrange("p (a d) -> p a d", a=4), ACT.Copy, v)
                bt.free = [w]
                kst_t[j] = w

            f, g = {}, {}
            for j in range(6):
                if j < 4:
                    f[j] = first(j)
                if j >= 2:
                    third(j - 2, g[j - 2])
                if 1 <= j < 5:
                    g[j - 1] = second(j - 1, f[j - 1])
                yield

        (some_ada(1))
        (b0, b1), t = lin_fm(HW, LW, hb, ncols=256, N=512)
        tk = act(KS[:, 0, :], b0[:, :], ACT.Copy, t)
        b0.free = [tk]
        kk["k"] = act(KS[:, 1, :], b1[:, :], ACT.Copy, t)
        b1.free = [kk["k"]]
        gens.append(decays())
        tick()
        some_ada(1)
        (b,), t = lin_fm(HX, LX, hx)
        kk["q"] = act(QS, b.two(), ACT.Copy, t)
        b.free = [kk["q"]]
        tick()
        some_ada(1)
        for i in range(2):
            for (a, (b, t)) in enumerate(lin_tm(4)):
                w = act(VT[:, 2 * a:2 * a + 2, i * 256:i * 256 + 256], b.two(), ACT.Copy, t)
                b.free = [w]
                vtok.append(w)
            tick()
            some_ada(1)
        (b,), t = lin_fm(HX, LX, hx)
        tg = act(GS[:, 0:2, :], b.two(), ACT.Silu, t)
        b.free = [tg]
        tick()
        drain()
        ph = everyone()
        arena_at[0] = base
        ST = ar(2048).rearrange("p (j n d) -> p j n d", j=4, n=4)
        SM = [ar(512), ar(512)]
        OTT = KS.rearrange("p k t -> p (k t)").rearrange("p (k t) -> p k t", k=4)
        sqt = QS.rearrange("p k t -> p (k t)")
        rst = SCM
        st_tok, otok = [None] * 4, [None] * 4

        def heads():
            def scores(h):
                m, p = h // 2, slice(64 * (h % 2), 64 * (h % 2) + 64)
                b = bank()
                for d in range(2):
                    for a in range(2):
                        c = slice(a * 128, a * 128 + 128)
                        t = mm(b[:, (d * 2 + a) * 128:(d * 2 + a) * 128 + 128], KB[p, 2 * d + m, c], QB[p, 2 * d + m, c],
                               True, True, qk, inc=True)
                s = SM[h % 2].rearrange("p (d a i) -> p d a i", d=2, a=2)
                for d in range(2):
                    u = tt(s[:, d, :, :], b[:, d * 256:d * 256 + 256].rearrange("p (a i) -> p a i", a=2),
                           GLM[:, d, :].unsqueeze(1).broadcast_to([128, 2, 128]), ALU.mult, t, smfree[h % 2], ph)
                b.free = [u]
                return u

            def states(j):
                d, m = j // 2, j % 2
                b = bank()
                for a in (2, 3):
                    t = mm(b[:, 0:256], KST[:, j, a, :], VT[:, a, m * 256:m * 256 + 256], a == 2, a == 3, kst_t, vtok,
                           inc=(a == 3))
                order_n = [0, 1, 2, 3] if d == 0 else [3, 2, 1, 0]
                for r in range(2):
                    p = slice(64 * r, 64 * r + 64)
                    u = vcopy(ST[p, j, order_n[0], :], b[p, r * 128:r * 128 + 128], t, ph)
                b.free = [u]
                for s in range(3):
                    n, nn = order_n[s], order_n[s + 1]
                    p = slice(64 * (n % 2), 64 * (n % 2) + 64)
                    b = bank()
                    t = mm(b[:, 0:256], KST[p, j, n // 2, :], VT[p, n // 2, m * 256:m * 256 + 256], True, True, inc=True)
                    for r in range(2):
                        p = slice(64 * r, 64 * r + 64)
                        v = stt(ST[p, j, nn, :], ST[p, j, n, :], DEC[p, j, n:n + 1], b[p, r * 128:r * 128 + 128],
                                ALU.mult, ALU.add, t, u)
                    u = v
                    b.free = [u]
                st_tok[j] = u

            def outs(h, u):
                m, p = h // 2, slice(64 * (h % 2), 64 * (h % 2) + 64)
                s = SM[h % 2].rearrange("p (d a i) -> p d a i", d=2, a=2)
                b = bank()
                for a in range(2):
                    o = b[:, a * 128:a * 128 + 128]
                    for d in range(2):
                        mm(o, VT[:, a, h * 128:h * 128 + 128], s[:, d, a, :], a == 0 and d == 0, False, u)
                        for n in (2 * a, 2 * a + 1):
                            t = mm(b[:, n * 64:n * 64 + 64], ST[p, 2 * d + m, n, :], QB[p, 2 * d + m, n * 64:n * 64 + 64],
                                   False, d == 1, st_tok[m], st_tok[2 + m], inc=True)
                smfree[h % 2] = [t]
                w = act(OTT[:, h, :], b[:, 0:256], ACT.Copy, t, ph)
                b.free = [w]
                otok[h] = w

            def gated(hp):
                o2 = OTT[:, 2 * hp:2 * hp + 2, :].rearrange("p a t -> p (a t)")
                a = act(sqt, o2, ACT.Square, otok[2 * hp:2 * hp + 2], gated.free)
                b = bank()
                t = mm(b[:, :], ones, sqt, True, True, a, inc=True)
                a = act(rst, b[:, :], ACT.Sqrt, t, gated.free, scale=1.0 / 128, bias=EPSA)
                b.free = [a]
                r = recip(rst, rst, a)
                u = stt(o2, o2, par("glag"), rst, ALU.mult, ALU.mult, r)
                gated.free = [t, u]
                u = tt(o2, o2, GS[:, 2 * hp:2 * hp + 2, :].rearrange("p a t -> p (a t)"), ALU.mult, u, gtok[hp])
                y = split_into(YH[:, 2 * hp:2 * hp + 2, :], YL[:, 2 * hp:2 * hp + 2, :], OTT[:, 2 * hp:2 * hp + 2, :], u)
                ytoks[2 * hp] = ytoks[2 * hp + 1] = y

            gated.free = [ph]
            smfree = [[], []]
            states(0)
            u0 = scores(0)
            yield
            states(2)
            u1 = scores(1)
            yield
            outs(0, u0)
            states(1)
            u0 = scores(2)
            yield
            outs(1, u1)
            states(3)
            u1 = scores(3)
            yield
            gated(0)
            outs(2, u0)
            yield
            outs(3, u1)
            yield
            gated(1)
            yield

        gtok = [tg, None]
        gens.append(heads())
        some_ada(4)
        (b,), t = lin_fm(HX, LX, hx)
        gtok[1] = tg = act(GS[:, 2:4, :], b.two(), ACT.Silu, t)
        b.free = [tg]
        tick()
        some_ada(5)
        drain()
        ada_turn()
        t1 = mod_rows(16, 48, ada_turn.tok)
        GTA, SHM, GTM = (MOD3[:, a:a + 8, 0] for a in (16, 24, 40))
        A2, B2, G2, G3, GF = small(8), small(8), small(8), small(8), small(8)
        tt(GF, par("final1"), par("ffn1n"), ALU.mult, t1)
        vcopy(B2, SHM, t1)
        vcopy(G2, GTA, t1)
        vcopy(G3, GTM, t1)
        t_mod = stt(A2, MOD3[:, 32:40, 0], 1.0, par("norm2"), ALU.add, ALU.mult, t1)
        DV.wait(t_mod)
        AC.wait(t_mod)

        def add_out(b, i, t, gate):
            for r in range(2):
                k = 2 * i + r
                s = gate if isinstance(gate, float) else gate[:, k:k + 1]
                u = stt(XT[:, k, :], b[:, r * 256:r * 256 + 256], s, XT[:, k, :], ALU.mult, ALU.add, t)
            b.free = [u]
            return u

        def stats(b, i, u):
            for k in (2 * i, 2 * i + 1):
                s = stat_step(XT[:, k, :], b, k, 8, u)
            return s

        class Unscaled:

            def __init__(self, gain, H, L):
                self.gain, self.H, self.L, self.free = gain, H, L, PE.last()
                self.toks, self.low = [None] * 8, []

            def block(self, i, u):
                low, self.low = self.low, []
                for k in (2 * i, 2 * i + 1):
                    g = self.gain[:, k:k + 1]
                    th = act(self.H[:, k, :], XT[:, k, :], ACT.Copy, u, self.free, scale=g)
                    self.low.append((k, g, th))
                self.lows(low)

            def lows(self, low):
                for k, g, th in low:
                    tl = stt(self.L[:, k, :], XT[:, k, :], g, self.H[:, k, :].bitcast(f32), ALU.mult, ALU.subtract, th, self.free)
                    self.toks[k] = [th, tl]

            def end(self):
                self.lows(self.low)
                return self.toks

        def project(yh, yl, toks, gate, rots, un=None):
            rotate(rots)
            us = []
            for i in range(4):
                (b,), t = lin_fm(yh, yl, toks)
                if i:
                    if i == 1:
                        PE.wait(AUX.free)
                    stats(AUX, i - 1, us[-1])
                us.append(add_out(b, i, t, gate))
                if un:
                    un.block(i, us[-1])
            return us

        us = project(YH, YL, ytoks, G2, BK[0:3] + BK[4:8])
        s = stats(AUX, 3, us[3])
        norm.src = XT
        H0, L0 = half(HHt, 0), half(HLt, 0)
        ht = norm(AUX, s, A2, B2, H0, L0, PE.last())

        arena_at[0] = 0
        ph = everyone()
        DV.wait(ph)
        AC.wait(ph)
        rotate(BK[0:3] + BK[4:8])
        CAP = 128
        TRI, IOTA = ar(128), ar(128)
        d_t = Dma("d_t")
        t_tri = d_t.go(SY, TRI, D["cst"][:, co["tri"][0]:co["tri"][1]], ph)
        t_tri = d_t.go(SY, IOTA, D["cst"][:, co["iota"][0]:co["iota"][1]])
        LG = ar(72).rearrange("p (a e) -> p a e", a=2)
        (b, t), = lin_tm(2, H=H0, L=L0, toks=ht, ncols=36)
        u = vcopy(LG, b.two()[:, :, 0:36], t)
        b.free = [u]
        TH = HHt[:, 2048:4096].rearrange("p (a f) -> p a f", a=2)
        TL = HLt[:, 2048:4096].rearrange("p (a f) -> p a f", a=2)
        t_tm = []
        free_half = PE.last()
        for src, dst in ((H0, TH), (L0, TL)):
            for a in range(2):
                for kq in range(2):
                    bt = bank()
                    for k in range(4):
                        t = transpose(bt[:, k * 128:(k + 1) * 128], src[:, 4 * kq + k, a * 128:a * 128 + 128].bitcast(f32),
                                      ident, ht)
                    w = act(dst[:, a, kq * 512:kq * 512 + 512], bt[:, :], ACT.Copy, t, free_half)
                    bt.free = [w]
                    t_tm.append(w)
        mg, e4, sg, gp = ar(2).unsqueeze(2), ar(8).rearrange("p (a g) -> p a g", a=2), ar(2).unsqueeze(2), ar(2).unsqueeze(2)
        L4, L32 = LG[:, :, 0:4], LG[:, :, 4:36].rearrange("p a (g j) -> p a g j", g=4)
        v1 = rmax(mg, L4, u)
        u = tt(e4, L4, mg.broadcast_to([128, 2, 4]), ALU.subtract, v1)
        w = act(e4, e4, ACT.Exp, u)
        u = rsum(sg, e4, w)
        u = recip(gp, sg, u)
        IW = cst("idxw")

        def first_max(x, mx, n, *toks):
            key, oh, km = ar(2 * n).rearrange("p (a j) -> p a j", a=2), ar(2 * n).rearrange("p (a j) -> p a j", a=2), ar(2).unsqueeze(2)
            u = tt(key, x, mx.broadcast_to([128, 2, n]), ALU.is_equal, *toks)
            u = tt(key, key, IW[:, 0:n].unsqueeze(1).broadcast_to([128, 2, n]), ALU.mult, u)
            u = rmax(km, key, u)
            u = tt(oh, key, km.broadcast_to([128, 2, n]), ALU.is_equal, u)
            return oh, u

        ohg, ug = first_max(L4, mg, 4, v1)
        b = bank()
        t = mm(b[:, 0:4], TRI, ohg[:, 0, :], True, True, ug, t_tri, inc=True)
        mm(b[:, 8:12], ones, ohg[:, 0, :], True, False)
        t = mm(b[:, 8:12], TRI, ohg[:, 1, :], False, True, inc=True)
        mm(b[:, 16:20], ones, ohg[:, 0, :], True, False)
        t = mm(b[:, 16:20], ones, ohg[:, 1, :], False, True, inc=True)
        RANK = ar(16).rearrange("p (a g) -> p a g", a=2)
        vr = vcopy(RANK, b[:, 0:16].rearrange("p (a g) -> p a g", a=2), t)
        MX, FLAG = ar(1), ar(1).bitcast(i32)
        vf = rmax(MX, b[:, 16:20], t)
        b.free = [vr, vf]
        t_flag = ts(FLAG, MX, CAP + 0.5, None, ALU.is_gt, None, vf)
        sel = ar(64).rearrange("p (a g j) -> p a g j", a=2, g=4)
        ug2 = None
        for a in range(2):
            ug2 = tt(sel[:, a], L32[:, a], ohg[:, a, :].unsqueeze(2).broadcast_to([128, 4, 8]), ALU.mult, ug)
        le = ar(16).rearrange("p (a j) -> p a j", a=2)
        for a in range(2):
            u = rsum(le[:, a, :].unsqueeze(2), sel[:, a].rearrange("p g j -> p j g"), ug2)
        m1, m2 = ar(2).unsqueeze(2), ar(2).unsqueeze(2)
        u1 = rmax(m1, le, u)
        oh1, u = first_max(le, m1, 8, u1)
        le2 = ar(16).rearrange("p (a j) -> p a j", a=2)
        u = stt(le2, oh1, -3e38, le, ALU.mult, ALU.add, u)
        u2 = rmax(m2, le2, u)
        oh2, u = first_max(le2, m2, 8, u2)
        ex, w1, w2, sd = ar(2).unsqueeze(2), ar(2).unsqueeze(2), ar(2).unsqueeze(2), ar(2).unsqueeze(2)
        u = tt(ex, m2, m1, ALU.subtract, u)
        w = act(ex, ex, ACT.Exp, u)
        u = ts(sd, ex, 1.0, None, ALU.add, None, w)
        u = recip(sd, sd, u)
        u = tt(w1, sd, gp, ALU.mult, u)
        u = tt(w2, w1, ex, ALU.mult, u)
        u = tt(oh1, oh1, w1.broadcast_to([128, 2, 8]), ALU.mult, u)
        u = tt(oh2, oh2, w2.broadcast_to([128, 2, 8]), ALU.mult, u)
        u = tt(oh1, oh1, oh2, ALU.add, u)
        G32 = ar(64).rearrange("p (a g j) -> p a g j", a=2, g=4)
        for a in range(2):
            ug = tt(G32[:, a], ohg[:, a, :].unsqueeze(2).broadcast_to([128, 4, 8]), oh1[:, a, :].unsqueeze(1).broadcast_to([128, 4, 8]),
                    ALU.mult, u)
        def fork(fast, general, flag, t_flag):
            lanes = [PE, DV, AC, SY]
            for L in lanes:
                L.wait(t_flag)
            lists = lambda: [x[:] for x in (sfree, sqfree, rsfree, tnfree)]
            keep = ([(L.q, L.n, dict(L.seen)) for L in lanes], dict(st), dict(released), dict(loaded), dict(parts), lists(),
                    [b.free for b in BK], dict(rot), sqn[0], arena_at[0], [d.n for d in RD])
            bodies, counts, dmas = [], [], []
            for body in (fast, general):
                for L, (q, n, seen) in zip(lanes, keep[0]):
                    L.q, L.n, L.seen = [], n, dict(seen)
                st.update(keep[1])
                for d, k in zip((released, loaded, parts), keep[2:5]):
                    d.clear()
                    d.update(k)
                for x, k in zip((sfree, sqfree, rsfree, tnfree), keep[5]):
                    x[:] = k
                for b, f in zip(BK, keep[6]):
                    b.free = f
                rot.update(keep[7])
                sqn[0], arena_at[0] = keep[8], keep[9]
                for d, n in zip(RD, keep[10]):
                    d.n = n
                body()
                bodies.append([L.q for L in lanes])
                counts.append([L.n for L in lanes])
                dmas.append(([d.n for d in RD], dict(st)))
            assert dmas[0] == dmas[1]
            for x, L in enumerate(lanes):
                top = max(c[x] for c in counts) + 1
                if L is not SY:
                    for c, bd in zip(counts, bodies):
                        bd[x].append(lambda e, L=L, n=c[x]: e.wait_ge(L.sem, n))
                        bd[x].append(lambda e, L=L, d=top - c[x]: e.sem_inc(L.sem, d))
                    L.n = top
                L.q, L.seen = keep[0][x][0], keep[0][x][2]
                L.q.append((flag, bodies[0][x], bodies[1][x]))
            for L in lanes:
                L.wait(everyone())
            return PE.last()

        def swiglu(n, ht, H, L, gated, scale, SB, TB, t_gt=None, late=None, hooks={}, un=None):
            rotate(BK[0:3])
            ahl = [None, None]
            pend = None
            sfr, tfr, afr = [[], []], [[], []], [[PE.last()], [PE.last()]]

            def down(i, toks):
                y = 4 * (i % 2)
                for k in range(2):
                    h, l, wt = unit(1)
                    res = []
                    for nb in range(8):
                        bb = YB[nb // 2]
                        if i == 0 and k == 0 and nb % 2 == 0:
                            PE.wait(bb.free)
                        t = mm3(bb[:, (nb % 2) * 256:(nb % 2) * 256 + 256], h[:, 0, nb * 128:nb * 128 + 128],
                                l[:, 0, nb * 128:nb * 128 + 128], YH[:, y + k, :], YL[:, y + k, :],
                                i == 0 and nb % 2 == 0 and k == 0, i == n - 1 and k == 1, wt, toks,
                                inc=(nb == 7 or i == n - 1))
                        res.append(t)
                    done(t)
                afr[i % 2] = [t]
                return res

            for i in range(n):
                (bg,), tg = lin_fm(H, L, ht)
                if gated:
                    PE.wait(AUX.free)
                    ta = mm(AUX[:, 0:256], ident[0:32, i:i + 1].broadcast_to([32, 128]), GT[0:32, :], True, True, t_gt, inc=True)
                (bu,), tu = lin_fm(H, L, ht)
                if i == 0 and late:
                    t_rs = late()
                if i in hooks:
                    hooks[i]()
                S, T = SB[i % 2], TB[i % 2]
                if late:
                    u = tt(S, bg.two(), RSX2, ALU.mult, tg, sfr[i % 2], t_rs)
                    bg.free = [u]
                    u = act(S, S, ACT.Silu, u)
                else:
                    u = act(S, bg.two(), ACT.Silu, tg, sfr[i % 2])
                    bg.free = [u]
                if gated:
                    u = tt(S, S, AUX[:, 0:256].unsqueeze(1).broadcast_to([128, 2, 256]), ALU.mult, u, ta)
                    AUX.free = [u]
                u = tt(T, S, bu.two(), ALU.mult, u, tu, tfr[i % 2])
                bu.free = [u]
                sfr[i % 2] = [u]
                if late:
                    u = tt(T, T, RSX2, ALU.mult, u)
                y = 4 * (i % 2)
                toks = split_into(YH[:, y:y + 2, :], YL[:, y:y + 2, :], T, u, afr[i % 2])
                tfr[i % 2] = toks
                if pend is not None:
                    down(*pend)
                pend = (i, toks)
            res = down(*pend)
            us = []
            for i in range(4):
                us.append(add_out(YB[i], i, res[2 * i + 1], scale))
                if un:
                    un.block(i, us[-1])
            return us

        def all_stats(us):
            PE.wait(AUX.free)
            for i in range(4):
                s = stats(AUX, i, us[i])
            return s

        SB, TB = [ar(512, 2), ar(512, 2)], [ar(512, 2), ar(512, 2)]
        GT = ar(256)

        def dense():
            b = bank()
            for a in range(2):
                t = transpose(b[0:32, a * 128:a * 128 + 128], G32[:, a].rearrange("p g j -> p (g j)"), ident, ug)
            t_gt = act(GT[0:32, :], b[0:32, 0:256], ACT.Copy, t)
            b.free = [t_gt]
            all_stats(swiglu(32, ht, H0, L0, True, G3, SB, TB, t_gt))

        def grouped():
            rotate(BK[0:3])
            PG = YHt[:, 1024:2048].rearrange("p (g a s) -> p g a s", g=4, a=2)
            PT = YLt[:, 1024:2048].rearrange("p (g t) -> p g t", g=4)
            YGH, YGL = YHt[:, 2048:3072], YLt[:, 2048:3072]
            fr = [PE.last()]
            for g in range(4):
                for a in range(2):
                    tp = ts(PG[:, g, a, :], IOTA, RANK[:, a, g:g + 1], ohg[:, a, g:g + 1], ALU.is_equal, ALU.mult,
                            vr, t_tri, fr)
            gx = [[], []]
            gfree = [[], []]

            def gather(g):
                toks = []
                for src, dst in ((TH, HHt), (TL, HLt)):
                    for kq in range(2):
                        b = bank()
                        for k in range(4):
                            c = slice((4 * kq + k) * 128, (4 * kq + k) * 128 + 128)
                            o = b[:, k * 128:k * 128 + 128]
                            mm(o, src[:, 0, c], PG[:, g, 0, :], True, False, tp, t_tm)
                            t = mm(o, src[:, 1, c], PG[:, g, 1, :], False, True, inc=True)
                        w = act(dst[:, 1024 * (g % 2) + 512 * kq:1024 * (g % 2) + 512 * kq + 512], b[:, :], ACT.Copy, t,
                                gfree[g % 2], fr)
                        b.free = [w]
                        toks.append(w)
                gx[g % 2] = [toks] * 8

            gather(0)
            GC = ar(32).rearrange("p (g j) -> p g j", g=4)
            b = bank()
            for g in range(4):
                for a in range(2):
                    t = mm(b[:, 8 * g:8 * g + 8], PG[:, g, a, :].bitcast(f32), G32[:, a, g, :], a == 0, a == 1, ug, tp,
                           inc=(a == 1))
            t_gc = vcopy(GC, b[:, 0:32].rearrange("p (g j) -> p g j", g=4), t)
            b.free = [t_gc]
            for gq in range(2):
                b = bank()
                for g in (2 * gq, 2 * gq + 1):
                    for a in range(2):
                        t = transpose(b[:, (g % 2) * 256 + a * 128:(g % 2) * 256 + a * 128 + 128],
                                      PG[:, g, a, :].bitcast(f32), ident, tp)
                t_pt = act(PT[:, 2 * gq:2 * gq + 2, :], b.two(), ACT.Copy, t, fr)
                b.free = [t_pt]
            sfr, tfr, afr = [[], []], [[], []], [[], []]
            sc = {"y": fr, "x": None}

            def down(i, toks):
                g, y = i // 8, 256 * (i % 2)
                ah = YHt[:, y:y + 256].rearrange("p (k s) -> p k s", k=2)
                al = YLt[:, y:y + 256].rearrange("p (k s) -> p k s", k=2)
                for k in range(2):
                    h, l, wt = unit(1)
                    res = []
                    for q in range(2):
                        b = YB[2 * (g % 2) + q]
                        if i % 8 == 0 and k == 0:
                            PE.wait(b.free)
                        t = mm3(b[:, :], ah[:, k, :], al[:, k, :], h[:, 0, q * 512:q * 512 + 512], l[:, 0, q * 512:q * 512 + 512],
                                i % 8 == 0 and k == 0, i % 8 == 7 and k == 1, wt, toks, inc=True)
                        res.append(t)
                    done(t)
                afr[i % 2] = [t]
                return res

            def lin_slots(X, XL, toks):
                b = bank()
                for u in range(2):
                    h, l, wt = unit(4)
                    for k in range(4):
                        c = 4 * u + k
                        t = mm3(b[:, 0:256], X[:, c, :], XL[:, c, :], h[:, k, :], l[:, k, :], c == 0, c == 7, wt, toks[c],
                                inc=(k == 3))
                    done(t)
                return b, t

            def scatter(g, res, last):
                for q in range(2):
                    b = YB[2 * (g % 2) + q]
                    c = slice(512 * q, 512 * q + 512)
                    th = act(YGH[:, c], b[:, :], ACT.Copy, res[q], sc["y"])
                    tl = tt(YGL[:, c], b[:, :], YGH[:, c].bitcast(f32), ALU.subtract, th, sc["y"])
                    b.free = [tl]
                for i in range(4):
                    b = bank()
                    for r in range(2):
                        k = 2 * i + r
                        o = b[:, r * 256:r * 256 + 256]
                        mm(o, YGH[:, k * 128:k * 128 + 128], PT[:, g, :], True, False, th, tl, t_pt)
                        t = mm(o, YGL[:, k * 128:k * 128 + 128], PT[:, g, :], False, True, inc=True)
                    u = add_out(b, i, [t, sc["x"]], G3)
                    if last:
                        stats(AUX, i, u)
                sc["x"] = u
                sc["y"] = [t]

            pend = None
            for i in range(32):
                g = i // 8
                X, XL = (T[:, 1024 * (g % 2):1024 * (g % 2) + 1024].rearrange("p (k s) -> p k s", k=8) for T in (HHt, HLt))
                bg, tg = lin_slots(X, XL, gx[g % 2])
                bu, tu = lin_slots(X, XL, gx[g % 2])
                if i % 8 == 7:
                    gfree[g % 2] = [tu]
                S, T = (v[i % 2].rearrange("p k t -> p (k t)")[:, 0:256] for v in (SB, TB))
                u = act(S, bg[:, 0:256], ACT.Silu, tg, sfr[i % 2])
                bg.free = [u]
                u = stt(T, S, GC[:, g, i % 8:i % 8 + 1], bu[:, 0:256], ALU.mult, ALU.mult, u, tu, tfr[i % 2], t_gc)
                bu.free = [u]
                sfr[i % 2] = [u]
                if pend is not None:
                    res = down(*pend)
                    if i % 8 == 0:
                        scatter(g - 1, res, False)
                PE.wait(AUX.free)
                for k in range(2):
                    t = transpose(AUX[:, k * 128:k * 128 + 128], T[:, k * 128:k * 128 + 128], ident, u)
                tfr[i % 2] = [t]
                y = 256 * (i % 2)
                toks = split_into(YHt[:, y:y + 256], YLt[:, y:y + 256], AUX[:, 0:256], t, afr[i % 2])
                AUX.free = toks
                pend = (i, toks)
                if i % 8 == 5 and g < 3:
                    gather(g + 1)
            res = down(*pend)
            PE.wait(AUX.free)
            scatter(3, res, True)

        s = fork(grouped, dense, FLAG, t_flag)
        top = AR - 2560
        hi = lambda n, k=None: (ARt[:, top:top + n] if k is None else ARt[:, top:top + n].rearrange("p (k t) -> p k t", k=k))
        COS, SIN = hi(512, 2), ARt[:, top + 512:top + 1024].rearrange("p (k t) -> p k t", k=2)
        DECM = ARt[:, top + 1024:AR].rearrange("p (h c) -> p h c", h=4)
        POSI, PF = ARt[:, top - 512:top - 256].bitcast(i32), ARt[:, top - 256:top]
        ANG, KK, RR = (ARt[:, a:a + 512].rearrange("p (k t) -> p k t", k=2) for a in (top - 1024, top - 1536, top - 2048))
        assert arena_at[0] + 256 < top - 2048
        ph = everyone()
        d_q = Dma("d_q")
        t_dec = d_q.go(SY, DECM.rearrange("p h c -> p (h c)"), D["cst"][:, co["dec"][0]:co["dec"][1]], ph)
        d_pos = Dma("d_pos")
        t_pos = d_pos.go(SY, POSI, D["pos"].broadcast_to([128, 256]), ph)
        rtab = []

        def rope_tables():
            u = vcopy(PF, POSI, t_pos)
            for i in range(2):
                u = ts(ANG[:, i, :], PF, cst("inv")[:, i:i + 1], None, ALU.mult, None, u)
            MAGIC = 12582912.0
            C1, C2 = 6.28125, float(np.float32(0.0019340515136718750))
            C3 = float(2 * np.pi - 6.28125 - np.float64(C2))
            u = ts(KK, ANG, float(1 / (2 * np.pi)), MAGIC, ALU.mult, ALU.add, u)
            u = ts(KK, KK, -MAGIC, None, ALU.add, None, u)
            u = stt(RR, KK, -C1, ANG, ALU.mult, ALU.add, u)
            u = stt(RR, KK, -C2, RR, ALU.mult, ALU.add, u)
            u = stt(RR, KK, -C3, RR, ALU.mult, ALU.add, u)
            PI = 3.1415925
            v = ts(ANG, RR, PI, -PI, ALU.min, ALU.max, u)
            w = act(SIN, ANG, ACT.Sin, v)
            u = ts(RR, RR, float(np.pi / 2), None, ALU.add, None, v)
            u = ts(KK, RR, float(np.pi), float(-2 * np.pi), ALU.is_gt, ALU.mult, u)
            u = tt(RR, RR, KK, ALU.add, u)
            u = ts(RR, RR, PI, -PI, ALU.min, ALU.max, u)
            rtab.extend([act(COS, RR, ACT.Sin, u), w])

        RSX = ar(256)
        RSX2 = RSX.unsqueeze(1).broadcast_to([128, 2, 256])
        un = Unscaled(GF, H0, L0)
        for i in range(4):
            un.block(i, s)
        ht = un.end()

        def late_first():
            t = rstd(AUX, s, 1.0 / 1024, EPSA)
            vcopy(RSX, RS[:, :], t)
            us = []
            for i in range(4):
                for k in (2 * i, 2 * i + 1):
                    u = stt(XT[:, k, :], XT[:, k, :], par("final1")[:, k:k + 1], RS[:, :], ALU.mult, ALU.mult, t, ht[k])
                us.append(u)
            rsfree[0] = [u]
            t = rstd(AUX, all_stats(us), 1.0 / 1024, EPSA)
            t = tt(RSX, RSX, RS[:, :], ALU.mult, t)
            rsfree[0] = [t]
            return t

        un = Unscaled(par("mixn"), H0, L0)
        us = swiglu(11, ht, H0, L0, False, 0.5, SB, TB, late=late_first, hooks={3: rope_tables}, un=un)
        ht = un.end()

        ph = everyone()
        DV.wait(ph)
        AC.wait(ph)
        arena_at[0] = 0
        rotate(BK[0:3] + BK[4:8])
        AC.wait(rtab)
        DV.wait(rtab)
        TR = [ar(512, 2), ar(512, 2)]
        TA = ar(512, 2)
        trf = [[], []]
        trn = [0]

        RT, rope_pend = {}, []

        def rope(b, n, t, kind, dst, name, t_rs=None):
            i = trn[0] % 2
            trn[0] += 1
            T = TR[i][:, 0:n, :]
            if t_rs:
                w = tt(T, b.two()[:, 0:n, :], RS[:, :].unsqueeze(1).broadcast_to([128, n, 256]), ALU.mult, t, trf[i], t_rs)
                rsfree[0] = [w]
            else:
                w = act(T, b.two()[:, 0:n, :], ACT.Copy, t, trf[i])
            b.free = [w]
            c = COS[:, kind, :].unsqueeze(1).broadcast_to([128, n, 256])
            s = SIN[:, kind, :].unsqueeze(1).broadcast_to([128, n, 256])

            def rest():
                b2 = bank()
                t = mm(b2[:, 0:n * 256], cst("rr" if kind else "ra"), T.rearrange("p k t -> p (k t)"), True, True, w, inc=True)
                u = tt(dst, T, c, ALU.mult, w)
                u2 = tt(T, b2.two()[:, 0:n, :], s, ALU.mult, t, u)
                b2.free = [u2]
                u = tt(dst, dst, T, ALU.add, u, u2)
                trf[i] = [u]
                RT.setdefault(name, []).append(u)

            rope_pend.append(rest)

        def rope_rest():
            while rope_pend:
                rope_pend.pop(0)()

        IK, IWT = ar(256), small(16).rearrange("p (a h) -> p a h", a=2)
        yn_at = arena_at[0]
        IQ, SCO, WK = ar(1024, 4), ar(512, 2), ar(512, 2)
        MB = ar(512, 2)
        H1, L1 = half(HHt, 1), half(HLt, 1)
        (b,), t = lin_fm(H0, L0, ht)
        hn = norm(AUX, all_stats(us), par("mixn"), None, H1, L1, PE.last())
        rope(b, 2, t, 0, IQ[:, 0:2, :], "iq", hn[0])
        (b,), t = lin_fm(H0, L0, ht)
        rope_rest()
        rope(b, 2, t, 0, IQ[:, 2:4, :], "iq", hn[0])
        b, t, b2, t2 = lin_mixed(8, H1, L1, hn)
        w_iw = ts(IWT, b2[:, 0:16].rearrange("p (a h) -> p a h", a=2), float(np.float32(8 ** -0.5)), 0.125, ALU.mult, ALU.mult, t2)
        b2.free = [w_iw]
        rope_rest()
        rope(b, 1, t, 0, IK.unsqueeze(1), "ik")
        RL = [ar(512, 2), ar(512, 2)]
        rlf = [[], []]
        M8 = small(16).rearrange("p (a h) -> p a h", a=2)

        def indexer():
            n = 0
            ut = None
            for a in range(2):
                for hp in range(4):
                    b = bank()
                    for r in range(2):
                        p = slice(64 * r, 64 * r + 64)
                        t = mm(b[:, r * 256:r * 256 + 256], IQ[p, hp, a * 128:a * 128 + 128], IK[p, :], True, True,
                               RT["ik"], RT["iq"], PE.last(), inc=True)
                    R = RL[n % 2]
                    w = act(R, b.two(), ACT.Relu, t, rlf[n % 2])
                    b.free = [w]
                    for r in range(2):
                        hh = 2 * hp + r
                        if hh == 0:
                            ut = ts(SCO[:, a, :], R[:, r, :], IWT[:, a, hh:hh + 1], None, ALU.mult, None, w)
                        else:
                            ut = stt(SCO[:, a, :], R[:, r, :], IWT[:, a, hh:hh + 1], SCO[:, a, :], ALU.mult, ALU.add, w, ut)
                    rlf[n % 2] = [ut]
                    n += 1
                    if hp == 1:
                        yield
                indexer.logits = t
                yield
            for p0, p1, a, c in ((0, 64, 0, 64), (64, 128, 0, 128), (0, 64, 1, 192)):
                v = DV.run(lambda e, p0=p0, p1=p1, a=a, c=c: e.memset(SCO[p0:p1, a, c:256], -1e30), ut)
            src = [SCO[:, 0, :], SCO[:, 1, :]]
            prev = [v, v]
            for r in range(8):
                for a in range(2):
                    u = DV.run(lambda e, a=a, s=src[a]: e.max(M8[:, a, :], s), prev[a])
                    prev[a] = DV.run(lambda e, a=a, s=src[a]: e.match_replace(WK[:, a, :], M8[:, a, :], s, -3e38), u)
                    src[a] = WK[:, a, :]
                if r % 4 == 3:
                    yield
            u = ts(MB, WK, -3e38, -1e30, ALU.is_gt, ALU.mult, prev)
            indexer.tok = u
            yield

        RQ_at = arena_at[0]
        RQ, RK, RV = ar(1024, 4), ar(1024, 4), ar(2048).rearrange("p (a c) -> p a c", a=2)
        AQ, AK = ar(1024, 4), ar(256)
        AV = IK.rearrange("p (a c) -> p a c", a=2)
        YN = ARt[:, yn_at:yn_at + 2048].rearrange("p (k t) -> p k t", k=8)
        P2 = [ARt[:, RQ_at:RQ_at + 512].rearrange("p (k t) -> p k t", k=2),
              ARt[:, RQ_at + 512:RQ_at + 1024].rearrange("p (k t) -> p k t", k=2)]
        PT = RK.rearrange("p k t -> p (k t)").rearrange("p (h s q) -> p h s q", h=2, s=2)
        SGA = RV.rearrange("p a c -> p (a c)").rearrange("p (j k t) -> p j k t", j=4, k=2)
        NM, SS = [small(4), small(4)], [small(4), small(4)]

        ret = {}
        t_rv, ynt = [None] * 4, [None] * 4

        def ret_scores(h4):
            b = bank()
            mm(b[:, 0:256], RK[:, h4, 0:128], RQ[:, h4, :], True, True, RT["rq"], RT["rk"])
            t = mm(b[:, 256:384], RK[:, h4, 128:256], RQ[:, h4, 128:256], True, True, inc=True)
            ret_scores.tok = t
            S = RL[h4 % 2].rearrange("p k t -> p (k t)")
            u = tt(S[:, 0:384], b[:, 0:384], DECM[:, h4, :], ALU.mult, t, t_dec, rlf[h4 % 2])
            b.free = [u]
            ret[h4] = u

        def ret_values(h4):
            S = RL[h4 % 2].rearrange("p k t -> p (k t)")
            b = bank()
            for e in range(2):
                c = slice(h4 * 256 + e * 128, h4 * 256 + e * 128 + 128)
                mm(b[:, e * 256:e * 256 + 256], RV[:, 0, c], S[:, 0:256], e == 0, False, ret[h4], t_rv[h4])
                t = mm(b[:, e * 256 + 128:e * 256 + 256], RV[:, 1, c], S[:, 256:384], False, True, inc=True)
            ret_values.tok = t
            rlf[h4 % 2] = [t]
            w = act(YN[:, 2 * h4:2 * h4 + 2, :], b.two(), ACT.Copy, t, indexer.logits if h4 < 2 else indexer.tok)
            b.free = [w]
            ret[h4] = w

        def ret_mean(h4):
            Y2 = YN[:, 2 * h4:2 * h4 + 2, :]
            b = bank()
            for e in range(2):
                t = mm(b[:, 0:256], ones, Y2[:, e, :], e == 0, e == 1, ret[h4], inc=(e == 1))
            u = stt(Y2, b[:, 0:256].unsqueeze(1).broadcast_to([128, 2, 256]), -1.0 / 256, Y2, ALU.mult, ALU.add, t)
            b.free = [u]
            sq = []
            for e in range(2):
                i = sqn[0] % 2
                sqn[0] += 1
                sq.append((i, act(SQ[i][:, :], Y2[:, e, :], ACT.Square, u, sqfree[i])))
            ret[h4] = (u, sq)

        def ret_var(h4):
            u, sq = ret[h4]
            b = bank()
            for e, (i, w) in enumerate(sq):
                t = mm(b[:, 0:256], ones, SQ[i][:, :], e == 0, e == 1, w, inc=True)
                sqfree[i] = [t]
            v = rstd(b, t, 1.0 / 256, EPSG)
            for k in (2 * h4, 2 * h4 + 1):
                u = stt(YN[:, k, :], YN[:, k, :], par("retgn")[:, k:k + 1], RS[:, :], ALU.mult, ALU.mult, v)
            rsfree[0] = [u]
            ynt[h4] = u

        def retention():
            for n in range(7):
                for k, step in enumerate((ret_var, ret_mean, ret_values, ret_scores)):
                    if 0 <= n - 3 + k < 4:
                        step(n - 3 + k)
                yield

        att, pf, pw, su, ptf = {}, [[], []], [[], []], [[], []], [[]]

        def att_probs(n):
            hp, a, i = n // 2, n % 2, n % 2
            b = bank()
            for r in range(2):
                p = slice(64 * r, 64 * r + 64)
                t = mm(b[:, r * 256:r * 256 + 256], AQ[p, hp, a * 128:a * 128 + 128], AK[p, :], True, True,
                       RT["aq"], RT["ak"], PE.last(), inc=True)
            P, M, Z = P2[i], NM[i], SS[i]
            u = stt(P, b.two(), 0.125, MB[:, a, :].unsqueeze(1).broadcast_to([128, 2, 256]), ALU.mult, ALU.add,
                    t, indexer.tok, pf[i], ret_scores.tok)
            b.free = [u]
            u = DV.run(lambda e: e.tensor_reduce(M[:, 0:2].unsqueeze(2), P, AX.X, ALU.max), u)
            u = ts(M[:, 2:4], M[:, 0:2], -1.0, None, ALU.mult, None, u, pw[i])
            for r in range(2):
                w = act(P[:, r, :], P[:, r, :], ACT.Exp, u, su[i], bias=M[:, 2 + r:3 + r], accum_out=Z[:, r:r + 1])
            pw[i] = [w]
            u = recip(Z[:, 2:4], Z[:, 0:2], w)
            for r in range(2):
                u = ts(P[:, r, :], P[:, r, :], Z[:, 2 + r:3 + r], None, ALU.mult, None, u)
            su[i] = [u]
            att[n] = u

        def att_turn(n):
            a, P = n % 2, P2[n % 2]
            b = bank()
            for r in range(2):
                for s in range(2):
                    t = transpose(b[:, (r * 2 + s) * 128:(r * 2 + s) * 128 + 128], P[:, r, s * 128:s * 128 + 128], ident, att[n])
            pf[n % 2] = [t]
            w = act(PT[:, :, :, a * 128:a * 128 + 128], b[:, :].rearrange("p (h s q) -> p h s q", h=2, s=2),
                    ACT.Copy, t, ptf[0])
            b.free = [w]
            att["pt"] = w

        def att_values(hp):
            b = bank()
            for r in range(2):
                for s in range(2):
                    t = mm(b[:, r * 256:r * 256 + 256], AV[:, s, :], PT[:, r, s, :], s == 0, s == 1, att["pt"], t_av, inc=(s == 1))
            ptf[0] = [t]
            for r in range(2):
                p = slice(64 * r, 64 * r + 64)
                th = act(YH[p, hp, :], b[p, r * 256:r * 256 + 256], ACT.Copy, t)
                tl = tt(YL[p, hp, :], b[p, r * 256:r * 256 + 256], YH[p, hp, :].bitcast(f32), ALU.subtract, th)
                AC.wait(tl)
            b.free = [tl, th]
            ytoks[hp] = [tl, th]

        def attention():
            for n in range(10):
                if n >= 3 and n % 2:
                    att_values((n - 3) // 2)
                if 1 <= n < 9:
                    att_turn(n - 1)
                if n < 8:
                    att_probs(n)
                yield

        gi, gr, ga_ = indexer(), retention(), attention()
        for name, dst in (("rq", RQ), ("rk", RK)):
            for i in range(2):
                (b,), t = lin_fm(H1, L1, hn)
                rope_rest()
                rope(b, 2, t, 1, dst[:, 2 * i:2 * i + 2, :], name)
                next(gi, None)
        for i in range(4):
            (b, t), = lin_tm(2, H=H1, L=L1, toks=hn)
            rope_rest()
            t_rv[i] = act(RV[:, :, i * 256:i * 256 + 256], b.two(), ACT.Copy, t)
            b.free = [t_rv[i]]
            next(gi, None)
            next(gr)
        for i in range(2):
            (b,), t = lin_fm(H1, L1, hn)
            rope_rest()
            rope(b, 2, t, 0, AQ[:, 2 * i:2 * i + 2, :], "aq")
            next(gr)
        b, t, b2, t2 = lin_mixed(64, H1, L1, hn)
        rope_rest()
        v2 = b2[:, 0:128].rearrange("p (a c) -> p a c", a=2)
        act(AV[:, :, 0:64], v2, ACT.Copy, t2, indexer.logits)
        t_av = act(AV[:, :, 64:128], v2, ACT.Copy, t2)
        b2.free = [t_av]
        rope(b, 1, t, 0, AK.unsqueeze(1), "ak")
        next(gr)
        rope_rest()
        sgf = [trf[0], trf[1]]
        for h4 in range(4):
            (b,), t = lin_fm(H1, L1, hn)
            S = TR[h4 % 2]
            w = act(S, b.two(), ACT.Silu, t, sgf[h4 % 2])
            b.free = [w]
            Y2 = YN[:, 2 * h4:2 * h4 + 2, :]
            u = tt(Y2, Y2, S, ALU.mult, w, ynt[h4])
            sgf[h4 % 2] = [u]
            y = split_into(YH[:, 4 + 2 * h4:6 + 2 * h4, :], YL[:, 4 + 2 * h4:6 + 2 * h4, :], Y2, u)
            ytoks[4 + 2 * h4] = ytoks[5 + 2 * h4] = y
            next(ga_)
        t_ga = [None] * 4
        for j in range(4):
            (b,), t = lin_fm(H1, L1, hn)
            t_ga[j] = act(SGA[:, j, :, :], b.two(), ACT.Sigmoid, t, ret_values.tok)
            b.free = [t_ga[j]]
            next(ga_)
        mtoks = [None] * 8
        t_gb, t_a, taf = [None] * 4, [None] * 4, []
        for name, j in MERGE:
            if name == "w2gb":
                (b,), t = lin_fm(H1, L1, hn)
                t_gb[j] = act(TR[j % 2], b.two(), ACT.Sigmoid, t, sgf[j % 2])
                b.free = [t_gb[j]]
                next(ga_, None)
            elif name == "wba":
                (b,), t = lin_fm(YH[:, 0:4, :], YL[:, 0:4, :], ytoks[0:4], nk=4)
                t_a[j] = tt(SGA[:, j, :, :], SGA[:, j, :, :], b.two(), ALU.mult, t_ga[j], t)
                b.free = [t_a[j]]
            else:
                (b,), t = lin_fm(YH[:, 4:12, :], YL[:, 4:12, :], ytoks[4:12])
                u = tt(TR[j % 2], TR[j % 2], b.two(), ALU.mult, t_gb[j], t)
                b.free = [u]
                u = tt(TA, SGA[:, j, :, :], TR[j % 2], ALU.add, u, t_a[j], taf)
                sgf[j % 2] = [u]
                taf = y = split_into(H0[:, 2 * j:2 * j + 2, :], L0[:, 2 * j:2 * j + 2, :], TA, u)
                mtoks[2 * j] = mtoks[2 * j + 1] = y
        un = Unscaled(par("ffn2n"), H1, L1)
        us = project(H0, L0, mtoks, 1.0, BK[0:3] + BK[4:8], un)
        ht = un.end()
        ph = everyone()
        arena_at[0] = 0
        SB, TB = [ar(512, 2), ar(512, 2)], [ar(512, 2), ar(512, 2)]
        PL = ar(512, 2)
        RSX = ar(256)
        RSX2 = RSX.unsqueeze(1).broadcast_to([128, 2, 256])
        d_l = Dma("d_l")
        t_pl = d_l.go(SY, PL.rearrange("p k t -> p (k t)"), D["ple"], ph)
        PH, PLO = H0[:, 0:2, :], L0[:, 0:2, :]
        t_ph = []

        def root(t):
            t = rstd(AUX, t, 1.0 / 1024, EPSA)
            t = vcopy(RSX, RS[:, :], t)
            rsfree[0] = [t]
            return t

        DV.wait(ph)
        AC.wait(ph)
        un = Unscaled(par("plen"), H1, L1)
        us = swiglu(11, ht, H1, L1, False, 0.5, SB, TB, late=lambda: root(stats(AUX, 3, us[3])),
                    hooks={3: lambda: t_ph.extend(split_into(PH, PLO, PL, t_pl, ph))}, un=un)
        ht = un.end()
        rotate(BK[0:3] + BK[4:8])
        sfr, up = [[], []], None
        for j in range(4):
            (b,), t = lin_fm(H1, L1, ht)
            if j == 0:
                t_rs = root(all_stats(us))
                PE.wait(AUX.free)
            S, T = SB[j % 2], TB[j % 2]
            u = tt(S, b.two(), RSX2, ALU.mult, t, sfr[j % 2], t_rs)
            b.free = [u]
            w = act(S, S, ACT.Sigmoid, u)
            (b,), t = lin_fm(PH, PLO, [t_ph, t_ph], nk=2)
            if j:
                stats(AUX, j - 1, up)
            u = tt(T, S, b.two(), ALU.mult, w, t)
            b.free = [u]
            sfr[j % 2] = [u]
            xs = XT[:, 2 * j:2 * j + 2, :]
            up = tt(xs, xs, T, ALU.add, u)
        s = stats(AUX, 3, up)
        t = rstd(AUX, s, 1.0 / 1024, EPSA)
        d_o = Dma("d_out")
        for k in range(8):
            u = stt(XT[:, k, :], XT[:, k, :], par("final2")[:, k:k + 1], RS[:, :], ALU.mult, ALU.mult, t, AC.last())
            if k % 2:
                to = d_o.go(SY, out[:, (k - 1) * 256:(k + 1) * 256], XTt[:, (k - 1) * 256:(k + 1) * 256], u)
        SY.wait(to)
        assert st["g"] == 2 * len(chunks) and st["f"] == len(chunks)

        block = cx.enter_context(nc.Block())

        def run_all(e, q):
            for f in q:
                if isinstance(f, tuple):
                    v = e.value_load(f[0][0:1, 0:1], min_val=0, max_val=1)
                    with e.If(v < 1):
                        run_all(e, f[1])
                    with e.Else():
                        run_all(e, f[2])
                else:
                    f(e)

        def play(lane):
            def body(e):
                run_all(e, lane.q)
            return body

        block.sync(play(SY))
        block.scalar(play(AC))
        block.vector(play(DV))
        block.tensor(play(PE))


def constants():
    f = np.float32
    parts = {}
    parts["ident"] = np.eye(128, dtype=f)
    parts["sel"] = np.zeros((128, 2), f)
    parts["sel"][0:4] = [[1, 0], [0, 1], [1, 0], [0, 1]]
    parts["ones"] = np.ones((128, 128), f)
    for name, half in (("ra", 32), ("rr", 64)):
        R = np.zeros((128, 128), f)
        for m in range(128):
            b, i = m // (2 * half) * 2 * half, m % (2 * half)
            if i < half:
                R[b + i + half, m] = -1
            else:
                R[b + i - half, m] = 1
        parts[name] = R
    inv = np.zeros((128, 2), f)
    for c, half in enumerate((32, 64)):
        t = f(10000.0) ** (-np.arange(half, dtype=f) / f(half))
        inv[:, c] = t[np.arange(128) % half]
    parts["inv"] = inv
    parts["idxw"] = np.tile(np.arange(8, 0, -1, dtype=f), (128, 1))
    sm = np.ones((128, 512), f)
    sm[:, [0, 64, 128, 192, 256]] = 0
    parts["scanm"] = sm
    j, i = np.arange(128)[:, None], np.arange(128)[None, :]
    same = j // 64 == i // 64
    parts["glam"] = np.concatenate([same & (j <= i), same & (j >= i)], 1).astype(f)

    def win(n, w):
        lo = w // 2
        hi = w - 1 - lo
        M = np.zeros((n, n))
        for t in range(n):
            s, e = max(t - lo, 0), min(t + hi + 1, n)
            M[t, s:e] = 1.0 / (e - s)
        return M

    pool = np.zeros((128, 2, 4, 256), f)
    for g, w in enumerate((2, 4, 8, 16)):
        M = np.kron(win(4, w), win(64, w)) - np.eye(256)
        pool[:, :, g, :] = M.T.reshape(2, 128, 256).transpose(1, 0, 2)
    parts["pool"] = pool.reshape(128, -1)
    dec = np.zeros((128, 4, 384))
    for h in range(4):
        lg = np.log1p(-(2.0 ** (-5.0 - h)))
        a, b = np.arange(256)[:, None], np.arange(256)[None, :]
        M = np.exp(lg * np.abs(a - b)) * (a // 64 <= b // 64) * 128 ** -0.5
        dec[:, h, 0:256] = M[0:128]
        dec[:, h, 256:384] = M[128:, 128:]
    parts["dec"] = dec.reshape(128, -1).astype(f)
    parts["tri"] = (np.arange(128)[:, None] < np.arange(128)[None, :]).astype(f)
    parts["iota"] = np.tile(np.arange(128, dtype=f), (128, 1))
    return np.ascontiguousarray(np.concatenate([parts[n] for n, _ in CON], 1))


def kernel(**I):
    import concourse.bacc as bacc
    from concourse import mybir
    from concourse.bass_utils import run_bass_kernel_spmd as run

    I = {k: np.asarray(v) for k, v in I.items()}

    def cols(w, lists):
        K = w.shape[0]
        r = w.reshape(K // 128, 128, -1)
        return np.ascontiguousarray(np.stack([r[:, :, c].transpose(1, 0, 2).reshape(128, -1) for c in lists]))

    def even(w, a, b, step=256):
        return cols(w, [np.arange(s, s + step) for s in range(a, b, step)])

    def rows(w):
        K, n = w.shape
        return np.ascontiguousarray(w.reshape(K // 256, 2, 128, n).transpose(0, 2, 1, 3).reshape(K // 256, 128, 2 * n))

    def fm(x):
        t, n = x.shape
        return np.ascontiguousarray(x.T.reshape(n // 128, 128, t).transpose(1, 0, 2).reshape(128, -1))

    col = lambda v: v.reshape(-1, 128).T
    w1 = I["w_in"][0]
    w2 = I["w_in_2"][0]
    A = {}
    A["w_ada"] = even(I["w_ada"][0], 0, 6144)
    w1a = np.zeros((1024, 128), w1.dtype)
    w1a[:, 0:32] = w1[:, 1536:1568]
    A["w1p"] = even(w1, 1568, 2080)
    A["w1a"] = even(w1a, 0, 128, 128)
    A["w1k"] = even(w1, 256, 512)
    A["w1q"] = even(w1, 0, 256)
    A["w1v"] = even(w1, 512, 1024)
    A["w1g"] = even(w1, 1024, 1536)
    A["w_out"] = even(I["w_out"][0], 0, 1024)
    A["w_r"] = even(np.concatenate([I["w_router_group"][0], I["w_router_expert"][0]], 1), 0, 36, 36)
    we = I["w_expert_in"][0]
    e4 = we.reshape(32, 8, 128, 2, 256).transpose(3, 0, 2, 1, 4).reshape(2, 32, 128, 2048)
    A["eg"], A["eu"] = np.ascontiguousarray(e4[0]), np.ascontiguousarray(e4[1])
    A["ed"] = rows(I["w_expert_out"][0].reshape(8192, 1024))
    for n in "12":
        A[f"f{n}g"] = even(I[f"ffn{n}_w_gate_2"][0], 0, 2816)
        A[f"f{n}u"] = even(I[f"ffn{n}_w_up_2"][0], 0, 2816)
        A[f"f{n}d"] = rows(I[f"ffn{n}_w_down_2"][0])
    ra = np.arange
    A["w2ik"] = cols(w2, [np.concatenate([ra(1152, 1216), ra(1152, 1216), ra(1216, 1224)])])
    A["w2iq"] = even(w2, 640, 1152)
    A["w2rq"] = even(w2, 1224, 1736)
    A["w2rk"] = even(w2, 1736, 2248)
    A["w2rv"] = even(w2, 2248, 3272)
    A["w2aq"] = even(w2, 0, 512)
    A["w2kv"] = cols(w2, [np.concatenate([ra(512, 576), ra(512, 576), ra(576, 640)])])
    A["w2rg"] = even(w2, 3272, 4296)
    A["w2ga"] = even(w2, 4296, 5320)
    A["w2gb"] = even(w2, 5320, 6344)
    A["wba"] = even(I["w_branch_a_2"][0], 0, 1024)
    A["wbb"] = even(I["w_branch_b_2"][0], 0, 1024)
    A["w_out2"] = even(I["w_out_2"][0], 0, 1024)
    A["wpg"] = even(I["w_ple_gate_2"][0], 0, 1024)
    A["wpp"] = even(I["w_ple_proj_2"][0], 0, 1024)
    A["x"] = fm(I["x"][0])
    A["ctx"] = fm(I["ctx"][0])
    A["ple"] = fm(I["p_2"][0, 0])
    A["cvec"] = fm(np.stack([I["c"][0], I["c_ctx"]]))
    A["pos"] = np.ascontiguousarray(I["positions_2"])
    A["par"] = np.ascontiguousarray(np.concatenate([
        col(I["norm1_g"]), col(I["b_ada"]), col(I["b_decay"]), col(I["gla_norm_g"]), col(I["pool_scale"]),
        col(I["norm2_g"]), col(I["final_norm_g"]), col(I["ffn1_norm_2"]), col(I["mix_norm_2"]), col(I["ret_gn_2"]),
        col(I["ffn2_norm_2"]), col(I["ple_norm_2"]), col(I["final_norm_2"])], 1))
    A["cst"] = constants()
    A["w_pool"] = np.ascontiguousarray(I["w_pool"][0].transpose(1, 0, 2).reshape(128, 512))
    wd = np.zeros((32, 2, 256), np.float32)
    wd[0:16, 0], wd[16:32, 1] = I["w_decay"][0, 0], I["w_decay"][0, 1]
    A["w_dec"] = wd.reshape(32, 512)

    nc = bacc.Bacc("TRN2", target_bir_lowering=False, num_devices=1)
    D = {n: nc.dram_tensor("in_" + n, a.shape, mybir.dt.from_np(a.dtype), kind="ExternalInput").ap() for n, a in A.items()}
    o = nc.dram_tensor("out0", (128, 2048), mybir.dt.float32, kind="ExternalOutput").ap()
    program(nc, D, o)
    r = run(nc, [{"in_" + n: a for n, a in A.items()}], core_ids=[0])
    y = r.results[0]["out0"].reshape(128, 8, 256).transpose(2, 1, 0).reshape(1, 256, 1024)
    return np.ascontiguousarray(y)
```
